# Optimizing a Trainium2 kernel written in Bass

```python
import math
import jax, jax.numpy as jnp
from jax import lax
import numpy as np

D_MODEL = 1024
BATCH = 1
SEQ = 512
DEPTH = 2

GRID_W = 64
CTX_LEN = 256
HEAD_DIM = 64
A_HEADS = D_MODEL // 128
A_KV_HEADS = A_HEADS // 4
A_GROUP = A_HEADS // A_KV_HEADS
B_HEADS = D_MODEL // 256
B_VDIM = 2 * HEAD_DIM
A_WIDTH = A_HEADS * HEAD_DIM
B_WIDTH = B_HEADS * B_VDIM
D_MIX = A_WIDTH + B_WIDTH
A_Q = A_HEADS * HEAD_DIM
A_KV = A_KV_HEADS * HEAD_DIM
B_QK = B_HEADS * 2 * HEAD_DIM
B_V = B_HEADS * B_VDIM
COL_SIZES = (A_Q, A_KV, A_KV, B_QK, B_QK, B_V)
D_IN = sum(COL_SIZES)
D_FF = ((8 * D_MODEL // 3 + 127) // 128) * 128
CONV_W = 3
Q_BLOCK = 128
ROPE_THETA = 10000.0
EPS = 1e-6

kernel_name = "hybrid_gqa_diffattn_convffn_dit"

def rmsnorm(x, g):
    xf = x.astype(jnp.float32)
    y = xf * lax.rsqrt(jnp.mean(xf * xf, axis=-1, keepdims=True) + EPS)
    return y.astype(x.dtype) * g

def modulate(h, shift, scale):
    return h * (1 + scale) + shift

def axial_rope_tables(rows, dtype):
    row = jnp.repeat(jnp.arange(rows, dtype=jnp.float32), GRID_W)
    col = jnp.tile(jnp.arange(GRID_W, dtype=jnp.float32), rows)
    quarter = HEAD_DIM // 4
    inv_freq = ROPE_THETA ** (-jnp.arange(quarter, dtype=jnp.float32) / quarter)
    ang_r = row[:, None] * inv_freq[None, :]
    ang_c = col[:, None] * inv_freq[None, :]
    cos = jnp.concatenate([jnp.cos(ang_r), jnp.cos(ang_r), jnp.cos(ang_c), jnp.cos(ang_c)], axis=-1)
    sin = jnp.concatenate([jnp.sin(ang_r), jnp.sin(ang_r), jnp.sin(ang_c), jnp.sin(ang_c)], axis=-1)
    return cos.astype(dtype), sin.astype(dtype)

def apply_rope(x, cos, sin):
    x1, x2, x3, x4 = jnp.split(x, 4, axis=-1)
    rot = jnp.concatenate([-x2, x1, -x4, x3], axis=-1)
    return x * cos + rot * sin

def split_cols(p):
    idx = np.cumsum(COL_SIZES)[:-1].tolist()
    return jnp.split(p, idx, axis=-1)

def gqa_heads(aq, ak, av, g_q, g_k):
    b, n, _ = aq.shape
    q = rmsnorm(aq.reshape(b, n, A_KV_HEADS, A_GROUP, HEAD_DIM), g_q).transpose(0, 2, 3, 1, 4)
    k = rmsnorm(ak.reshape(b, n, A_KV_HEADS, HEAD_DIM), g_k).transpose(0, 2, 1, 3)
    v = av.reshape(b, n, A_KV_HEADS, HEAD_DIM).transpose(0, 2, 1, 3)
    return q, k, v

def diff_heads(bq, bk, bv):
    b, n, _ = bq.shape
    q = bq.reshape(b, n, B_HEADS, 2, HEAD_DIM).transpose(0, 2, 3, 1, 4)
    k = bk.reshape(b, n, B_HEADS, 2, HEAD_DIM).transpose(0, 2, 3, 1, 4)
    v = bv.reshape(b, n, B_HEADS, B_VDIM).transpose(0, 2, 1, 3)
    return q, k, v

def gqa_attend(q, k, v):
    s = jnp.einsum('bkgqd,bknd->bkgqn', q, k) * (HEAD_DIM ** -0.5)
    p = jax.nn.softmax(s.astype(jnp.float32), axis=-1).astype(v.dtype)
    return jnp.einsum('bkgqn,bknd->bkgqd', p, v)

def diff_attend(q, k, v, lam):
    s = jnp.einsum('bhjqd,bhjnd->bhjqn', q, k) * (HEAD_DIM ** -0.5)
    p = jax.nn.softmax(s.astype(jnp.float32), axis=-1)
    a = (p[:, :, 0] - lam * p[:, :, 1]).astype(v.dtype)
    return jnp.einsum('bhqn,bhnv->bhqv', a, v)

def over_query_blocks(fn, q, q_axis, out_axis):
    n = q.shape[q_axis]
    nb = n // Q_BLOCK
    qb = q.reshape(q.shape[:q_axis] + (nb, Q_BLOCK) + q.shape[q_axis + 1:])
    qb = jnp.moveaxis(qb, q_axis, 0)
    ob = lax.map(fn, qb)
    ob = jnp.moveaxis(ob, 0, out_axis)
    return ob.reshape(ob.shape[:out_axis] + (n,) + ob.shape[out_axis + 2:])

def merge_heads(a_out, b_out, g_sub, lam_init):
    b, _, _, n, _ = a_out.shape
    a = a_out.transpose(0, 3, 1, 2, 4).reshape(b, n, A_WIDTH)
    bo = rmsnorm(b_out, g_sub) * (1.0 - lam_init)
    bo = bo.transpose(0, 2, 1, 3).reshape(b, n, B_WIDTH)
    return jnp.concatenate([a, bo], axis=-1)

def conv_ffn(h, w_up, conv_w, conv_b, w_down):
    u = h @ w_up
    u = lax.conv_general_dilated(u, conv_w[:, None, :], window_strides=(1,),
                                 padding=((CONV_W // 2, CONV_W // 2),),
                                 dimension_numbers=('NWC', 'WIO', 'NWC'),
                                 feature_group_count=u.shape[-1]) + conv_b
    g, v = jnp.split(u, 2, axis=-1)
    return (jax.nn.silu(g) * v) @ w_down

def setup_inputs(seed: int = 0) -> dict:
    key = jax.random.key(seed)
    ks = jax.random.split(key, 24)
    f32 = jnp.float32
    nrm = lambda k, shape, s: jax.random.normal(k, shape, f32) * s
    return {
        "x": nrm(ks[0], (BATCH, SEQ, D_MODEL), 1.0),
        "c": nrm(ks[1], (BATCH, D_MODEL), 1.0),
        "ctx": nrm(ks[2], (BATCH, CTX_LEN, D_MODEL), 1.0),
        "c_ctx": nrm(ks[3], (D_MODEL,), 1.0),
        "w_ada": nrm(ks[4], (DEPTH, D_MODEL, 6 * D_MODEL), 0.3 * D_MODEL ** -0.5),
        "b_ada": nrm(ks[5], (DEPTH, 6 * D_MODEL), 0.02),
        "g_attn": 1.0 + nrm(ks[6], (DEPTH, D_MODEL), 0.02),
        "w_in": nrm(ks[7], (DEPTH, D_MODEL, D_IN), D_MODEL ** -0.5),
        "g_qa": 1.0 + nrm(ks[8], (DEPTH, HEAD_DIM), 0.02),
        "g_ka": 1.0 + nrm(ks[9], (DEPTH, HEAD_DIM), 0.02),
        "lam_q1": nrm(ks[10], (DEPTH, HEAD_DIM), 0.1),
        "lam_k1": nrm(ks[11], (DEPTH, HEAD_DIM), 0.1),
        "lam_q2": nrm(ks[12], (DEPTH, HEAD_DIM), 0.1),
        "lam_k2": nrm(ks[13], (DEPTH, HEAD_DIM), 0.1),
        "g_sub": 1.0 + nrm(ks[14], (DEPTH, B_VDIM), 0.02),
        "w_o": nrm(ks[15], (DEPTH, D_MIX, D_MODEL), D_MIX ** -0.5),
        "g_ffn": 1.0 + nrm(ks[16], (DEPTH, D_MODEL), 0.02),
        "w_up": nrm(ks[17], (DEPTH, D_MODEL, 2 * D_FF), D_MODEL ** -0.5),
        "conv_w": nrm(ks[18], (DEPTH, CONV_W, 2 * D_FF), CONV_W ** -0.5),
        "conv_b": nrm(ks[19], (DEPTH, 2 * D_FF), 0.02),
        "w_down": nrm(ks[20], (DEPTH, D_FF, D_MODEL), D_FF ** -0.5),
        "g_final": 1.0 + nrm(ks[21], (D_MODEL,), 0.02),
    }

def reference(x, c, ctx, c_ctx, w_ada, b_ada, g_attn, w_in, g_qa, g_ka,
              lam_q1, lam_k1, lam_q2, lam_k2, g_sub, w_o, g_ffn,
              w_up, conv_w, conv_b, w_down, g_final):
    n = x.shape[1]
    rows = n // GRID_W
    cos, sin = axial_rope_tables(rows, x.dtype)
    f32 = jnp.float32
    x_lat, x_ctx = x, ctx
    for l in range(DEPTH):
        last = l == DEPTH - 1
        lam_init = 0.8 - 0.6 * math.exp(-0.3 * l)
        mod_x = (jax.nn.silu(c) @ w_ada[l] + b_ada[l])[:, None, :]
        mod_c = (jax.nn.silu(c_ctx) @ w_ada[l] + b_ada[l])[None, None, :]
        sh1x, sc1x, g1x, sh2x, sc2x, g2x = jnp.split(mod_x, 6, axis=-1)
        sh1c, sc1c, g1c, sh2c, sc2c, g2c = jnp.split(mod_c, 6, axis=-1)

        hx = modulate(rmsnorm(x_lat, g_attn[l]), sh1x, sc1x)
        hc = modulate(rmsnorm(x_ctx, g_attn[l]), sh1c, sc1c)
        aqx, akx, avx, bqx, bkx, bvx = split_cols(hx @ w_in[l])
        aqc, akc, avc, bqc, bkc, bvc = split_cols(hc @ w_in[l])

        qx, kx, vx = gqa_heads(aqx, akx, avx, g_qa[l], g_ka[l])
        qx, kx = apply_rope(qx, cos, sin), apply_rope(kx, cos, sin)
        qc, kc, vc = gqa_heads(aqc, akc, avc, g_qa[l], g_ka[l])
        k_all = jnp.concatenate([kc, kx], axis=2)
        v_all = jnp.concatenate([vc, vx], axis=2)
        a_out_x = over_query_blocks(lambda qb: gqa_attend(qb, k_all, v_all), qx, 3, 3)

        lam = (jnp.exp(jnp.sum(lam_q1[l].astype(f32) * lam_k1[l].astype(f32)))
               - jnp.exp(jnp.sum(lam_q2[l].astype(f32) * lam_k2[l].astype(f32))) + lam_init)
        dqx, dkx, dvx = diff_heads(bqx, bkx, bvx)
        dqx, dkx = apply_rope(dqx, cos, sin), apply_rope(dkx, cos, sin)
        dqc, dkc, dvc = diff_heads(bqc, bkc, bvc)
        dk_all = jnp.concatenate([dkc, dkx], axis=3)
        dv_all = jnp.concatenate([dvc, dvx], axis=2)
        b_out_x = over_query_blocks(lambda qb: diff_attend(qb, dk_all, dv_all, lam), dqx, 3, 2)

        x_lat = x_lat + g1x * (merge_heads(a_out_x, b_out_x, g_sub[l], lam_init) @ w_o[l])
        if not last:
            a_out_c = gqa_attend(qc, kc, vc)
            b_out_c = diff_attend(dqc, dkc, dvc, lam)
            x_ctx = x_ctx + g1c * (merge_heads(a_out_c, b_out_c, g_sub[l], lam_init) @ w_o[l])

        hx = modulate(rmsnorm(x_lat, g_ffn[l]), sh2x, sc2x)
        x_lat = x_lat + g2x * conv_ffn(hx, w_up[l], conv_w[l], conv_b[l], w_down[l])
        if not last:
            hc = modulate(rmsnorm(x_ctx, g_ffn[l]), sh2c, sc2c)
            x_ctx = x_ctx + g2c * conv_ffn(hc, w_up[l], conv_w[l], conv_b[l], w_down[l])

    return rmsnorm(x_lat, g_final)


_drawn_inputs = setup_inputs


def setup_inputs(seed=0):
    import zlib

    import numpy as np

    out = dict(_drawn_inputs(seed))
    spreads = {}
    factors = {'g_attn': 8.0,
     'g_qa': 8.0,
     'g_ka': 8.0,
     'lam_q1': 8.0,
     'lam_k1': 8.0,
     'lam_q2': 4.483,
     'lam_k2': 3.747,
     'g_sub': 8.0,
     'g_ffn': 8.0,
     'conv_b': 8.0,
     'g_final': 2.742}
    for name, (base, spread) in spreads.items():
        noise = np.random.default_rng([zlib.crc32(name.encode()), seed]).standard_normal(out[name].shape)
        drawn = base * np.exp(spread * noise) if base else spread * noise
        out[name] = __import__('jax').numpy.asarray(drawn.astype(out[name].dtype))
    for name, factor in factors.items():
        out[name] = (out[name] * factor).astype(out[name].dtype)
    return out
```

```python
import math
from contextlib import ExitStack

import concourse.bass as bass
from concourse import mybir

D = 1024
DEPTH = 2
SEQ, CTX = 512, 256
TOK = SEQ + CTX
GRID_W = 64
P = 128
HD = 64
KT = D // P
A_HEADS, A_KV, B_HEADS = D // 128, D // 512, D // 256
FF_TILES = ((8 * D // 3 + 127) // 128)
EPS = 1e-6
SCALE = HD ** -0.5
N_ADA = 6 * KT

CHUNK = 384
UNIT = 1024
UNIT_K = 2
IN_UNITS = KT // UNIT_K
PARTS = [8, 8, FF_TILES - 16]
LAYER_UNITS = 6 * IN_UNITS + KT + 2 * FF_TILES + len(PARTS) * KT
N_UNITS = DEPTH * LAYER_UNITS
RAW, RING = 2, 4
PROBS = 8
TURNS = 3
LEADS = 4

LAM_INIT = [0.8 - 0.6 * math.exp(-0.3 * l) for l in range(DEPTH)]

S_IDENT, S_ONES = 0, 128
S_COS, S_SIN = 256, 512
S_BADA = 768
S_GATTN = S_BADA + DEPTH * N_ADA
S_GFFN = S_GATTN + DEPTH * KT
S_GFIN = S_GFFN + DEPTH * KT
S_CONV = S_GFIN + KT
S_GSUB = S_CONV + DEPTH * 2 * FF_TILES * 4
S_GQ = S_GSUB + DEPTH
S_GK = S_GQ + DEPTH * HD
S_END = S_GK + DEPTH * HD
LAM_COLS = DEPTH * 4 * HD


def token_groups(l):
    return [(0, SEQ), (SEQ, TOK)] if l < DEPTH - 1 else [(0, SEQ)]


def unit0(l):
    return l * LAYER_UNITS


def in_unit(l, p, c):
    return unit0(l) + (2 * p + c) * IN_UNITS


def wo_unit(l):
    return unit0(l) + 6 * IN_UNITS


def up_unit(l, part):
    return wo_unit(l) + KT + sum(2 * n + KT for n in PARTS[:part])


def down_unit(l, part):
    return up_unit(l, part) + 2 * PARTS[part]


def evac_index(n):
    l, r = divmod(n, LAYER_UNITS)
    return l * (LAYER_UNITS - 6 * IN_UNITS) + r - 6 * IN_UNITS


def chunk_plan():
    plan = []
    for l in range(DEPTH):
        last = l == DEPTH - 1
        for p in range(3):
            for c in range(2):
                ch = dict(l=l, p=p, c=c, q=len(plan), unit=in_unit(l, p, c), tiles=[])
                for t in range(TOK // P):
                    full = not (last and t >= SEQ // P)
                    if p == 0:
                        maps = [(0, 2, "k", 8), (4, 2, "q", 0)] if c == 0 else [(0, 6, "q", 2)]
                        v = (2, 2) if c == 0 else None
                    else:
                        maps = [(0, 4, "k", 4), (4, 2, "q", 0)] if c == 0 else [(0, 2, "q", 2)]
                        v = (2, 4) if c == 1 else None
                    cols = (0, CHUNK)
                    if not full:
                        maps = [m for m in maps if m[2] == "k"]
                        if c == 0:
                            cols = (0, 256)
                        elif p == 0:
                            continue
                        else:
                            cols = (128, CHUNK)
                    ch["tiles"].append(dict(t=t, maps=maps, v=v, cols=cols))
                plan.append(ch)
    n_acc = n_tile = n_v = n_group = n_hi = 0
    for ch in plan:
        for x in ch["tiles"]:
            x["acc"] = n_acc
            n_acc += 1
            if x["maps"]:
                x["tile"] = n_tile
                n_tile += 1
                x["groups"] = []
                b = 0
                for s0, n, kind, store in x["maps"]:
                    blocks = n * (2 if kind == "k" else 1)
                    for g in range(0, blocks, 4):
                        m = min(4, blocks - g)
                        x["groups"].append((n_group, b + g, m, store + g))
                        n_group += 1
                    b += blocks
                x["his"] = n_hi + len(x["maps"])
                n_hi += len(x["maps"])
            if x["v"]:
                x["vn"] = n_v
                n_v += 1
    return plan


def attention_plan():
    phases = []
    sid = tid = item_id = 0
    for l in range(DEPTH):
        for p in range(3):
            items = []
            for g, (t0, t1) in enumerate(token_groups(l)):
                keys = range(TOK // P) if g == 0 else range(SEQ // P, TOK // P)
                for h in range(A_HEADS if p == 0 else 2):
                    it = dict(id=item_id, l=l, p=p, g=g, h=h, t0=t0, t1=t1, qt=list(range(t0 // P, t1 // P)),
                              kt=list(keys), maps=1 if p == 0 else 2, first=not items)
                    it["k0"], it["k1"] = keys[0] * P, (keys[-1] + 1) * P
                    it["S"] = []
                    for qi, q in enumerate(it["qt"]):
                        for m in range(it["maps"]):
                            it["S"].append(dict(sid=sid, q=q, qi=qi, m=m, item=it))
                            sid += 1
                    it["T"] = [dict(tid=tid + j, j=j, kt=kt, item=it) for j, kt in enumerate(it["kt"])]
                    tid += len(it["kt"])
                    item_id += 1
                    items.append(it)
            slot = 0
            users = {}
            for n, it in enumerate(items):
                it["slots"], it["freed_by"] = [], []
                for _ in it["qt"]:
                    it["slots"].append(slot)
                    it["freed_by"].append(users.get(slot))
                    users[slot] = it
                    slot = (slot + 1) % PROBS

            order = [("S", s) for s in items[0]["S"]]
            n_front = 1
            for i, it in enumerate(items):
                T = it["T"]
                back = []
                for j in range(len(T)):
                    back.append(("T", T[j]))
                    if j >= 2:
                        back.append(("V", T[j - 2]))
                back += [("V", x) for x in T[-2:]]
                upto = i + 2
                if upto < len(items) and items[upto]["g"] == 1 and it not in items[upto]["freed_by"]:
                    upto += 1
                rest = [("S", s) for x in items[n_front:upto] for s in x["S"]]
                n_front = max(n_front, min(upto, len(items)))
                per_t = -(-len(rest) // LEADS)
                for kind, x in back:
                    if kind == "T":
                        order += rest[:per_t]
                        rest = rest[per_t:]
                    order.append((kind, x))
                order += rest
            phases.append(dict(l=l, p=p, items=items, order=order))
    return phases


def backbone(nc, x_in, cc_in, small_in, lam_in, ada_in, w_in, out, x_spill):
    f32, f32r, bf16 = mybir.dt.float32, mybir.dt.float32r, mybir.dt.bfloat16
    ALU = mybir.AluOpType
    ACT = mybir.ActivationFunctionType
    AX = mybir.AxisListType

    chunks = chunk_plan()
    phases = attention_plan()

    def chunk_of(l, p, c):
        return chunks[6 * l + 2 * p + c]

    def phase_of(l, p):
        return phases[3 * l + p]

    base = -(-nc.sbuf_base // 64) * 64
    KB = 1024
    R_X = base
    R_H = R_X + 35 * KB
    R_QKV = R_H + 48 * KB
    R_O = R_QKV + 48 * KB
    R_W = R_O + 24 * KB
    R_TAB = R_W + 40 * KB
    R_SMALL = R_TAB + 4 * KB
    at = [R_SMALL]

    def place(name, shape, dt, offset):
        return nc.alloc_sbuf_tensor_at(name, shape, dt, offset=offset)

    def small(name, shape, dt=f32):
        n = 4
        for s in shape[1:]:
            n *= s
        a = place(name, shape, dt, at[0])
        at[0] += -(-n // 32) * 32
        return a

    x_sb = place("x_sb", [P, KT, TOK], f32, R_X)
    p_sb = place("p_sb", [P, PROBS, TOK], f32, R_X)
    ptmp = place("ptmp", [P, TOK], f32, R_X + 24 * KB)
    pt_at = [R_X + 27 * KB, R_X + 31 * KB, R_TAB]
    pt_hi = [place(f"pt_hi{i}", [P, SEQ], f32r, pt_at[i]) for i in range(TURNS)]
    pt_lo = [place(f"pt_lo{i}", [P, SEQ], f32r, pt_at[i] + 2 * KB) for i in range(TURNS)]
    raw = place("raw", [P, 6, CHUNK], f32, R_X)
    rawsq = place("rawsq", [P, 6, CHUNK], f32, R_X + 9 * KB)
    split = place("split", [P, 2, 10, 2, HD], f32, R_X + 18 * KB)
    rope1 = place("rope1", [P, 6, HD], f32, R_X + 28 * KB)
    rope2 = place("rope2", [P, 6, HD], f32, R_X + 28 * KB + 1536)
    roped = place("roped", [P, 2, 6, HD], f32, R_X + 31 * KB)
    c_bc = place("c_bc", [P, 2, D], f32, R_X + 24 * KB)
    sqsum = place("sqsum", [P, TOK], f32, R_X + 32 * KB)
    h_hi = place("h_hi", [P, KT, TOK], f32r, R_H)
    h_lo = place("h_lo", [P, KT, TOK], f32r, R_H + 24 * KB)
    y_sb = place("y_sb", [P, KT, SEQ], f32, R_H)
    osq = place("osq", [P, 2, TOK], f32, R_H)
    dgo = place("dgo", [P, 4, P], f32, R_H + 6 * KB)
    qk = place("qk", [P, 12, TOK], f32r, R_QKV)
    v_hi = place("v_hi", [P, 6, 256], f32r, R_QKV + 36 * KB)
    v_lo = place("v_lo", [P, 6, 256], f32r, R_QKV + 42 * KB)
    oh = place("oh", [P, KT, TOK], f32r, R_QKV)
    ol = place("ol", [P, KT, TOK], f32r, R_QKV + 24 * KB)
    a_hi = place("a_hi", [P, 8, TOK], f32r, R_QKV)
    a_lo = place("a_lo", [P, 8, TOK], f32r, R_QKV + 24 * KB)
    o_sb = place("o_sb", [P, KT, TOK], f32, R_O)
    conv_g = place("conv_g", [P, TOK], f32, R_O)
    conv_v = place("conv_v", [P, TOK], f32, R_O + 3 * KB)
    sqt = place("sqt", [P, 2, TOK], f32, R_O)
    ht = place("ht", [P, 2, TOK], f32, R_O + 6 * KB)
    ada_b = [place("ada_b0", [P, D], f32, R_TAB), place("ada_b1", [P, D], f32, R_O + 16 * KB)]
    ada_junk = place("ada_junk", [P, D], bf16, R_O + 20 * KB)
    dgn = place("dgn", [P, 4, P], f32, R_O + 22 * KB)
    lamv = place("lamv", [P, DEPTH, 4, HD], f32, R_O + 12 * KB)
    w_raw = place("w_raw", [P, RAW, UNIT], f32, R_W)
    w_hi = place("w_hi", [P, RING, UNIT], f32r, R_W + 8 * KB)
    w_lo = place("w_lo", [P, RING, UNIT], f32r, R_W + 24 * KB)
    tabs = place("tabs", [P, 4, 4, HD], f32, R_TAB)
    sm = small("sm", [P, S_END])
    mod = small("mod", [P, DEPTH, 2, N_ADA])
    ada_sum = small("ada_sum", [P, 2, 4])
    gs1 = small("gs1", [P, 2, KT])
    gs2 = small("gs2", [P, 2, KT])
    eps = small("eps", [P, 1])
    zero = small("zero", [P, 1])
    act_scrap = small("act_scrap", [P, 1])
    lamw = small("lamw", [P, 4])
    nlam = small("nlam", [P, DEPTH])
    gsub = small("gsub", [P, DEPTH])
    head_ss = small("head_ss", [P, 36])
    head_sd = small("head_sd", [P, 36])
    head_r = small("head_r", [P, 36])
    nb = small("nb", [P, 8])
    rs = small("rs", [P, 8])
    ri = small("ri", [P, 8])
    rl = small("rl", [P, 8])
    n_sd = small("n_sd", [P, 24])
    n_r = small("n_r", [P, 24])
    assert at[0] <= nc.sbuf_usable_end, (at[0], nc.sbuf_usable_end)

    ident = sm[:, S_IDENT:S_IDENT + P]
    ones = sm[:, S_ONES:S_ONES + P]

    ctx = ExitStack()
    with ctx:
        ps = ctx.enter_context(nc.psum_tensor("ps", [P, 8, 512], f32))

        def sem(name):
            return ctx.enter_context(nc.semaphore(name))

        small_loaded = sem("small_loaded")
        x_loaded = sem("x_loaded")
        c_loaded = sem("c_loaded")
        c_ready = sem("c_ready")
        ada_loaded = [sem("ada_loaded0"), sem("ada_loaded1")]
        ada_used = sem("ada_used")
        w_loaded = [sem("w_loaded0"), sem("w_loaded1")]
        w_hi_done = sem("w_hi_done")
        w_lo_done = sem("w_lo_done")
        unit_done = sem("unit_done")
        acc_done = sem("acc_done")
        acc_copied = sem("acc_copied")
        raw_squared = sem("raw_squared")
        head_ss_done = sem("head_ss_done")
        head_sd_done = sem("head_sd_done")
        rope_done = sem("rope_done")
        split_hi_done = sem("split_hi_done")
        split_lo_done = sem("split_lo_done")
        v_hi_done = sem("v_hi_done")
        v_lo_done = sem("v_lo_done")
        qk_turned = sem("qk_turned")
        qk_stored = sem("qk_stored")
        scores_done = sem("scores_done")
        bias_done = sem("bias_done")
        exp_done = sem("exp_done")
        recip_done = sem("recip_done")
        scaled_done = sem("scaled_done")
        probs_done = sem("probs_done")
        turned = sem("turned")
        pt_hi_done = sem("pt_hi_done")
        pt_lo_done = sem("pt_lo_done")
        pv_done = sem("pv_done")
        o_done = sem("o_done")
        osq_done = sem("osq_done")
        o_normed = sem("o_normed")
        o_hi_done = sem("o_hi_done")
        o_lo_done = sem("o_lo_done")
        sq_done = sem("sq_done")
        sqsum_done = sem("sqsum_done")
        ss_done = sem("ss_done")
        sd_done = sem("sd_done")
        diag_done = sem("diag_done")
        spread_done = sem("spread_done")
        ht_done = sem("ht_done")
        h_hi_done = sem("h_hi_done")
        h_lo_done = sem("h_lo_done")
        bank_read = sem("bank_read")
        conv_started = sem("conv_started")
        silu_done = sem("silu_done")
        prod_done = sem("prod_done")
        a_hi_done = sem("a_hi_done")
        a_lo_done = sem("a_lo_done")
        lam_sum = sem("lam_sum")
        lam_exp = sem("lam_exp")
        x_spilled = sem("x_spilled")
        y_done = sem("y_done")
        stored = sem("stored")
        dve_step = sem("dve_step")
        act_step = sem("act_step")

        class Steps:

            def __init__(self, eng, s):
                self.eng, self.s, self.n, self.i, self.per, self.k = eng, s, 0, 0, 0, 0

            def mark(self, ins):
                self.k += 1
                ins.then_inc(self.s, 1)

            def wait(self):
                self.eng.wait_ge(self.s, self.i * self.per + (self.n + self.k))

            def __call__(self, ins):
                self.mark(ins)
                self.wait()

            def loop(self, n, per, body):
                self.n, self.k = self.n + self.k, 0
                self.per = per
                with self.eng.Fori(0, n) as i:
                    self.i = i
                    body(i)
                    assert self.k == per, (self.k, per)
                self.n, self.i, self.k, self.per = self.n + n * per, 0, 0, 0

        def wait_unit(e, c, i=0):
            l, r = divmod(c, LAYER_UNITS)
            done_in = l * 6 + min(r, 6 * IN_UNITS) // IN_UNITS
            if r < 6 * IN_UNITS and r % IN_UNITS == IN_UNITS - 1:
                e.wait_ge(acc_done, chunks[l * 6 + r // IN_UNITS]["tiles"][-1]["acc"] + 1)
            else:
                e.wait_ge(unit_done, 4 * i + (c + 1 - done_in))

        norms = []
        for l in range(DEPTH):
            norms += [[(0, SEQ), (SEQ, TOK)], token_groups(l)]
        norms.append([(0, SEQ)])

        def n_tiles(groups):
            return sum((b - a) // P for a, b in groups)

        def norm_counts(j):
            tiles = sum(n_tiles(g) for g in norms[:j])
            hs = sum(len(g) * KT for g in norms[:j])
            return tiles, hs

        stat_order = [("norm", 0)]
        for l in range(DEPTH):
            stat_order += [("sub", l), ("norm", 2 * l + 1), ("norm", 2 * l + 2)]

        def stat_tiles(s):
            kind, j = s
            return 4 * n_tiles(token_groups(j)) if kind == "sub" else n_tiles(norms[j])

        def stat_index(s):
            return stat_order.index(s)

        def stat_base(s):
            return sum(stat_tiles(r) for r in stat_order[:stat_index(s)])

        sub_oh = [sum(KT * len(token_groups(k)) for k in range(l)) for l in range(DEPTH)]
        sub_sq = [sum(4 for k in range(l)) for l in range(DEPTH)]

        block = ctx.enter_context(nc.Block())

        @block.sync
        def _(sp):
            def load_unit(c, i=0, first=False):
                if not first:
                    sp.wait_ge(w_lo_done, 4 * i + (c - RAW + 1))
                sp.dma_start(w_raw[:, c % RAW, :], w_in[4 * i + c, :, :]).then_inc(w_loaded[c % RAW], 16)

            def load_ada(c, i=0, first=False):
                if not first:
                    sp.wait_ge(ada_used, 4 * i + (c - 1))
                sp.dma_start(ada_b[c % 2][:, :], ada_in[4 * i + c, :, :]).then_inc(ada_loaded[c % 2], 16)

            sp.dma_start(sm[:, :], small_in).then_inc(small_loaded, 16)
            sp.dma_start(c_bc[:, :, :].rearrange("p a k -> p (a k)"),
                         cc_in.partition_broadcast(P)).then_inc(c_loaded, 16)
            for a in range(2):
                load_ada(a, first=True)
            sp.dma_start(x_sb[:, :, :], x_in).then_inc(x_loaded, 16)
            sp.dma_start(lamv[:, :, :, :].rearrange("p l a k -> p (l a k)"), lam_in).then_inc(small_loaded, 16)
            for n in range(RING):
                load_unit(n, first=n < RAW)
            for a in range(2, N_ADA):
                load_ada(a)

            def units(a, b):
                with sp.Fori(0, (b - a) // RING) as i:
                    for j in range(RING):
                        load_unit(a + j, i)

            done = RING
            units(done, up_unit(0, 0) + RING)
            sp.wait_ge(h_lo_done, norm_counts(2)[1])
            sp.dma_start(c_bc[:, :, :].rearrange("p a k -> p (a k)"),
                         cc_in.partition_broadcast(P)).then_inc(c_loaded, 16)
            a = N_ADA
            for part, n in enumerate(PARTS):
                u = up_unit(0, part) + RING
                with sp.Fori(0, n // 2) as i:
                    for j in range(4):
                        load_unit(u + j, i)
                        load_ada(a + j, i)
                a += 2 * n
                u = down_unit(0, part) + RING
                if part < len(PARTS) - 1:
                    units(u, u + KT)
                else:
                    for j in range(KT):
                        load_unit(u + j)
                        if j % 2 == 1:
                            load_ada(a + j // 2)
            units(down_unit(0, len(PARTS) - 1) + KT + RING, N_UNITS)

        @block.gpsimd
        def _(pool):
            def split_unit(c, i=0):
                pool.wait_ge(w_hi_done, 4 * i + (c + 1))
                nc.gpsimd.tensor_tensor(w_lo[:, c % RING, :], w_raw[:, c % RAW, :],
                                        w_hi[:, c % RING, :].bitcast(f32), ALU.subtract).then_inc(w_lo_done, 1)

            def units(a, b):
                with pool.Fori(0, (b - a) // RING) as i:
                    for j in range(RING):
                        split_unit(a + j, i)

            for n in range(RING):
                split_unit(n)
            done = RING
            for l in range(DEPTH):
                for p in range(3):
                    upto = in_unit(l, p, 1) + IN_UNITS + RING
                    units(done, upto)
                    done = upto
                    for kind, s in phase_of(l, p)["order"]:
                        if kind != "S" or s["m"]:
                            continue
                        it, sid = s["item"], s["sid"]
                        k = it["k1"] - it["k0"]
                        pool.wait_ge(recip_done, sid + 1)
                        buf = p_sb[:, it["slots"][s["qi"]], 0:k]
                        nc.gpsimd.tensor_tensor(buf, buf, ri[:, sid % 8:sid % 8 + 1].broadcast_to([P, k]),
                                                ALU.mult).then_inc(scaled_done, 1)
                upto = min(up_unit(l, 0) + RING, N_UNITS)
                units(done, upto)
                end = min(unit0(l + 1) + RING, N_UNITS)
                units(upto, end)
                done = end

        scaled_no = {}
        for ph in phases:
            for kind, s in ph["order"]:
                if kind == "S" and s["m"] == 0:
                    scaled_no[s["sid"]] = len(scaled_no) + 1
        comb_no = {}
        for ph in phases:
            for kind, s in ph["order"]:
                if kind == "S" and s["m"] == 1:
                    comb_no[s["sid"]] = len(comb_no) + 1

        def wait_probs(e, it):
            if it["maps"] == 1:
                e.wait_ge(scaled_done, scaled_no[it["S"][-1]["sid"]])
            else:
                e.wait_ge(probs_done, comb_no[it["S"][-1]["sid"]])

        @block.tensor
        def _(pe):
            def spread_stats(s, cols, pieces):
                for k, (bank, col) in enumerate(pieces):
                    g = stat_base(s) + cols + k
                    dg = dgo if s[0] == "sub" else dgn
                    pe.wait_ge(diag_done, g + 1)
                    nc.tensor.matmul(ps[:, bank, col:col + P], ones, dg[:, (cols + k) % 4, :],
                                     start=True, stop=True).then_inc(spread_done, 1)

            def norm_stats(j):
                groups = norms[j]
                pe.wait_ge(sqsum_done, KT * (j + 1))
                for t in range(n_tiles(groups)):
                    mm = nc.tensor.matmul(ps[:, 5, t:t + 1], sqsum[:, t * P:(t + 1) * P], ones[:, 0:1],
                                          start=True, stop=True)
                mm.then_inc(ss_done, 1)
                spread_stats(("norm", j), 0, [(6 + t // 4, (t % 4) * P) for t in range(n_tiles(groups))])

            def three(out, lhs, rhs, first, last):
                (lh, ll), (rh, rl_) = lhs, rhs
                nc.tensor.matmul(out, lh, rh, start=first, stop=False)
                nc.tensor.matmul(out, lh, rl_, start=False, stop=False)
                return nc.tensor.matmul(out, ll, rh, start=False, stop=last)

            def turn_tile(x, last_item=None):
                if "tile" not in x:
                    return
                pe.wait_ge(split_lo_done, x["his"])
                for g, b, m, store in x["groups"]:
                    if g >= 2:
                        pe.wait_ge(qk_stored, g - 1)
                    if last_item is not None:
                        pe.wait_ge(pt_lo_done, last_item["T"][-1]["tid"] + 1)
                        pe.wait_ge(o_done, last_item["id"] + 1)
                        last_item = None
                    for k in range(m):
                        mm = nc.tensor.transpose(ps[:, 6 + g % 2, k * P:(k + 1) * P],
                                                 split[:, x["tile"] % 2, b + k, :, :].rearrange("p a d -> p (a d)"),
                                                 ident)
                    mm.then_inc(qk_turned, 1)

            def project(l, p, c):
                ch = chunk_of(l, p, c)
                prev = chunk_of(l, p, 0) if c == 1 else None
                for u in range(IN_UNITS):
                    n = ch["unit"] + u
                    pe.wait_ge(w_lo_done, n + 1)
                    if p == 0 and c == 0:
                        _, hs = norm_counts(2 * l)
                        pe.wait_ge(h_lo_done, hs + 2 * (UNIT_K * u + UNIT_K))
                    for x in ch["tiles"]:
                        t = x["t"]
                        if u == 0:
                            if c == 1:
                                pe.wait_ge(acc_copied, prev["tiles"][t]["acc"] + 1)
                            elif p > 0 and t == 0:
                                last = phase_of(l, p - 1)["items"][-1]
                                pe.wait_ge(exp_done, last["S"][-1]["sid"] + 1)
                                pe.wait_ge(pt_lo_done, last["T"][-1]["tid"] + 1)
                        c0, c1 = x["cols"]
                        for kk in range(UNIT_K):
                            k = UNIT_K * u + kk
                            tok = slice(t * P, (t + 1) * P)
                            col = slice(kk * CHUNK + c0, kk * CHUNK + c1)
                            mm = three(ps[:, t, c0:c1], (h_hi[:, k, tok], h_lo[:, k, tok]),
                                       (w_hi[:, n % RING, col], w_lo[:, n % RING, col]), k == 0, k == KT - 1)
                        if u == IN_UNITS - 1:
                            mm.then_inc(acc_done, 1)
                    if u < IN_UNITS - 1:
                        mm.then_inc(unit_done, 1)
                    if prev and u > 0:
                        for x in prev["tiles"][2 * u - 2:2 * u]:
                            turn_tile(x, phase_of(l, p - 1)["items"][-1] if p > 0 and x["t"] == 0 else None)
                if c == 1:
                    for x in ch["tiles"]:
                        turn_tile(x)

            def attend(l, p):
                ph = phase_of(l, p)
                a, b = chunk_of(l, p, 0), chunk_of(l, p, 1)
                stored_all = [x["groups"][-1][0] + 1 for ch in (a, b) for x in ch["tiles"] if "tile" in x][-1]
                v_all = [x["vn"] + 1 for ch in (a, b) for x in ch["tiles"] if x["v"]][-1]
                pe.wait_ge(qk_stored, stored_all)
                pe.wait_ge(v_lo_done, v_all)
                for kind, s in ph["order"]:
                    it = s["item"]
                    if kind == "S":
                        sid, m = s["sid"], s["m"]
                        if p == 0:
                            qs, ks = it["h"], 8 + 2 * (it["h"] // (A_HEADS // A_KV))
                        else:
                            qs, ks = 2 * it["h"] + m, 4 + 2 * (2 * it["h"] + m)
                        if sid >= 2:
                            pe.wait_ge(exp_done, sid - 1)
                        lhs = qk[:, qs, s["q"] * P:(s["q"] + 1) * P]
                        k0 = it["k0"]
                        while k0 < it["k1"]:
                            k1 = min(k0 + 512, it["k1"])
                            at0 = k0 - it["k0"]
                            dst = ps[:, 2 * (sid % 2) + at0 // 512, 0:k1 - k0]
                            nc.tensor.matmul(dst, lhs, qk[:, ks, k0:k1], start=True, stop=False)
                            mm = nc.tensor.matmul(dst, lhs, qk[:, ks + 1, k0:k1], start=False, stop=True)
                            k0 = k1
                        mm.then_inc(scores_done, 1)
                    elif kind == "T":
                        tid, j = s["tid"], s["j"]
                        if j == 0:
                            wait_probs(pe, it)
                        if tid >= TURNS:
                            pe.wait_ge(pt_lo_done, tid - TURNS + 1)
                        for qi in range(len(it["qt"])):
                            mm = nc.tensor.transpose(ps[:, 4 + tid % TURNS, qi * P:(qi + 1) * P],
                                                     p_sb[:, it["slots"][qi], j * P:(j + 1) * P], ident)
                        mm.then_inc(turned, 1)
                    else:
                        tid, j = s["tid"], s["j"]
                        nq = it["t1"] - it["t0"]
                        if j == 0 and it["id"] >= 1:
                            pe.wait_ge(o_done, it["id"])
                        pe.wait_ge(pt_lo_done, tid + 1)
                        vc = slice(P * (it["h"] // (A_HEADS // A_KV)), P * (it["h"] // (A_HEADS // A_KV)) + P) \
                            if p == 0 else slice(P * it["h"], P * it["h"] + P)
                        mm = three(ps[:, 7, 0:nq], (v_hi[:, s["kt"], vc], v_lo[:, s["kt"], vc]),
                                   (pt_hi[tid % TURNS][:, 0:nq], pt_lo[tid % TURNS][:, 0:nq]), j == 0, j == len(it["T"]) - 1)
                        mm.then_inc(pv_done, 1)

            def sub_stats(l):
                nt = n_tiles(token_groups(l))
                for b in range(B_HEADS):
                    pe.wait_ge(osq_done, sub_sq[l] + b + 1)
                    for t in range(nt):
                        mm = nc.tensor.matmul(ps[:, 5, b * nt + t:b * nt + t + 1], osq[:, b % 2, t * P:(t + 1) * P],
                                              ones[:, 0:1], start=True, stop=True)
                    mm.then_inc(ss_done, 1)
                for b in range(B_HEADS):
                    if b >= 1:
                        pe.wait_ge(o_normed, sub_sq[l] + b)
                    spread_stats(("sub", l), b * nt, [(6 + t // 4, (t % 4) * P) for t in range(nt)])

            def feature_unit(c, i, groups, kn, moving, wait_bank):
                pe.wait_ge(w_lo_done, 4 * i + (c + 1))
                if wait_bank:
                    pe.wait_ge(bank_read, 4 * i + (evac_index(c) - 3))
                mh, ml = moving
                for g, (t0, t1) in enumerate(groups):
                    for k in range(kn):
                        col = slice(k * P, (k + 1) * P)
                        mm = three(ps[:, 2 * (c % 4) + g, 0:t1 - t0], (w_hi[:, c % RING, col], w_lo[:, c % RING, col]),
                                   (mh[:, k, t0:t1], ml[:, k, t0:t1]), k == 0, k == kn - 1)
                mm.then_inc(unit_done, 1)

            pe.wait_ge(small_loaded, 32)
            for l in range(DEPTH):
                groups = token_groups(l)
                if l == 0:
                    norm_stats(0)
                for p in range(3):
                    for c in range(2):
                        project(l, p, c)
                    attend(l, p)
                sub_stats(l)
                pe.wait_ge(o_lo_done, sub_oh[l] + KT * len(groups))
                first = wo_unit(l)
                for j in range(RING):
                    feature_unit(first + j, 0, groups, KT, (oh, ol), False)
                for j in range(RING):
                    feature_unit(first + RING + j, 0, groups, KT, (oh, ol), True)
                norm_stats(2 * l + 1)
                _, hs = norm_counts(2 * l + 1)
                for part, n in enumerate(PARTS):
                    if part == 0:
                        pe.wait_ge(h_lo_done, hs + KT * len(groups))
                    with pe.Fori(0, n // 2) as i:
                        for j in range(RING):
                            feature_unit(up_unit(l, part) + j, i, groups, KT, (h_hi, h_lo), True)
                    pe.wait_ge(a_lo_done, 1 + l * FF_TILES + sum(PARTS[:part + 1]))
                    with pe.Fori(0, KT // RING) as i:
                        for j in range(RING):
                            feature_unit(down_unit(l, part) + j, i, groups, n, (a_hi, a_lo), True)
                norm_stats(2 * l + 2)

        @block.scalar
        def _(act):
            A = nc.scalar.activation
            step = Steps(act, act_step)

            def unit_hi(c, i=0):
                half = (c - c % RING) // 2
                if c >= RING:
                    wait_unit(act, c - RING, i)
                act.wait_ge(w_loaded[c % RAW], 32 * i + 16 * (c // RAW + 1))
                A(w_hi[:, c % RING, :], w_raw[:, c % RAW, :], ACT.Copy).then_inc(w_hi_done, 1)

            def stats_sd(s, cols, width, n):
                ss_no = {("norm", 0): 1}
                k = 1
                for r in stat_order[1:]:
                    k += B_HEADS if r[0] == "sub" else 1
                    ss_no[r] = k
                act.wait_ge(ss_done, ss_no[s])
                A(n_sd[:, 0:cols], ps[:, 5, 0:cols], ACT.Sqrt, bias=eps[:, :], scale=1.0 / width).then_inc(sd_done, 1)

            def norm_hi(j):
                groups = norms[j]
                _, hs = norm_counts(j)
                l = j // 2
                sh = 0 if j % 2 == 0 else 3 * KT
                stats_sd(("norm", j), n_tiles(groups), D, j)
                if j == len(norms) - 1:
                    return
                for k in range(KT):
                    for g, (t0, t1) in enumerate(groups):
                        n = hs + k * len(groups) + g
                        act.wait_ge(ht_done, n + 1)
                        A(h_hi[:, k, t0:t1], ht[:, k % 2, t0:t1], ACT.Identity,
                          bias=mod[:, l, g, sh + k:sh + k + 1]).then_inc(h_hi_done, 1)

            def square_x(d, j, groups, i=0):
                T = groups[-1][1]
                n = KT * j + d
                if not (isinstance(i, int) and n < 2):
                    act.wait_ge(sqsum_done, 4 * i + (n - 1))
                A(sqt[:, d % 2, 0:T], x_sb[:, 4 * i + d, 0:T], ACT.Square).then_inc(sq_done, 1)

            def tile_hi(x, l):
                if x["v"]:
                    s0, n = x["v"]
                    act.wait_ge(acc_copied, x["acc"] + 1)
                    if n == 2:
                        src = raw[:, x["t"], s0 * HD:(s0 + 2) * HD].rearrange("p (k d) -> p k d", k=2) \
                            .unsqueeze(2).broadcast_to([P, 2, 2, HD])
                        dst = v_hi[:, x["t"], :].rearrange("p (k a d) -> p k a d", k=2, a=2)
                    else:
                        src = raw[:, x["t"], s0 * HD:(s0 + n) * HD]
                        dst = v_hi[:, x["t"], :]
                    A(dst, src, ACT.Copy).then_inc(v_hi_done, 1)
                if "tile" not in x:
                    return
                b = 0
                i = x["tile"] % 2
                act.wait_ge(rope_done, x["tile"] + 1)
                if x["tile"] >= 2:
                    act.wait_ge(qk_turned, x["prev2"])
                for s0, n, kind, _ in x["maps"]:
                    u = roped[:, i, s0:s0 + n, :]
                    if kind == "q":
                        ins = A(split[:, i, b:b + n, 0, :].bitcast(f32r), u, ACT.Copy, scale=SCALE)
                        b += n
                    else:
                        dst = split[:, i, b:b + 2 * n:2, :, :].bitcast(f32r)
                        ins = A(dst, u.unsqueeze(2).broadcast_to([P, n, 2, HD]), ACT.Copy)
                        b += 2 * n
                    ins.then_inc(split_hi_done, 1)

            def tile_store(x):
                for g, b, m, store in x.get("groups", []):
                    act.wait_ge(qk_turned, g + 1)
                    A(qk[:, store:store + m, x["t"] * P:(x["t"] + 1) * P],
                      ps[:, 6 + g % 2, 0:m * P].rearrange("p (m t) -> p m t", m=m), ACT.Copy).then_inc(qk_stored, 1)

            tiles = [x for ch in chunks for x in ch["tiles"] if "tile" in x]
            for n, x in enumerate(tiles):
                if n >= 2:
                    x["prev2"] = tiles[n - 2]["groups"][-1][0] + 1

            def chunk_copies(ch):
                q, l, p, c = ch["q"], ch["l"], ch["p"], ch["c"]
                for x in ch["tiles"]:
                    act.wait_ge(acc_done, x["acc"] + 1)
                    if c == 1:
                        y = chunk_of(l, p, 0)["tiles"][x["t"]]
                        if "tile" in y:
                            act.wait_ge(rope_done, y["tile"] + 1)
                        if y["v"]:
                            act.wait_ge(v_lo_done, y["vn"] + 1)
                    elif p > 0 and x["t"] == 0:
                        last = phase_of(l, p - 1)["items"][-1]
                        act.wait_ge(pv_done, last["T"][-1]["tid"] + 1)
                    c0, c1 = x["cols"]
                    A(raw[:, x["t"], c0:c1], ps[:, x["t"], c0:c1], ACT.Copy).then_inc(acc_copied, 1)
                if p == 0:
                    full = [x for x in ch["tiles"] if x["cols"][1] == CHUNK]
                    act.wait_ge(acc_copied, ch["tiles"][-1]["acc"] + 1)
                    n = len(full)
                    ins = A(rawsq[:, 0:n, :], raw[:, 0:n, :], ACT.Square)
                    if n < len(ch["tiles"]):
                        ins = A(rawsq[:, n:, 0:256], raw[:, n:6, 0:256], ACT.Square)
                    ins.then_inc(raw_squared, 1)

            def head_sd_step(ch):
                if ch["p"] == 0:
                    k = 2 * ch["l"] + ch["c"]
                    act.wait_ge(head_ss_done, k + 1)
                    n = 36 if len(ch["tiles"]) == 6 else 24
                    A(head_sd[:, 0:n], head_ss[:, 0:n], ACT.Sqrt, bias=eps[:, :], scale=1.0 / HD) \
                        .then_inc(head_sd_done, 1)

            def project(l, p, c):
                ch = chunk_of(l, p, c)
                prev = chunk_of(l, p, 0) if c == 1 else None
                for u in range(IN_UNITS):
                    n = ch["unit"] + u
                    if prev and u == 0:
                        head_sd_step(prev)
                    xs = prev["tiles"][2 * u - 2:2 * u] if prev and u > 0 else []
                    if u == IN_UNITS - 1:
                        for x in xs:
                            tile_hi(x, l)
                            tile_store(x)
                        chunk_copies(ch)
                        unit_hi(n + RING)
                    else:
                        for x in xs:
                            tile_hi(x, l)
                        unit_hi(n + RING)
                        for x in xs:
                            tile_store(x)
                if c == 1:
                    head_sd_step(ch)
                    for x in ch["tiles"]:
                        tile_hi(x, l)
                        tile_store(x)

            def attend(l, p):
                waiting = []

                def exponentials(s):
                    it, sid, m = s["item"], s["sid"], s["m"]
                    k = it["k1"] - it["k0"]
                    act.wait_ge(bias_done, sid + 1)
                    if m == 0:
                        dst = p_sb[:, it["slots"][s["qi"]], 0:k]
                        before = it["freed_by"][s["qi"]]
                        if before:
                            act.wait_ge(turned, before["T"][-1]["tid"] + 1)
                    else:
                        dst = ptmp[:, 0:k]
                        if comb_no[sid] > 1:
                            act.wait_ge(probs_done, comb_no[sid] - 1)
                    src = ps[:, 2 * (sid % 2):2 * (sid % 2) + 2, :].rearrange("p a b -> p (a b)")[:, 0:k]
                    A(dst, src, ACT.Exp, bias=nb[:, sid % 8:sid % 8 + 1],
                      accum_out=rs[:, sid % 8:sid % 8 + 1]).then_inc(exp_done, 1)

                for kind, s in phase_of(l, p)["order"]:
                    it = s["item"]
                    if kind == "S":
                        while waiting:
                            exponentials(waiting.pop(0))
                        waiting.append(s)
                    elif kind == "T":
                        if s["j"] == 0:
                            while waiting and waiting[0]["item"] is it:
                                exponentials(waiting.pop(0))
                        tid = s["tid"]
                        nq = it["t1"] - it["t0"]
                        act.wait_ge(turned, tid + 1)
                        if tid >= TURNS:
                            act.wait_ge(pv_done, tid - TURNS + 1)
                        A(pt_hi[tid % TURNS][:, 0:nq], ps[:, 4 + tid % TURNS, 0:nq], ACT.Copy).then_inc(pt_hi_done, 1)
                        while waiting:
                            exponentials(waiting.pop(0))
                    elif s["j"] == len(it["T"]) - 1:
                        while waiting:
                            exponentials(waiting.pop(0))
                        act.wait_ge(pv_done, s["tid"] + 1)
                        nq = it["t1"] - it["t0"]
                        if p == 0:
                            r = slice(HD * (it["h"] % 2), HD * (it["h"] % 2) + HD)
                            A(o_sb[r, it["h"] // 2, it["t0"]:it["t1"]], ps[r, 7, 0:nq], ACT.Copy).then_inc(o_done, 1)
                        else:
                            A(o_sb[:, 4 + 2 * (p - 1) + it["h"], it["t0"]:it["t1"]], ps[:, 7, 0:nq], ACT.Copy) \
                                .then_inc(o_done, 1)

            act.wait_ge(c_loaded, 16)
            A(c_bc[:, :, :], c_bc[:, :, :], ACT.Silu).then_inc(c_ready, 1)
            for n in range(RING):
                unit_hi(n)
            act.wait_ge(lam_sum, 1)
            A(lamw[:, :], lamw[:, :], ACT.Exp).then_inc(lam_exp, 1)
            act.wait_ge(x_loaded, 16)
            for d in range(KT):
                square_x(d, 0, norms[0])
            norm_hi(0)
            for l in range(DEPTH):
                groups = token_groups(l)
                T = groups[-1][1]
                for p in range(3):
                    for c in range(2):
                        project(l, p, c)
                    attend(l, p)
                last_item = phase_of(l, 2)["items"][-1]
                act.wait_ge(pv_done, last_item["T"][-1]["tid"] + 1)
                if l == 0:
                    act.dma_start(x_sb[:, :, :], x_in).then_inc(x_loaded, 16)
                else:
                    act.wait_ge(x_spilled, 16)
                    act.dma_start(x_sb[:, :, 0:SEQ], x_spill).then_inc(x_loaded, 16)
                act.wait_ge(o_done, last_item["id"] + 1)
                for b in range(B_HEADS):
                    if b >= 2:
                        act.wait_ge(ss_done, 1 + (B_HEADS + 2) * l + b - 1)
                    A(osq[:, b % 2, 0:T], o_sb[:, 4 + b, 0:T], ACT.Square).then_inc(osq_done, 1)
                stats_sd(("sub", l), B_HEADS * n_tiles(groups), B_HEADS * 32, l)
                for k in range(KT):
                    if k >= 4:
                        act.wait_ge(o_normed, sub_sq[l] + k - 3)
                    for g, (t0, t1) in enumerate(groups):
                        A(oh[:, k, t0:t1], o_sb[:, k, t0:t1], ACT.Copy).then_inc(o_hi_done, 1)
                for d in range(KT):
                    act.wait_ge(bank_read, evac_index(wo_unit(l) + d) + 1)
                    unit_hi(wo_unit(l) + d + RING)
                    square_x(d, 2 * l + 1, groups)
                norm_hi(2 * l + 1)
                if l == 0:
                    act.wait_ge(c_loaded, 32)
                    A(c_bc[:, :, :], c_bc[:, :, :], ACT.Silu).then_inc(c_ready, 1)
                for part, n in enumerate(PARTS):
                    pair0 = l * FF_TILES + sum(PARTS[:part])

                    A(act_scrap[:, :], sm[:, 0:1], ACT.Silu)

                    def pairs(i, part=part, pair0=pair0, groups=groups, T=T, l=l):
                        for half in range(2):
                            for gv, buf in enumerate((conv_g, conv_v)):
                                c = up_unit(l, part) + 2 * half + gv
                                wcol = S_CONV + (l * 2 * FF_TILES + gv * FF_TILES + sum(PARTS[:part]) + half) * 4
                                wait_unit(act, c, i)
                                act.wait_ge(a_lo_done, 2 * i + (pair0 + half + 1))
                                for g, (t0, t1) in enumerate(groups):
                                    ins = A(buf[:, t0:t1], ps[:, 2 * (c % 4) + g, 0:t1 - t0], ACT.Identity,
                                            bias=sm[:, bass.ds(8 * i + (wcol + 3), 1)],
                                            scale=sm[:, bass.ds(8 * i + (wcol + 1), 1)])
                                ins.then_inc(conv_started, 1)
                                unit_hi(c + RING, i)
                            act.wait_ge(bank_read, 4 * i + (evac_index(up_unit(l, part) + 2 * half) + 1))
                            A(conv_g[:, 0:T], conv_g[:, 0:T], ACT.Silu).then_inc(silu_done, 1)
                            act.wait_ge(prod_done, 2 * i + (pair0 + half + 1))
                            A(a_hi[:, 2 * i + half, 0:T], conv_g[:, 0:T], ACT.Copy).then_inc(a_hi_done, 1)

                    step.loop(n // 2, 0, pairs)
                    last_part = part == len(PARTS) - 1
                    for d in range(KT):
                        c = down_unit(l, part) + d
                        if c + RING < N_UNITS:
                            unit_hi(c + RING)
                        if last_part:
                            act.wait_ge(bank_read, evac_index(c) + 1)
                            square_x(d, 2 * l + 2, norms[2 * l + 2])
                if l == 0:
                    act.wait_ge(bank_read, evac_index(down_unit(0, len(PARTS) - 1) + KT - 1) + 1)
                    act.dma_start(x_spill, x_sb[:, :, 0:SEQ]).then_inc(x_spilled, 16)
                norm_hi(2 * l + 2)
                if l == 0:
                    act.wait_ge(x_spilled, 16)
            for k in range(KT):
                act.wait_ge(y_done, k + 1)
                act.dma_start(out[:, k, :], y_sb[:, k, :]).then_inc(stored, 16)
            act.wait_ge(stored, 16 * KT)

        @block.vector
        def _(dve):
            V = nc.vector
            step = Steps(dve, dve_step)

            def ada_tile(c, streams, i, dst):
                dve.wait_ge(ada_loaded[c % 2], 32 * i + 16 * (c // 2 + 1))
                if not isinstance(i, int) or c > 0:
                    dve.wait_ge(ada_used, 4 * i + c)
                for s in range(streams):
                    o = ada_junk[:, :]
                    ins = V.tensor_tensor_reduce(o, ada_b[c % 2][:, :], c_bc[:, s, :], 1.0, 0.0, ALU.mult, ALU.add,
                                                 dst(s))
                    if s == streams - 1:
                        ins.then_inc(ada_used, 1)
                    else:
                        step(ins)

            def finish_mod(l):
                streams = 2
                dve.wait_ge(ada_used, N_ADA * (l + 1))
                for s in range(streams):
                    n = N_ADA if s == 0 or l < DEPTH - 1 else 2 * KT
                    b = S_BADA + l * N_ADA
                    step(V.tensor_tensor(mod[:, l, s, 0:n], mod[:, l, s, 0:n], sm[:, b:b + n], ALU.add))
                    step(V.scalar_tensor_tensor(gs1[:, s, :], mod[:, l, s, KT:2 * KT], 1.0,
                                                sm[:, S_GATTN + l * KT:S_GATTN + (l + 1) * KT], ALU.add, ALU.mult))
                    if n == N_ADA:
                        step(V.scalar_tensor_tensor(gs2[:, s, :], mod[:, l, s, 4 * KT:5 * KT], 1.0,
                                                    sm[:, S_GFFN + l * KT:S_GFFN + (l + 1) * KT], ALU.add, ALU.mult))

            cos = sm[:, S_COS:S_COS + 4 * HD].rearrange("p (t d) -> p t d", t=4)
            sin = sm[:, S_SIN:S_SIN + 4 * HD].rearrange("p (t d) -> p t d", t=4)

            def rope_tables(l):
                for n, col in enumerate((S_GQ, S_GK)):
                    g = sm[:, col + l * HD:col + (l + 1) * HD]
                    step(V.tensor_tensor(tabs[:, 2 * n, :, :], cos, g.unsqueeze(1).broadcast_to([P, 4, HD]), ALU.mult))
                    gv = g.rearrange("p (a b d) -> p a b d", a=2, b=2)
                    for t in range(4):
                        sv = sm[:, S_SIN + t * HD:S_SIN + (t + 1) * HD].rearrange("p (a b d) -> p a b d", a=2, b=2)
                        ov = tabs[:, 2 * n + 1, t, :].rearrange("p (a b d) -> p a b d", a=2, b=2)
                        for b in range(2):
                            step(V.tensor_tensor(ov[:, :, b, :], sv[:, :, b, :], gv[:, :, 1 - b, :], ALU.mult))

            def stats_scales(s, cols, banks_of):
                no = stat_index(s) + 1
                dve.wait_ge(sd_done, no)
                step(V.reciprocal(n_r[:, 0:cols], n_sd[:, 0:cols]))

            def diag(s, k):
                g = stat_base(s) + k
                dg = dgo if s[0] == "sub" else dgn
                if k >= 4:
                    dve.wait_ge(spread_done, g - 3)
                V.tensor_scalar(dg[:, k % 4, :], ident, n_r[:, k:k + 1], None, ALU.mult).then_inc(diag_done, 1)

            def add_squares(d, j, groups, i=0):
                T = groups[-1][1]
                dve.wait_ge(sq_done, 4 * i + (KT * j + d + 1))
                if not (isinstance(i, int) and d == 0):
                    dve.wait_ge(sqsum_done, KT * j + d)
                    V.tensor_tensor(sqsum[:, 0:T], sqsum[:, 0:T], sqt[:, d % 2, 0:T], ALU.add).then_inc(sqsum_done, 1)
                else:
                    V.tensor_copy(sqsum[:, 0:T], sqt[:, d % 2, 0:T]).then_inc(sqsum_done, 1)

            def norm(j):
                groups = norms[j]
                s = ("norm", j)
                nt = n_tiles(groups)
                _, hs = norm_counts(j)
                l = j // 2
                gs = gs1 if j % 2 == 0 else gs2
                sh = 0 if j % 2 == 0 else 3 * KT
                final = j == len(norms) - 1
                stats_scales(s, nt, None)
                for t in range(nt):
                    diag(s, t)

                def lo(k, g):
                    t0, t1 = groups[g]
                    dve.wait_ge(h_hi_done, hs + k * len(groups) + g + 1)
                    V.scalar_tensor_tensor(h_lo[:, k, t0:t1], ht[:, k % 2, t0:t1], mod[:, l, g, sh + k:sh + k + 1],
                                           h_hi[:, k, t0:t1].bitcast(f32), ALU.add, ALU.subtract).then_inc(h_lo_done, 1)

                dve.wait_ge(spread_done, stat_base(s) + nt)
                for k in range(KT):
                    for g, (t0, t1) in enumerate(groups):
                        scale = sm[:, S_GFIN + k:S_GFIN + k + 1] if final else gs[:, g, k:k + 1]
                        if final:
                            dst, done = y_sb[:, k, t0:t1], y_done
                        else:
                            dst, done = ht[:, k % 2, t0:t1], ht_done
                            if k >= 2:
                                dve.wait_ge(h_lo_done, hs + (k - 2) * len(groups) + g + 1)
                        V.scalar_tensor_tensor(dst, x_sb[:, k, t0:t1], scale, ps[:, 6 + g, 0:t1 - t0],
                                               ALU.mult, ALU.mult).then_inc(done, 1)
                    if k >= 1 and not final:
                        for g in range(len(groups)):
                            lo(k - 1, g)
                if not final:
                    for g in range(len(groups)):
                        lo(KT - 1, g)

            def head_norms(ch):
                k = 2 * ch["l"] + ch["c"]
                dve.wait_ge(raw_squared, k + 1)
                nt = len(ch["tiles"])
                rows = [(0, nt, 0, 6)] if ch["tiles"][-1]["cols"][1] == CHUNK else [(0, 4, 0, 6), (4, 6, 0, 4)]
                sq = rawsq[:, :, :].rearrange("p t (s d) -> p t s d", d=HD)
                ssv = head_ss[:, :].rearrange("p (t s) -> p t s", s=6)
                if len(rows) > 1:
                    step(V.memset(head_ss[:, :], 1.0))
                for n, (a, b, s0, s1) in enumerate(rows):
                    ins = V.tensor_reduce(ssv[:, a:b, s0:s1], sq[:, a:b, s0:s1, :], AX.X, ALU.add)
                    if n == len(rows) - 1:
                        ins.then_inc(head_ss_done, 1)
                dve.wait_ge(head_sd_done, k + 1)
                n = 36 if nt == 6 else 24
                step(V.reciprocal(head_r[:, 0:n], head_sd[:, 0:n]))

            def rope_tile(ch, x):
                t, i = x["t"], x["tile"] % 2
                if x["tile"] >= 1:
                    dve.wait_ge(rope_done, x["tile"])
                if x["tile"] >= 2:
                    dve.wait_ge(split_lo_done, x["prev2_his"])
                p = ch["p"]
                last = len(x["maps"]) - 1
                for n, (s0, m, kind, _) in enumerate(x["maps"]):
                    src = raw[:, t, s0 * HD:(s0 + m) * HD].rearrange("p (m d) -> p m d", m=m)
                    if p == 0:
                        r = head_r[:, 6 * t + s0:6 * t + s0 + m].unsqueeze(2).broadcast_to([P, m, HD])
                        step(V.tensor_tensor(src, src, r, ALU.mult))
                    dst = roped[:, i, s0:s0 + m, :]
                    if t >= SEQ // P:
                        if p == 0:
                            col = (S_GQ if kind == "q" else S_GK) + ch["l"] * HD
                            ins = V.tensor_tensor(dst, src, sm[:, col:col + HD].unsqueeze(1).broadcast_to([P, m, HD]),
                                                  ALU.mult)
                        else:
                            ins = V.tensor_copy(dst, src)
                    else:
                        if p == 0:
                            w = 0 if kind == "q" else 2
                            ct, st = tabs[:, w, t, :], tabs[:, w + 1, t, :]
                        else:
                            ct, st = cos[:, t, :], sin[:, t, :]
                        r1 = rope1[:, s0:s0 + m, :]
                        step.mark(V.tensor_tensor(r1, src, ct.unsqueeze(1).broadcast_to([P, m, HD]), ALU.mult))
                        sv = src.rearrange("p m (a b d) -> p m a b d", a=2, b=2)
                        tv = st.rearrange("p (a b d) -> p a b d", a=2, b=2)
                        ov = rope2[:, s0:s0 + m, :].rearrange("p m (a b d) -> p m a b d", a=2, b=2)
                        for b in range(2):
                            step.mark(V.tensor_tensor(ov[:, :, :, b, :], sv[:, :, :, 1 - b, :],
                                                      tv[:, :, b, :].unsqueeze(1).broadcast_to([P, m, 2, 16]),
                                                      ALU.mult))
                        step.wait()
                        ins = V.tensor_tensor(dst, r1, rope2[:, s0:s0 + m, :], ALU.add)
                    if n == last:
                        ins.then_inc(rope_done, 1)
                    else:
                        step.mark(ins)

            def tile_lo(x):
                i = x["tile"] % 2
                b = 0
                for n, (s0, m, kind, _) in enumerate(x["maps"]):
                    dve.wait_ge(split_hi_done, x["his"] - len(x["maps"]) + n + 1)
                    u = roped[:, i, s0:s0 + m, :]
                    if kind == "q":
                        ins = V.scalar_tensor_tensor(split[:, i, b:b + m, 1, :], u, SCALE, split[:, i, b:b + m, 0, :],
                                                     ALU.mult, ALU.subtract)
                        b += m
                    else:
                        ins = V.tensor_tensor(split[:, i, b + 1:b + 2 * m:2, :, :],
                                              u.unsqueeze(2).broadcast_to([P, m, 2, HD]),
                                              split[:, i, b:b + 2 * m:2, :, :], ALU.subtract)
                        b += 2 * m
                    ins.then_inc(split_lo_done, 1)

            def values_lo(x):
                s0, n = x["v"]
                t = x["t"]
                dve.wait_ge(v_hi_done, x["vn"] + 1)
                if n == 2:
                    src = raw[:, t, s0 * HD:(s0 + 2) * HD].rearrange("p (k d) -> p k d", k=2)
                    hv = v_hi[:, t, :].bitcast(f32).rearrange("p (k a d) -> p k a d", k=2, a=2)
                    lv = v_lo[:, t, :].rearrange("p (k a d) -> p k a d", k=2, a=2)
                    for a in range(2):
                        ins = V.tensor_tensor(lv[:, :, a, :], src, hv[:, :, a, :], ALU.subtract)
                else:
                    ins = V.tensor_tensor(v_lo[:, t, :], raw[:, t, s0 * HD:(s0 + n) * HD],
                                          v_hi[:, t, :].bitcast(f32), ALU.subtract)
                ins.then_inc(v_lo_done, 1)

            tiles = [x for ch in chunks for x in ch["tiles"] if "tile" in x]
            for n, x in enumerate(tiles):
                if n >= 2:
                    x["prev2_his"] = tiles[n - 2]["his"]

            def project(l, p, c):
                ch = chunk_of(l, p, c)
                if p == 0:
                    head_norms(ch)
                before = None
                for x in ch["tiles"]:
                    if "tile" in x:
                        if p > 0:
                            dve.wait_ge(acc_copied, x["acc"] + 1)
                        rope_tile(ch, x)
                    if before:
                        tile_lo(before)
                    before = x if "tile" in x else None
                    if x["v"]:
                        values_lo(x)
                if before:
                    tile_lo(before)

            def attend(l, p):
                def finish(s):
                    it, sid = s["item"], s["sid"]
                    k = it["k1"] - it["k0"]
                    c = slice(sid % 8, sid % 8 + 1)
                    dve.wait_ge(exp_done, sid + 1)
                    ins = V.reciprocal(ri[:, c], rs[:, c])
                    ins.then_inc(recip_done, 1)
                    if s["m"] == 1:
                        dve.wait_ge(recip_done, sid + 1)
                        step(V.tensor_scalar(rl[:, c], ri[:, c], nlam[:, l:l + 1], None, ALU.mult))
                        dve.wait_ge(scaled_done, scaled_no[sid - 1])
                        buf = p_sb[:, it["slots"][s["qi"]], 0:k]
                        V.scalar_tensor_tensor(buf, ptmp[:, 0:k], rl[:, c], buf, ALU.mult, ALU.add) \
                            .then_inc(probs_done, 1)

                def pt_rest(s):
                    tid = s["tid"]
                    nq = s["item"]["t1"] - s["item"]["t0"]
                    dve.wait_ge(pt_hi_done, tid + 1)
                    V.tensor_tensor(pt_lo[tid % TURNS][:, 0:nq], ps[:, 4 + tid % TURNS, 0:nq],
                                    pt_hi[tid % TURNS][:, 0:nq].bitcast(f32), ALU.subtract).then_inc(pt_lo_done, 1)

                sums, rests = [], []
                for kind, s in phase_of(l, p)["order"]:
                    it = s["item"]
                    if kind == "S":
                        sid = s["sid"]
                        k = it["k1"] - it["k0"]
                        dve.wait_ge(scores_done, sid + 1)
                        src = ps[:, 2 * (sid % 2):2 * (sid % 2) + 2, :].rearrange("p a b -> p (a b)")[:, 0:k]
                        V.tensor_reduce(nb[:, sid % 8:sid % 8 + 1], src, AX.X, ALU.max, negate=True) \
                            .then_inc(bias_done, 1)
                        while rests:
                            pt_rest(rests.pop(0))
                        while sums:
                            finish(sums.pop(0)[0])
                        sums.append([s, 0])
                    elif kind == "T":
                        while sums and (sums[0][0]["item"] is it or sums[0][1]):
                            finish(sums.pop(0)[0])
                        for r in sums:
                            r[1] += 1
                        while rests:
                            pt_rest(rests.pop(0))
                        rests.append(s)
                    elif rests and rests[0] is s:
                        pt_rest(rests.pop(0))
                assert not sums and not rests

            step.mark(V.memset(eps[:, :], EPS))
            V.memset(zero[:, :], 0.0).then_inc(a_lo_done, 1)
            dve.wait_ge(small_loaded, 32)
            for l in range(DEPTH):
                for n in range(2):
                    step(V.tensor_tensor_reduce(ht[:, 0, 0:HD],
                                                lamv[:, l, 2 * n, :], lamv[:, l, 2 * n + 1, :], 1.0, 0.0,
                                                ALU.mult, ALU.add, lamw[:, 2 * l + n:2 * l + n + 1]))
            V.tensor_scalar(gsub[:, 0:1], sm[:, S_GSUB:S_GSUB + 1], 1.0 - LAM_INIT[0], None, ALU.mult) \
                .then_inc(lam_sum, 1)
            step(V.tensor_scalar(gsub[:, 1:2], sm[:, S_GSUB + 1:S_GSUB + 2], 1.0 - LAM_INIT[1], None, ALU.mult))
            dve.wait_ge(c_ready, 1)
            for a in range(N_ADA):
                ada_tile(a, 2, 0, lambda s: mod[:, 0, s, a:a + 1])
            finish_mod(0)
            rope_tables(0)
            dve.wait_ge(lam_exp, 1)
            for l in range(DEPTH):
                step(V.tensor_tensor(nlam[:, l:l + 1], lamw[:, 2 * l + 1:2 * l + 2], lamw[:, 2 * l:2 * l + 1],
                                     ALU.subtract))
                step(V.tensor_scalar(nlam[:, l:l + 1], nlam[:, l:l + 1], -LAM_INIT[l], None, ALU.add))
            for d in range(KT):
                add_squares(d, 0, norms[0])
            norm(0)
            for l in range(DEPTH):
                groups = token_groups(l)
                T = groups[-1][1]
                nt = n_tiles(groups)
                for p in range(3):
                    for c in range(2):
                        project(l, p, c)
                    attend(l, p)
                s = ("sub", l)
                stats_scales(s, B_HEADS * nt, None)

                def o_lo(k):
                    for g, (t0, t1) in enumerate(groups):
                        dve.wait_ge(o_hi_done, sub_oh[l] + k * len(groups) + g + 1)
                        V.tensor_tensor(ol[:, k, t0:t1], o_sb[:, k, t0:t1], oh[:, k, t0:t1].bitcast(f32),
                                        ALU.subtract).then_inc(o_lo_done, 1)

                for b in range(B_HEADS):
                    for t in range(nt):
                        diag(s, b * nt + t)
                    dve.wait_ge(spread_done, stat_base(s) + (b + 1) * nt)
                    for g, (t0, t1) in enumerate(groups):
                        ins = V.scalar_tensor_tensor(o_sb[:, 4 + b, t0:t1], o_sb[:, 4 + b, t0:t1], gsub[:, l:l + 1],
                                                     ps[:, 6 + g, 0:t1 - t0], ALU.mult, ALU.mult)
                    ins.then_inc(o_normed, 1)
                for k in range(KT):
                    o_lo(k)

                def update(c, gate, i=0, x_col=0):
                    wait_unit(dve, c, i)
                    for g, (t0, t1) in enumerate(groups):
                        xs = x_sb[:, 4 * i + x_col, t0:t1]
                        ins = V.scalar_tensor_tensor(xs, ps[:, 2 * (c % 4) + g, 0:t1 - t0],
                                                     mod[:, l, g, bass.ds(4 * i + (gate + x_col), 1)],
                                                     xs, ALU.mult, ALU.add)
                    ins.then_inc(bank_read, 1)

                dve.wait_ge(x_loaded, 16 * (l + 2))
                for d in range(KT):
                    update(wo_unit(l) + d, 2 * KT, 0, d)
                    add_squares(d, 2 * l + 1, groups)
                norm(2 * l + 1)
                if l == 0:
                    dve.wait_ge(c_ready, 2)
                for part, n in enumerate(PARTS):
                    pair0 = l * FF_TILES + sum(PARTS[:part])
                    ada0 = N_ADA + 2 * sum(PARTS[:part])

                    def pairs(i, part=part, pair0=pair0, l=l, groups=groups, T=T, ada0=ada0):
                        for half in range(2):
                            for gv, buf in enumerate((conv_g, conv_v)):
                                c = up_unit(l, part) + 2 * half + gv
                                wcol = S_CONV + (l * 2 * FF_TILES + gv * FF_TILES + sum(PARTS[:part]) + half) * 4
                                dve.wait_ge(conv_started, 4 * i + (2 * (pair0 + half) + gv + 1))
                                for tap in range(2):
                                    w = wcol + 2 * tap
                                    for g, (t0, t1) in enumerate(groups):
                                        dst = buf[:, t0 + 1:t1] if tap == 0 else buf[:, t0:t1 - 1]
                                        n_ = t1 - t0
                                        src = ps[:, 2 * (c % 4) + g, 0:n_ - 1] if tap == 0 else \
                                            ps[:, 2 * (c % 4) + g, 1:n_]
                                        ins = V.scalar_tensor_tensor(dst, src, sm[:, bass.ds(8 * i + w, 1)], dst,
                                                                     ALU.mult, ALU.add)
                                        if tap == 0 or g < len(groups) - 1:
                                            step.mark(ins)
                                    if tap == 0:
                                        step.wait()
                                ins.then_inc(bank_read, 1)
                            dve.wait_ge(silu_done, 2 * i + (pair0 + half + 1))
                            dve.wait_ge(bank_read, 4 * i + (evac_index(c) + 1))
                            V.tensor_tensor(conv_g[:, 0:T], conv_g[:, 0:T], conv_v[:, 0:T], ALU.mult) \
                                .then_inc(prod_done, 1)
                            dve.wait_ge(a_hi_done, 2 * i + (pair0 + half + 1))
                            V.tensor_tensor(a_lo[:, 2 * i + half, 0:T], conv_g[:, 0:T],
                                            a_hi[:, 2 * i + half, 0:T].bitcast(f32), ALU.subtract).then_inc(a_lo_done, 1)
                            if l == 0:
                                for j in range(2):
                                    a = ada0 + 2 * half + j
                                    ada_tile(a, 2 if part == 0 else 1, i,
                                             lambda s: ada_sum[:, s, 2 * half + j:2 * half + j + 1])
                        if l == 0:
                            dve.wait_ge(ada_used, 4 * i + (ada0 + 4))
                            for s in range(2 if part == 0 else 1):
                                step(V.tensor_copy(mod[:, 1, s, bass.ds(4 * i + (ada0 - N_ADA), 4)], ada_sum[:, s, :]))

                    per = 2 * 2 * (len(groups) + len(groups) - 1)
                    if l == 0:
                        per += 6 if part == 0 else 1
                    step.loop(n // 2, per, pairs)
                    for d in range(KT):
                        c = down_unit(l, part) + d
                        update(c, 5 * KT, 0, d)
                        if part == len(PARTS) - 1:
                            add_squares(d, 2 * l + 2, norms[2 * l + 2])
                            if l == 0 and d % 2 == 1:
                                a = ada0 + 2 * n + d // 2
                                ada_tile(a, 1, 0, lambda s: mod[:, 1, s, a - N_ADA:a - N_ADA + 1])
                if l == 0:
                    finish_mod(1)
                    rope_tables(1)
                norm(2 * l + 2)


_OUT_SHAPE = (P, KT, SEQ)


def kernel(x, c, ctx, c_ctx, w_ada, b_ada, g_attn, w_in, g_qa, g_ka, lam_q1, lam_k1, lam_q2, lam_k2,
           g_sub, w_o, g_ffn, w_up, conv_w, conv_b, w_down, g_final):
    import numpy as np
    import concourse.bacc as bacc
    from concourse import mybir as mb
    from concourse.bass_utils import run_bass_kernel_spmd

    f = np.float32

    def feature_cols(v):
        v = np.asarray(v)
        return np.moveaxis(v.reshape(v.shape[:-1] + (-1, P)), -1, 0)

    def tiles(w):
        k, n = w.shape
        return w.reshape(k // P, P, n // P, P).transpose(2, 1, 0, 3).reshape(n // P, P, k)

    tok = np.concatenate([np.asarray(x)[0], np.asarray(ctx)[0]], axis=0)
    x_arr = np.ascontiguousarray(tok.T.reshape(KT, P, TOK).transpose(1, 0, 2))
    cc = np.concatenate([np.asarray(c)[0], np.asarray(c_ctx)])
    pos = np.arange(SEQ)
    quarter = HD // 4
    inv = (f(10000.0) ** (-np.arange(quarter, dtype=f) / f(quarter))).astype(f)
    ang_r = (pos // GRID_W).astype(f)[:, None] * inv[None]
    ang_c = (pos % GRID_W).astype(f)[:, None] * inv[None]
    cos = np.concatenate([np.cos(ang_r)] * 2 + [np.cos(ang_c)] * 2, -1).astype(f)
    sin = np.concatenate([-np.sin(ang_r), np.sin(ang_r), -np.sin(ang_c), np.sin(ang_c)], -1).astype(f)

    sm = np.zeros((P, S_END), f)
    sm[:, S_IDENT:S_IDENT + P] = np.eye(P, dtype=f)
    sm[:, S_ONES:S_ONES + P] = 1
    sm[:, S_COS:S_COS + 4 * HD] = cos.reshape(4, P, HD).transpose(1, 0, 2).reshape(P, -1)
    sm[:, S_SIN:S_SIN + 4 * HD] = sin.reshape(4, P, HD).transpose(1, 0, 2).reshape(P, -1)
    sm[:, S_BADA:S_GATTN] = feature_cols(b_ada).reshape(P, -1)
    sm[:, S_GATTN:S_GFFN] = feature_cols(g_attn).reshape(P, -1)
    sm[:, S_GFFN:S_GFIN] = feature_cols(g_ffn).reshape(P, -1)
    sm[:, S_GFIN:S_CONV] = feature_cols(g_final).reshape(P, -1)
    conv = np.concatenate([np.asarray(conv_w), np.asarray(conv_b)[:, None]], axis=1)
    sm[:, S_CONV:S_GSUB] = feature_cols(conv).transpose(0, 1, 3, 2).reshape(P, -1)
    sm[:, S_GSUB:S_GQ] = np.asarray(g_sub).T
    sm[:, S_GQ:S_GK] = np.asarray(g_qa).reshape(1, -1)
    sm[:, S_GK:S_END] = np.asarray(g_ka).reshape(1, -1)
    lam = np.stack([np.asarray(v) for v in (lam_q1, lam_k1, lam_q2, lam_k2)], axis=1).reshape(1, -1)
    lam = np.ascontiguousarray(np.broadcast_to(lam, (P, LAM_COLS)))
    ada = np.ascontiguousarray(np.asarray(w_ada).transpose(0, 2, 1).reshape(DEPTH * N_ADA, P, D))

    w_in, w_o, w_up, w_down = (np.asarray(w) for w in (w_in, w_o, w_up, w_down))
    stream = np.zeros((N_UNITS, P, UNIT), f)
    aq, ak, av, bq, bk, bv = 0, 512, 640, 768, 1280, 1792
    for l in range(DEPTH):
        for p in range(3):
            if p == 0:
                cols = [[(ak, 128), (av, 128), (aq, 128)], [(aq + 128, 384)]]
            else:
                o = 256 * (p - 1)
                cols = [[(bk + o, 256), (bq + o, 128)], [(bq + o + 128, 128), (bv + o, 256)]]
            for c_ in range(2):
                w = np.concatenate([w_in[l][:, a:a + n] for a, n in cols[c_]], axis=1)
                u = in_unit(l, p, c_)
                stream[u:u + IN_UNITS, :, :UNIT_K * CHUNK] = \
                    w.reshape(IN_UNITS, UNIT_K, P, CHUNK).transpose(0, 2, 1, 3).reshape(IN_UNITS, P, -1)
        stream[wo_unit(l):wo_unit(l) + KT] = tiles(w_o[l])
        up = tiles(w_up[l])
        for part, n in enumerate(PARTS):
            k0 = sum(PARTS[:part])
            u = up_unit(l, part)
            stream[u:u + 2 * n:2] = up[k0:k0 + n]
            stream[u + 1:u + 2 * n:2] = up[FF_TILES + k0:FF_TILES + k0 + n]
            d = down_unit(l, part)
            stream[d:d + KT, :, :n * P] = tiles(w_down[l][k0 * P:(k0 + n) * P])

    nc = bacc.Bacc("TRN2", target_bir_lowering=False, num_devices=1)
    arrays = dict(x_d=x_arr, cc_d=cc, small_d=sm, lam_d=lam, ada_d=ada, w_d=stream)
    aps = [nc.dram_tensor(n, a.shape, mb.dt.from_np(a.dtype), kind="ExternalInput").ap() for n, a in arrays.items()]
    out = nc.dram_tensor("out_d", _OUT_SHAPE, mb.dt.float32, kind="ExternalOutput").ap()
    spill = nc.dram_tensor("x_spill_d", _OUT_SHAPE, mb.dt.float32, kind="Internal").ap()
    backbone(nc, *aps, out, spill)
    r = run_bass_kernel_spmd(nc, [arrays], core_ids=[0])
    y = r.results[0]["out_d"]
    return y.transpose(1, 0, 2).reshape(D, SEQ).T.reshape(1, SEQ, D)
```

```python
import math
from contextlib import ExitStack

import concourse.bass as bass
from concourse import mybir

D = 1024
DEPTH = 2
SEQ, CTX = 512, 256
TOK = SEQ + CTX
GRID_W = 64
P = 128
HD = 64
KT = D // P
A_HEADS, A_KV, B_HEADS = D // 128, D // 512, D // 256
FF_TILES = ((8 * D // 3 + 127) // 128)
EPS = 1e-6
SCALE = HD ** -0.5
N_ADA = 6 * KT

CHUNK = 384
UNIT = 1024
UNIT_K = 2
IN_UNITS = KT // UNIT_K
PARTS = [8, 8, FF_TILES - 16]
LAYER_UNITS = 6 * IN_UNITS + KT + 2 * FF_TILES + len(PARTS) * KT
N_UNITS = DEPTH * LAYER_UNITS
RAW, RING = 2, 4
PROBS = 8
TURNS = 3
FIRST_ADA = 2 * KT
ADA_GROUP = 2

LAYER_STEPS = [("project", 0, 0), ("project", 0, 1), ("project", 1, 0), ("attend", 0),
               ("project", 1, 1), ("project", 2, 0), ("attend", 1), ("project", 2, 1), ("attend", 2)]
LEADS = 4

LAM_INIT = [0.8 - 0.6 * math.exp(-0.3 * l) for l in range(DEPTH)]

S_IDENT, S_ONES = 0, 128
S_COS, S_SIN = 256, 512
S_BADA = 768
S_GATTN = S_BADA + DEPTH * N_ADA
S_GFFN = S_GATTN + DEPTH * KT
S_GFIN = S_GFFN + DEPTH * KT
S_CONV = S_GFIN + KT
S_GSUB = S_CONV + DEPTH * 2 * FF_TILES * 4
S_GQ = S_GSUB + DEPTH
S_GK = S_GQ + DEPTH * HD
S_END = S_GK + DEPTH * HD
LAM_COLS = DEPTH * 4 * HD


def token_groups(l):
    return [(0, SEQ), (SEQ, TOK)] if l < DEPTH - 1 else [(0, SEQ)]


def unit0(l):
    return l * LAYER_UNITS


def in_unit(l, p, c):
    return unit0(l) + (2 * p + c) * IN_UNITS


def wo_unit(l):
    return unit0(l) + 6 * IN_UNITS


def up_unit(l, part):
    return wo_unit(l) + KT + sum(2 * n + KT for n in PARTS[:part])


def down_unit(l, part):
    return up_unit(l, part) + 2 * PARTS[part]


def unit_width(n):
    return UNIT_K * CHUNK if n % LAYER_UNITS < 6 * IN_UNITS else UNIT


def unit_runs(a, b):
    cuts = [a] + [c for l in range(DEPTH) for c in (unit0(l), wo_unit(l)) if a < c < b] + [b]
    return [(c, d) for c, d in zip(cuts, cuts[1:]) if d > c]


def evac_index(n):
    l, r = divmod(n, LAYER_UNITS)
    return l * (LAYER_UNITS - 6 * IN_UNITS) + r - 6 * IN_UNITS


def chunk_plan():
    plan = []
    for l in range(DEPTH):
        last = l == DEPTH - 1
        for p in range(3):
            for c in range(2):
                ch = dict(l=l, p=p, c=c, q=len(plan), unit=in_unit(l, p, c), tiles=[])
                for t in range(TOK // P):
                    full = not (last and t >= SEQ // P)
                    if p == 0:
                        maps = [(0, 2, "k", 8), (4, 2, "q", 0)] if c == 0 else [(0, 6, "q", 2)]
                        v = (2, 2) if c == 0 else None
                    else:
                        maps = [(0, 4, "k", 4), (4, 2, "q", 0)] if c == 0 else [(0, 2, "q", 2)]
                        v = (2, 4) if c == 1 else None
                    cols = (0, CHUNK)
                    if not full:
                        maps = [m for m in maps if m[2] == "k"]
                        if c == 0:
                            cols = (0, 256)
                        elif p == 0:
                            continue
                        else:
                            cols = (128, CHUNK)
                    ch["tiles"].append(dict(t=t, maps=maps, v=v, cols=cols))
                plan.append(ch)
    n_acc = n_tile = n_v = n_group = n_hi = 0
    for ch in plan:
        ch["prev"] = plan[ch["q"] - 1] if ch["q"] % 6 else None
        ch["after"] = {(1, 1): 0, (2, 1): 1}.get((ch["p"], ch["c"]))
        for x in ch["tiles"]:
            x["acc"] = n_acc
            n_acc += 1
            if x["maps"]:
                x["tile"] = n_tile
                n_tile += 1
                x["groups"] = []
                b = 0
                for s0, n, kind, store in x["maps"]:
                    blocks = n * (2 if kind == "k" else 1)
                    for g in range(0, blocks, 4):
                        m = min(4, blocks - g)
                        x["groups"].append((n_group, b + g, m, store + g))
                        n_group += 1
                    b += blocks
                x["his"] = n_hi + len(x["maps"])
                n_hi += len(x["maps"])
            if x["v"]:
                x["vn"] = n_v
                n_v += 1
    return plan


def attention_plan():
    phases = []
    sid = tid = item_id = 0
    buf_user = {}
    for l in range(DEPTH):
        for p in range(3):
            items = []
            for g, (t0, t1) in enumerate(token_groups(l)):
                keys = range(TOK // P) if g == 0 else range(SEQ // P, TOK // P)
                for h in range(A_HEADS if p == 0 else 2):
                    it = dict(id=item_id, l=l, p=p, g=g, h=h, t0=t0, t1=t1, qt=list(range(t0 // P, t1 // P)),
                              kt=list(keys), maps=1 if p == 0 else 2, first=not items)
                    it["k0"], it["k1"] = keys[0] * P, (keys[-1] + 1) * P
                    it["S"] = []
                    for qi, q in enumerate(it["qt"]):
                        for m in range(it["maps"]):
                            it["S"].append(dict(sid=sid, q=q, qi=qi, m=m, item=it))
                            sid += 1
                    it["T"] = [dict(tid=tid + j, j=j, kt=kt, item=it) for j, kt in enumerate(it["kt"])]
                    for x in it["T"]:
                        x["buf"] = x["tid"] % (2 if p == 1 else TURNS)
                        x["buf_before"] = buf_user.get(x["buf"])
                        buf_user[x["buf"]] = x["tid"]
                    tid += len(it["kt"])
                    item_id += 1
                    items.append(it)
            slot = 0
            users = {}
            for n, it in enumerate(items):
                it["slots"], it["freed_by"] = [], []
                for _ in it["qt"]:
                    it["slots"].append(slot)
                    it["freed_by"].append(users.get(slot))
                    users[slot] = it
                    slot = (slot + 1) % PROBS

            order = [("S", s) for s in items[0]["S"]]
            n_front = 1
            for i, it in enumerate(items):
                T = it["T"]
                back = []
                for j in range(len(T)):
                    back.append(("T", T[j]))
                    if j >= 2:
                        back.append(("V", T[j - 2]))
                back += [("V", x) for x in T[-2:]]
                upto = i + 2
                if upto < len(items) and items[upto]["g"] == 1 and it not in items[upto]["freed_by"]:
                    upto += 1
                rest = [("S", s) for x in items[n_front:upto] for s in x["S"]]
                n_front = max(n_front, min(upto, len(items)))
                per_t = -(-len(rest) // LEADS)
                for kind, x in back:
                    if kind == "T":
                        order += rest[:per_t]
                        rest = rest[per_t:]
                    order.append((kind, x))
                order += rest
            phases.append(dict(l=l, p=p, items=items, order=order))
    return phases


def backbone(nc, x_in, cc_in, small_in, lam_in, ada_in, w_in, out, x_spill):
    f32, f32r, bf16 = mybir.dt.float32, mybir.dt.float32r, mybir.dt.bfloat16
    ALU = mybir.AluOpType
    ACT = mybir.ActivationFunctionType
    AX = mybir.AxisListType

    chunks = chunk_plan()
    phases = attention_plan()

    def chunk_of(l, p, c):
        return chunks[6 * l + 2 * p + c]

    def phase_of(l, p):
        return phases[3 * l + p]

    base = -(-nc.sbuf_base // 64) * 64
    KB = 1024
    R_X = base
    R_H = R_X + 35 * KB
    R_QKV = R_H + 48 * KB
    R_O = R_QKV + 48 * KB
    R_W = R_O + 24 * KB
    R_TAB = R_W + 40 * KB
    R_SMALL = R_TAB + 4 * KB
    at = [R_SMALL]

    def place(name, shape, dt, offset):
        return nc.alloc_sbuf_tensor_at(name, shape, dt, offset=offset)

    def small(name, shape, dt=f32):
        n = 4
        for s in shape[1:]:
            n *= s
        a = place(name, shape, dt, at[0])
        at[0] += -(-n // 32) * 32
        return a

    x_sb = place("x_sb", [P, KT, TOK], f32, R_X)
    p_sb = place("p_sb", [P, PROBS, TOK], f32, R_X)
    ptmp = place("ptmp", [P, TOK], f32, R_X + 24 * KB)
    pt_at = [R_X + 27 * KB, R_X + 31 * KB, R_TAB]
    pt_hi = [place(f"pt_hi{i}", [P, SEQ], f32r, pt_at[i]) for i in range(TURNS)]
    pt_lo = [place(f"pt_lo{i}", [P, SEQ], f32r, pt_at[i] + 2 * KB) for i in range(TURNS)]
    raw = place("raw", [P, 6, CHUNK], f32, R_X)
    raw_10 = place("raw_10", [P, 6, CHUNK], f32, R_O + 12 * KB)
    raw_20 = place("raw_20", [P, 4, CHUNK], f32, R_O + 18 * KB)
    raw_20c = place("raw_20c", [P, 2, CHUNK], f32, R_TAB)
    rawsq = place("rawsq", [P, 6, CHUNK], f32, R_X + 9 * KB)
    split = place("split", [P, 2, 10, 2, HD], f32, R_X + 18 * KB)
    rope1 = place("rope1", [P, 6, HD], f32, R_X + 28 * KB)
    rope2 = place("rope2", [P, 6, HD], f32, R_X + 28 * KB + 1536)
    roped = place("roped", [P, 2, 6, HD], f32, R_X + 31 * KB)
    c_bc = place("c_bc", [P, 2, D], f32, R_X + 24 * KB)
    sqsum = place("sqsum", [P, TOK], f32, R_X + 32 * KB)
    h_hi = place("h_hi", [P, KT, TOK], f32r, R_H)
    h_lo = place("h_lo", [P, KT, TOK], f32r, R_H + 24 * KB)
    y_sb = place("y_sb", [P, KT, SEQ], f32, R_H)
    osq = place("osq", [P, 2, TOK], f32, R_H)
    dgo = place("dgo", [P, 4, P], f32, R_H + 6 * KB)
    qk = place("qk", [P, 12, TOK], f32r, R_QKV)
    v_hi = place("v_hi", [P, 6, 256], f32r, R_QKV + 36 * KB)
    v_lo = place("v_lo", [P, 6, 256], f32r, R_QKV + 42 * KB)
    oh = place("oh", [P, KT, TOK], f32r, R_QKV)
    ol = place("ol", [P, KT, TOK], f32r, R_QKV + 24 * KB)
    a_hi = place("a_hi", [P, 8, TOK], f32r, R_QKV)
    a_lo = place("a_lo", [P, 8, TOK], f32r, R_QKV + 24 * KB)
    o_sb = place("o_sb", [P, KT, TOK], f32, R_O)
    conv_g = place("conv_g", [P, TOK], f32, R_O)
    conv_v = place("conv_v", [P, TOK], f32, R_O + 3 * KB)
    sqt = place("sqt", [P, 2, TOK], f32, R_O)
    ht = place("ht", [P, 2, TOK], f32, R_O + 6 * KB)
    ada_first = place("ada_first", [P, FIRST_ADA, D], f32, R_H)
    ada_b = [place(f"ada_b{i}", [P, D], f32, R_O + (14 + 4 * i) * KB) for i in range(2)]
    ada_junk = place("ada_junk", [P, D], bf16, R_O + 12 * KB)
    dgn = place("dgn", [P, 4, P], f32, R_O + 22 * KB)
    lamv = place("lamv", [P, DEPTH, 4, HD], f32, R_O)
    w_raw = place("w_raw", [P, RAW, UNIT], f32, R_W)
    w_hi = place("w_hi", [P, RING, UNIT], f32r, R_W + 8 * KB)
    w_lo = place("w_lo", [P, RING, UNIT], f32r, R_W + 24 * KB)
    tabs = place("tabs", [P, 4, 4, HD], f32, R_TAB)
    sm = small("sm", [P, S_END])
    mod = small("mod", [P, 2, DEPTH * N_ADA])
    ada_sum = small("ada_sum", [P, 2, 4])
    gs1 = small("gs1", [P, 2, KT])
    gs2 = small("gs2", [P, 2, KT])
    eps = small("eps", [P, 1])
    zero = small("zero", [P, 1])
    act_scrap = small("act_scrap", [P, 1])
    lamw = small("lamw", [P, 4])
    nlam = small("nlam", [P, DEPTH])
    gsub = small("gsub", [P, DEPTH])
    head_ss = small("head_ss", [P, 36])
    head_sd = small("head_sd", [P, 36])
    head_r = small("head_r", [P, 36])
    nb = small("nb", [P, 8])
    rs = small("rs", [P, 8])
    ri = small("ri", [P, 8])
    rl = small("rl", [P, 8])
    n_sd = small("n_sd", [P, 24])
    n_r = small("n_r", [P, 24])
    assert at[0] <= nc.sbuf_usable_end, (at[0], nc.sbuf_usable_end)

    def raw_of(ch, t):
        if (ch["p"], ch["c"]) == (1, 0):
            return raw_10[:, t, :]
        if (ch["p"], ch["c"]) == (2, 0):
            return raw_20[:, t, :] if t < 4 else raw_20c[:, t - 4, :]
        return raw[:, t, :]

    ident = sm[:, S_IDENT:S_IDENT + P]
    ones = sm[:, S_ONES:S_ONES + P]

    ctx = ExitStack()
    with ctx:
        ps = ctx.enter_context(nc.psum_tensor("ps", [P, 8, 512], f32))

        def sem(name):
            return ctx.enter_context(nc.semaphore(name))

        small_loaded = sem("small_loaded")
        x_loaded = sem("x_loaded")
        c_loaded = sem("c_loaded")
        c_ready = sem("c_ready")
        ada_loaded = [sem("ada_loaded0"), sem("ada_loaded1")]
        first_ada_loaded = [sem(f"first_ada_loaded{i}") for i in range(FIRST_ADA // ADA_GROUP)]
        ada_used = sem("ada_used")
        w_loaded = [sem("w_loaded0"), sem("w_loaded1")]
        w_hi_done = sem("w_hi_done")
        w_lo_done = sem("w_lo_done")
        unit_done = sem("unit_done")
        acc_done = sem("acc_done")
        acc_copied = sem("acc_copied")
        raw_squared = sem("raw_squared")
        head_ss_done = sem("head_ss_done")
        head_sd_done = sem("head_sd_done")
        rope_done = sem("rope_done")
        split_hi_done = sem("split_hi_done")
        split_lo_done = sem("split_lo_done")
        v_hi_done = sem("v_hi_done")
        v_lo_done = sem("v_lo_done")
        qk_turned = sem("qk_turned")
        qk_stored = sem("qk_stored")
        scores_done = sem("scores_done")
        bias_done = sem("bias_done")
        exp_done = sem("exp_done")
        recip_done = sem("recip_done")
        scaled_done = sem("scaled_done")
        probs_done = sem("probs_done")
        turned = sem("turned")
        pt_hi_done = sem("pt_hi_done")
        pt_lo_done = sem("pt_lo_done")
        pv_done = sem("pv_done")
        o_done = sem("o_done")
        osq_done = sem("osq_done")
        o_normed = sem("o_normed")
        o_hi_done = sem("o_hi_done")
        o_lo_done = sem("o_lo_done")
        sq_done = sem("sq_done")
        sqsum_done = sem("sqsum_done")
        ss_done = sem("ss_done")
        sd_done = sem("sd_done")
        diag_done = sem("diag_done")
        spread_done = sem("spread_done")
        ht_done = sem("ht_done")
        h_hi_done = sem("h_hi_done")
        h_lo_done = sem("h_lo_done")
        bank_read = sem("bank_read")
        conv_started = sem("conv_started")
        silu_done = sem("silu_done")
        prod_done = sem("prod_done")
        a_hi_done = sem("a_hi_done")
        a_lo_done = sem("a_lo_done")
        lam_sum = sem("lam_sum")
        lam_exp = sem("lam_exp")
        x_spilled = sem("x_spilled")
        y_done = sem("y_done")
        stored = sem("stored")
        dve_step = sem("dve_step")
        act_step = sem("act_step")

        class Steps:

            def __init__(self, eng, s):
                self.eng, self.s, self.n, self.i, self.per, self.k = eng, s, 0, 0, 0, 0

            def mark(self, ins):
                self.k += 1
                ins.then_inc(self.s, 1)

            def wait(self):
                self.eng.wait_ge(self.s, self.i * self.per + (self.n + self.k))

            def __call__(self, ins):
                self.mark(ins)
                self.wait()

            def loop(self, n, per, body):
                self.n, self.k = self.n + self.k, 0
                self.per = per
                with self.eng.Fori(0, n) as i:
                    self.i = i
                    body(i)
                    assert self.k == per, (self.k, per)
                self.n, self.i, self.k, self.per = self.n + n * per, 0, 0, 0

        def wait_unit(e, c, i=0):
            l, r = divmod(c, LAYER_UNITS)
            done_in = l * 6 + min(r, 6 * IN_UNITS) // IN_UNITS
            if r < 6 * IN_UNITS and r % IN_UNITS == IN_UNITS - 1:
                e.wait_ge(acc_done, chunks[l * 6 + r // IN_UNITS]["tiles"][-1]["acc"] + 1)
            else:
                e.wait_ge(unit_done, 4 * i + (c + 1 - done_in))

        norms = []
        for l in range(DEPTH):
            norms += [[(0, SEQ), (SEQ, TOK)], token_groups(l)]
        norms.append([(0, SEQ)])

        def n_tiles(groups):
            return sum((b - a) // P for a, b in groups)

        def norm_counts(j):
            tiles = sum(n_tiles(g) for g in norms[:j])
            hs = sum(len(g) * KT for g in norms[:j])
            return tiles, hs

        stat_order = [("norm", 0)]
        for l in range(DEPTH):
            stat_order += [("sub", l), ("norm", 2 * l + 1), ("norm", 2 * l + 2)]

        def stat_tiles(s):
            kind, j = s
            return 4 * n_tiles(token_groups(j)) if kind == "sub" else n_tiles(norms[j])

        def stat_index(s):
            return stat_order.index(s)

        def stat_base(s):
            return sum(stat_tiles(r) for r in stat_order[:stat_index(s)])

        sub_oh = [sum(KT * len(token_groups(k)) for k in range(l)) for l in range(DEPTH)]
        sub_sq = [sum(4 for k in range(l)) for l in range(DEPTH)]

        block = ctx.enter_context(nc.Block())

        @block.sync
        def _(sp):
            def load_unit(c, i=0, first=False):
                if not first:
                    sp.wait_ge(w_lo_done, 4 * i + (c - RAW + 1))
                n = unit_width(c)
                sp.dma_start(w_raw[:, c % RAW, 0:n], w_in[4 * i + c, :, 0:n]).then_inc(w_loaded[c % RAW], 16)

            def load_ada(c, i=0, first=False):
                if not first:
                    sp.wait_ge(ada_used, 4 * i + (c - 1))
                sp.dma_start(ada_b[c % 2][:, :], ada_in[4 * i + c, :, :]).then_inc(ada_loaded[c % 2], 16)

            def load_c():
                sp.dma_start(c_bc[:, :, :].rearrange("p a k -> p (a k)"),
                             cc_in.partition_broadcast(P)).then_inc(c_loaded, 16)

            def units(a, b):
                for c, d in unit_runs(a, b):
                    with sp.Fori(0, (d - c) // RING) as i:
                        for j in range(RING):
                            load_unit(c + j, i)

            load_c()
            sp.dma_start(sm[:, :], small_in).then_inc(small_loaded, 16)
            sp.dma_start(lamv[:, :, :, :].rearrange("p l a k -> p (l a k)"), lam_in).then_inc(small_loaded, 16)
            for g in range(FIRST_ADA // ADA_GROUP):
                a = slice(g * ADA_GROUP, (g + 1) * ADA_GROUP)
                sp.dma_start(ada_first[:, a, :], ada_in[a, :, :].rearrange("a p k -> p a k")) \
                    .then_inc(first_ada_loaded[g], 16)
            sp.dma_start(x_sb[:, :, :], x_in).then_inc(x_loaded, 16)
            for n in range(RING):
                load_unit(n, first=n < RAW)
            a = FIRST_ADA
            for j in range(2):
                load_ada(a + j, first=True)
            for j in range(RING):
                load_unit(RING + j)
                if j:
                    load_ada(a + 2 * j)
                    load_ada(a + 2 * j + 1)
            units(2 * RING, wo_unit(0) + RING)
            sp.wait_ge(o_lo_done, sub_oh[1])
            load_c()
            a = 3 * KT
            for j in range(2):
                load_ada(a + j)
            for d in range(KT):
                load_unit(wo_unit(0) + RING + d)
                load_ada(a + 2 + 2 * d)
                load_ada(a + 3 + 2 * d)
            a = 5 * KT + 2
            for part, n in enumerate(PARTS):
                u = up_unit(0, part) + RING
                with sp.Fori(0, n // 2) as i:
                    for j in (0, 2):
                        for unit in (u + j, u + j + 1):
                            load_unit(unit, i)
                        for tile in (a + j, a + j + 1):
                            load_ada(tile, i)
                a += 2 * n
                u = down_unit(0, part) + RING
                if part == 1:
                    units(u, u + KT)
                else:
                    for j in range(KT):
                        load_unit(u + j)
                        if part == 0 or j in (1, 3):
                            load_ada(a)
                            a += 1
            assert a == DEPTH * N_ADA
            units(down_unit(0, len(PARTS) - 1) + KT + RING, N_UNITS)

        @block.gpsimd
        def _(pool):
            def split_unit(c, i=0):
                pool.wait_ge(w_hi_done, 4 * i + (c + 1))
                n = unit_width(c)
                nc.gpsimd.tensor_tensor(w_lo[:, c % RING, 0:n], w_raw[:, c % RAW, 0:n],
                                        w_hi[:, c % RING, 0:n].bitcast(f32), ALU.subtract).then_inc(w_lo_done, 1)

            def units(a, b):
                for c, d in unit_runs(a, b):
                    with pool.Fori(0, (d - c) // RING) as i:
                        for j in range(RING):
                            split_unit(c + j, i)

            for n in range(RING):
                split_unit(n)
            done = RING
            for l in range(DEPTH):
                for at_step, (what, p, *c) in enumerate(LAYER_STEPS):
                    if what == "project":
                        if LAYER_STEPS[at_step + 1][0] == "attend":
                            upto = in_unit(l, p, c[0]) + IN_UNITS + RING
                            units(done, upto)
                            done = upto
                        continue
                    for kind, s in phase_of(l, p)["order"]:
                        if kind != "S" or s["m"]:
                            continue
                        it, sid = s["item"], s["sid"]
                        k = it["k1"] - it["k0"]
                        pool.wait_ge(recip_done, sid + 1)
                        buf = p_sb[:, it["slots"][s["qi"]], 0:k]
                        nc.gpsimd.tensor_tensor(buf, buf, ri[:, sid % 8:sid % 8 + 1].broadcast_to([P, k]),
                                                ALU.mult).then_inc(scaled_done, 1)
                upto = min(up_unit(l, 0) + RING, N_UNITS)
                units(done, upto)
                end = min(unit0(l + 1) + RING, N_UNITS)
                units(upto, end)
                done = end

        scaled_no = {}
        for ph in phases:
            for kind, s in ph["order"]:
                if kind == "S" and s["m"] == 0:
                    scaled_no[s["sid"]] = len(scaled_no) + 1
        comb_no = {}
        for ph in phases:
            for kind, s in ph["order"]:
                if kind == "S" and s["m"] == 1:
                    comb_no[s["sid"]] = len(comb_no) + 1

        def wait_probs(e, it):
            if it["maps"] == 1:
                e.wait_ge(scaled_done, scaled_no[it["S"][-1]["sid"]])
            else:
                e.wait_ge(probs_done, comb_no[it["S"][-1]["sid"]])

        @block.tensor
        def _(pe):
            def spread_stats(s, cols, pieces):
                for k, (bank, col) in enumerate(pieces):
                    g = stat_base(s) + cols + k
                    dg = dgo if s[0] == "sub" else dgn
                    pe.wait_ge(diag_done, g + 1)
                    nc.tensor.matmul(ps[:, bank, col:col + P], ones, dg[:, (cols + k) % 4, :],
                                     start=True, stop=True).then_inc(spread_done, 1)

            def norm_stats(j):
                groups = norms[j]
                pe.wait_ge(sqsum_done, KT * (j + 1))
                for t in range(n_tiles(groups)):
                    mm = nc.tensor.matmul(ps[:, 5, t:t + 1], sqsum[:, t * P:(t + 1) * P], ones[:, 0:1],
                                          start=True, stop=True)
                mm.then_inc(ss_done, 1)
                spread_stats(("norm", j), 0, [(6 + t // 4, (t % 4) * P) for t in range(n_tiles(groups))])

            def three(out, lhs, rhs, first, last):
                (lh, ll), (rh, rl_) = lhs, rhs
                nc.tensor.matmul(out, lh, rh, start=first, stop=False)
                nc.tensor.matmul(out, lh, rl_, start=False, stop=False)
                return nc.tensor.matmul(out, ll, rh, start=False, stop=last)

            def turn_tile(x, last_item=None):
                if "tile" not in x:
                    return
                pe.wait_ge(split_lo_done, x["his"])
                for g, b, m, store in x["groups"]:
                    if g >= 2:
                        pe.wait_ge(qk_stored, g - 1)
                    if last_item is not None:
                        pe.wait_ge(pt_lo_done, last_item["T"][-1]["tid"] + 1)
                        pe.wait_ge(o_done, last_item["id"] + 1)
                        last_item = None
                    for k in range(m):
                        mm = nc.tensor.transpose(ps[:, 6 + g % 2, k * P:(k + 1) * P],
                                                 split[:, x["tile"] % 2, b + k, :, :].rearrange("p a d -> p (a d)"),
                                                 ident)
                    mm.then_inc(qk_turned, 1)

            def project(l, p, c):
                ch = chunk_of(l, p, c)
                prev = ch["prev"]
                last_item = None if ch["after"] is None else phase_of(l, ch["after"])["items"][-1]
                for u in range(IN_UNITS):
                    n = ch["unit"] + u
                    pe.wait_ge(w_lo_done, n + 1)
                    if p == 0 and c == 0:
                        _, hs = norm_counts(2 * l)
                        pe.wait_ge(h_lo_done, hs + 2 * (UNIT_K * u + UNIT_K))
                    for x in ch["tiles"]:
                        t = x["t"]
                        if u == 0:
                            if last_item is not None:
                                if t == 0:
                                    pe.wait_ge(exp_done, last_item["S"][-1]["sid"] + 1)
                                elif t == 4:
                                    pe.wait_ge(pt_lo_done, last_item["T"][-1]["tid"] + 1)
                            elif prev:
                                pe.wait_ge(acc_copied, [y["acc"] for y in prev["tiles"] if y["t"] <= t][-1] + 1)
                        c0, c1 = x["cols"]
                        for kk in range(UNIT_K):
                            k = UNIT_K * u + kk
                            tok = slice(t * P, (t + 1) * P)
                            col = slice(kk * CHUNK + c0, kk * CHUNK + c1)
                            mm = three(ps[:, t, c0:c1], (h_hi[:, k, tok], h_lo[:, k, tok]),
                                       (w_hi[:, n % RING, col], w_lo[:, n % RING, col]), k == 0, k == KT - 1)
                        if u == IN_UNITS - 1:
                            mm.then_inc(acc_done, 1)
                    if u < IN_UNITS - 1:
                        mm.then_inc(unit_done, 1)
                    if prev and u > 0:
                        for x in prev["tiles"][2 * u - 2:2 * u]:
                            turn_tile(x, last_item if x["t"] == 0 else None)
                if (p, c) == (2, 1):
                    for x in ch["tiles"]:
                        turn_tile(x)

            def attend(l, p):
                ph = phase_of(l, p)
                a, b = chunk_of(l, p, 0), chunk_of(l, p, 1)
                stored_all = [x["groups"][-1][0] + 1 for ch in (a, b) for x in ch["tiles"] if "tile" in x][-1]
                v_all = [x["vn"] + 1 for ch in (a, b) for x in ch["tiles"] if x["v"]][-1]
                pe.wait_ge(qk_stored, stored_all)
                pe.wait_ge(v_lo_done, v_all)
                left = b if p == 2 else chunk_of(l, p + 1, 0)
                pe.wait_ge(acc_copied, left["tiles"][-1]["acc"] + 1)
                for kind, s in ph["order"]:
                    it = s["item"]
                    if kind == "S":
                        sid, m = s["sid"], s["m"]
                        if p == 0:
                            qs, ks = it["h"], 8 + 2 * (it["h"] // (A_HEADS // A_KV))
                        else:
                            qs, ks = 2 * it["h"] + m, 4 + 2 * (2 * it["h"] + m)
                        if sid >= 2:
                            pe.wait_ge(exp_done, sid - 1)
                        lhs = qk[:, qs, s["q"] * P:(s["q"] + 1) * P]
                        k0 = it["k0"]
                        while k0 < it["k1"]:
                            k1 = min(k0 + 512, it["k1"])
                            at0 = k0 - it["k0"]
                            dst = ps[:, 2 * (sid % 2) + at0 // 512, 0:k1 - k0]
                            nc.tensor.matmul(dst, lhs, qk[:, ks, k0:k1], start=True, stop=False)
                            mm = nc.tensor.matmul(dst, lhs, qk[:, ks + 1, k0:k1], start=False, stop=True)
                            k0 = k1
                        mm.then_inc(scores_done, 1)
                    elif kind == "T":
                        tid, j = s["tid"], s["j"]
                        if j == 0:
                            wait_probs(pe, it)
                        if tid >= TURNS:
                            pe.wait_ge(pt_lo_done, tid - TURNS + 1)
                        for qi in range(len(it["qt"])):
                            mm = nc.tensor.transpose(ps[:, 4 + tid % TURNS, qi * P:(qi + 1) * P],
                                                     p_sb[:, it["slots"][qi], j * P:(j + 1) * P], ident)
                        mm.then_inc(turned, 1)
                    else:
                        tid, j = s["tid"], s["j"]
                        nq = it["t1"] - it["t0"]
                        if j == 0 and it["id"] >= 1:
                            pe.wait_ge(o_done, it["id"])
                        pe.wait_ge(pt_lo_done, tid + 1)
                        vc = slice(P * (it["h"] // (A_HEADS // A_KV)), P * (it["h"] // (A_HEADS // A_KV)) + P) \
                            if p == 0 else slice(P * it["h"], P * it["h"] + P)
                        mm = three(ps[:, 7, 0:nq], (v_hi[:, s["kt"], vc], v_lo[:, s["kt"], vc]),
                                   (pt_hi[s["buf"]][:, 0:nq], pt_lo[s["buf"]][:, 0:nq]), j == 0, j == len(it["T"]) - 1)
                        mm.then_inc(pv_done, 1)

            def sub_stats(l):
                nt = n_tiles(token_groups(l))
                for b in range(B_HEADS):
                    pe.wait_ge(osq_done, sub_sq[l] + b + 1)
                    for t in range(nt):
                        mm = nc.tensor.matmul(ps[:, 5, b * nt + t:b * nt + t + 1], osq[:, b % 2, t * P:(t + 1) * P],
                                              ones[:, 0:1], start=True, stop=True)
                    mm.then_inc(ss_done, 1)
                for b in range(B_HEADS):
                    if b >= 1:
                        pe.wait_ge(o_normed, sub_sq[l] + b)
                    spread_stats(("sub", l), b * nt, [(6 + t // 4, (t % 4) * P) for t in range(nt)])

            def feature_unit(c, i, groups, kn, moving, wait_bank):
                pe.wait_ge(w_lo_done, 4 * i + (c + 1))
                if wait_bank:
                    pe.wait_ge(bank_read, 4 * i + (evac_index(c) - 3))
                mh, ml = moving
                for g, (t0, t1) in enumerate(groups):
                    for k in range(kn):
                        col = slice(k * P, (k + 1) * P)
                        mm = three(ps[:, 2 * (c % 4) + g, 0:t1 - t0], (w_hi[:, c % RING, col], w_lo[:, c % RING, col]),
                                   (mh[:, k, t0:t1], ml[:, k, t0:t1]), k == 0, k == kn - 1)
                mm.then_inc(unit_done, 1)

            pe.wait_ge(small_loaded, 32)
            for l in range(DEPTH):
                groups = token_groups(l)
                if l == 0:
                    norm_stats(0)
                for what, *args in LAYER_STEPS:
                    (project if what == "project" else attend)(l, *args)
                sub_stats(l)
                pe.wait_ge(o_lo_done, sub_oh[l] + KT * len(groups))
                first = wo_unit(l)
                for j in range(RING):
                    feature_unit(first + j, 0, groups, KT, (oh, ol), False)
                for j in range(RING):
                    feature_unit(first + RING + j, 0, groups, KT, (oh, ol), True)
                norm_stats(2 * l + 1)
                _, hs = norm_counts(2 * l + 1)
                for part, n in enumerate(PARTS):
                    if part == 0:
                        pe.wait_ge(h_lo_done, hs + KT * len(groups))
                    with pe.Fori(0, n // 2) as i:
                        for j in range(RING):
                            feature_unit(up_unit(l, part) + j, i, groups, KT, (h_hi, h_lo), True)
                    pe.wait_ge(a_lo_done, 1 + l * FF_TILES + sum(PARTS[:part + 1]))
                    with pe.Fori(0, KT // RING) as i:
                        for j in range(RING):
                            feature_unit(down_unit(l, part) + j, i, groups, n, (a_hi, a_lo), True)
                norm_stats(2 * l + 2)

        @block.scalar
        def _(act):
            A = nc.scalar.activation
            step = Steps(act, act_step)

            def unit_hi(c, i=0):
                half = (c - c % RING) // 2
                if c >= RING:
                    wait_unit(act, c - RING, i)
                act.wait_ge(w_loaded[c % RAW], 32 * i + 16 * (c // RAW + 1))
                n = unit_width(c)
                A(w_hi[:, c % RING, 0:n], w_raw[:, c % RAW, 0:n], ACT.Copy).then_inc(w_hi_done, 1)

            def stats_sd(s, cols, width, n):
                ss_no = {("norm", 0): 1}
                k = 1
                for r in stat_order[1:]:
                    k += B_HEADS if r[0] == "sub" else 1
                    ss_no[r] = k
                act.wait_ge(ss_done, ss_no[s])
                A(n_sd[:, 0:cols], ps[:, 5, 0:cols], ACT.Sqrt, bias=eps[:, :], scale=1.0 / width).then_inc(sd_done, 1)

            def norm_hi(j):
                groups = norms[j]
                _, hs = norm_counts(j)
                l = j // 2
                sh = 0 if j % 2 == 0 else 3 * KT
                stats_sd(("norm", j), n_tiles(groups), D, j)
                if j == len(norms) - 1:
                    return
                for k in range(KT):
                    for g, (t0, t1) in enumerate(groups):
                        n = hs + k * len(groups) + g
                        act.wait_ge(ht_done, n + 1)
                        A(h_hi[:, k, t0:t1], ht[:, k % 2, t0:t1], ACT.Identity,
                          bias=mod[:, g, l * N_ADA + sh + k:l * N_ADA + sh + k + 1]).then_inc(h_hi_done, 1)

            def square_x(d, j, groups, i=0):
                T = groups[-1][1]
                n = KT * j + d
                if not (isinstance(i, int) and n < 2):
                    act.wait_ge(sqsum_done, 4 * i + (n - 1))
                A(sqt[:, d % 2, 0:T], x_sb[:, 4 * i + d, 0:T], ACT.Square).then_inc(sq_done, 1)

            def tile_hi(ch, x):
                if x["v"]:
                    s0, n = x["v"]
                    act.wait_ge(acc_copied, x["acc"] + 1)
                    if n == 2:
                        src = raw_of(ch, x["t"])[:, s0 * HD:(s0 + 2) * HD].rearrange("p (k d) -> p k d", k=2) \
                            .unsqueeze(2).broadcast_to([P, 2, 2, HD])
                        dst = v_hi[:, x["t"], :].rearrange("p (k a d) -> p k a d", k=2, a=2)
                    else:
                        src = raw_of(ch, x["t"])[:, s0 * HD:(s0 + n) * HD]
                        dst = v_hi[:, x["t"], :]
                    A(dst, src, ACT.Copy).then_inc(v_hi_done, 1)
                if "tile" not in x:
                    return
                b = 0
                i = x["tile"] % 2
                act.wait_ge(rope_done, x["tile"] + 1)
                if x["tile"] >= 2:
                    act.wait_ge(qk_turned, x["prev2"])
                for s0, n, kind, _ in x["maps"]:
                    u = roped[:, i, s0:s0 + n, :]
                    if kind == "q":
                        ins = A(split[:, i, b:b + n, 0, :].bitcast(f32r), u, ACT.Copy, scale=SCALE)
                        b += n
                    else:
                        dst = split[:, i, b:b + 2 * n:2, :, :].bitcast(f32r)
                        ins = A(dst, u.unsqueeze(2).broadcast_to([P, n, 2, HD]), ACT.Copy)
                        b += 2 * n
                    ins.then_inc(split_hi_done, 1)

            def tile_store(x):
                for g, b, m, store in x.get("groups", []):
                    act.wait_ge(qk_turned, g + 1)
                    A(qk[:, store:store + m, x["t"] * P:(x["t"] + 1) * P],
                      ps[:, 6 + g % 2, 0:m * P].rearrange("p (m t) -> p m t", m=m), ACT.Copy).then_inc(qk_stored, 1)

            tiles = [x for ch in chunks for x in ch["tiles"] if "tile" in x]
            for n, x in enumerate(tiles):
                if n >= 2:
                    x["prev2"] = tiles[n - 2]["groups"][-1][0] + 1

            def chunk_copies(ch):
                q, l, p, c = ch["q"], ch["l"], ch["p"], ch["c"]
                for x in ch["tiles"]:
                    act.wait_ge(acc_done, x["acc"] + 1)
                    if (p, c) == (0, 1):
                        y = ch["prev"]["tiles"][x["t"]]
                        if "tile" in y:
                            act.wait_ge(rope_done, y["tile"] + 1)
                        if y["v"]:
                            act.wait_ge(v_lo_done, y["vn"] + 1)
                    c0, c1 = x["cols"]
                    A(raw_of(ch, x["t"])[:, c0:c1], ps[:, x["t"], c0:c1], ACT.Copy).then_inc(acc_copied, 1)
                if p == 0:
                    full = [x for x in ch["tiles"] if x["cols"][1] == CHUNK]
                    act.wait_ge(acc_copied, ch["tiles"][-1]["acc"] + 1)
                    n = len(full)
                    ins = A(rawsq[:, 0:n, :], raw[:, 0:n, :], ACT.Square)
                    if n < len(ch["tiles"]):
                        ins = A(rawsq[:, n:, 0:256], raw[:, n:6, 0:256], ACT.Square)
                    ins.then_inc(raw_squared, 1)

            def head_sd_step(ch):
                if ch["p"] == 0:
                    k = 2 * ch["l"] + ch["c"]
                    act.wait_ge(head_ss_done, k + 1)
                    n = 36 if len(ch["tiles"]) == 6 else 24
                    A(head_sd[:, 0:n], head_ss[:, 0:n], ACT.Sqrt, bias=eps[:, :], scale=1.0 / HD) \
                        .then_inc(head_sd_done, 1)

            def project(l, p, c):
                ch = chunk_of(l, p, c)
                prev = ch["prev"]
                for u in range(IN_UNITS):
                    n = ch["unit"] + u
                    if prev and u == 0:
                        head_sd_step(prev)
                    xs = prev["tiles"][2 * u - 2:2 * u] if prev and u > 0 else []
                    if u == IN_UNITS - 1:
                        for x in xs:
                            tile_hi(prev, x)
                            tile_store(x)
                        chunk_copies(ch)
                        unit_hi(n + RING)
                    else:
                        for x in xs:
                            tile_hi(prev, x)
                        unit_hi(n + RING)
                        for x in xs:
                            tile_store(x)
                if (p, c) == (2, 1):
                    for x in ch["tiles"]:
                        tile_hi(ch, x)
                        tile_store(x)

            def attend(l, p):
                waiting = []

                def exponentials(s):
                    it, sid, m = s["item"], s["sid"], s["m"]
                    k = it["k1"] - it["k0"]
                    act.wait_ge(bias_done, sid + 1)
                    if m == 0:
                        dst = p_sb[:, it["slots"][s["qi"]], 0:k]
                        before = it["freed_by"][s["qi"]]
                        if before:
                            act.wait_ge(turned, before["T"][-1]["tid"] + 1)
                    else:
                        dst = ptmp[:, 0:k]
                        if comb_no[sid] > 1:
                            act.wait_ge(probs_done, comb_no[sid] - 1)
                    src = ps[:, 2 * (sid % 2):2 * (sid % 2) + 2, :].rearrange("p a b -> p (a b)")[:, 0:k]
                    A(dst, src, ACT.Exp, bias=nb[:, sid % 8:sid % 8 + 1],
                      accum_out=rs[:, sid % 8:sid % 8 + 1]).then_inc(exp_done, 1)

                for kind, s in phase_of(l, p)["order"]:
                    it = s["item"]
                    if kind == "S":
                        while waiting:
                            exponentials(waiting.pop(0))
                        waiting.append(s)
                    elif kind == "T":
                        if s["j"] == 0:
                            while waiting and waiting[0]["item"] is it:
                                exponentials(waiting.pop(0))
                        tid = s["tid"]
                        nq = it["t1"] - it["t0"]
                        act.wait_ge(turned, tid + 1)
                        if s["buf_before"] is not None:
                            act.wait_ge(pv_done, s["buf_before"] + 1)
                        A(pt_hi[s["buf"]][:, 0:nq], ps[:, 4 + tid % TURNS, 0:nq], ACT.Copy).then_inc(pt_hi_done, 1)
                        while waiting:
                            exponentials(waiting.pop(0))
                    elif s["j"] == len(it["T"]) - 1:
                        while waiting:
                            exponentials(waiting.pop(0))
                        act.wait_ge(pv_done, s["tid"] + 1)
                        nq = it["t1"] - it["t0"]
                        if p == 0:
                            r = slice(HD * (it["h"] % 2), HD * (it["h"] % 2) + HD)
                            A(o_sb[r, it["h"] // 2, it["t0"]:it["t1"]], ps[r, 7, 0:nq], ACT.Copy).then_inc(o_done, 1)
                        else:
                            A(o_sb[:, 4 + 2 * (p - 1) + it["h"], it["t0"]:it["t1"]], ps[:, 7, 0:nq], ACT.Copy) \
                                .then_inc(o_done, 1)

            act.wait_ge(c_loaded, 16)
            A(c_bc[:, :, :], c_bc[:, :, :], ACT.Silu).then_inc(c_ready, 1)
            for n in range(RING):
                unit_hi(n)
            act.wait_ge(lam_sum, 1)
            A(lamw[:, :], lamw[:, :], ACT.Exp).then_inc(lam_exp, 1)
            act.wait_ge(x_loaded, 16)
            for d in range(KT):
                square_x(d, 0, norms[0])
            norm_hi(0)
            for l in range(DEPTH):
                groups = token_groups(l)
                T = groups[-1][1]
                for what, *args in LAYER_STEPS:
                    (project if what == "project" else attend)(l, *args)
                last_item = phase_of(l, 2)["items"][-1]
                act.wait_ge(pv_done, last_item["T"][-1]["tid"] + 1)
                if l == 0:
                    act.dma_start(x_sb[:, :, :], x_in).then_inc(x_loaded, 16)
                else:
                    act.wait_ge(x_spilled, 16)
                    act.dma_start(x_sb[:, :, 0:SEQ], x_spill).then_inc(x_loaded, 16)
                act.wait_ge(o_done, last_item["id"] + 1)
                for b in range(B_HEADS):
                    if b >= 2:
                        act.wait_ge(ss_done, 1 + (B_HEADS + 2) * l + b - 1)
                    A(osq[:, b % 2, 0:T], o_sb[:, 4 + b, 0:T], ACT.Square).then_inc(osq_done, 1)
                stats_sd(("sub", l), B_HEADS * n_tiles(groups), B_HEADS * 32, l)
                for k in range(KT):
                    if k >= 4:
                        act.wait_ge(o_normed, sub_sq[l] + k - 3)
                    for g, (t0, t1) in enumerate(groups):
                        A(oh[:, k, t0:t1], o_sb[:, k, t0:t1], ACT.Copy).then_inc(o_hi_done, 1)
                if l == 0:
                    act.wait_ge(c_loaded, 32)
                    A(c_bc[:, :, :], c_bc[:, :, :], ACT.Silu).then_inc(c_ready, 1)
                for d in range(KT):
                    act.wait_ge(bank_read, evac_index(wo_unit(l) + d) + 1)
                    unit_hi(wo_unit(l) + d + RING)
                    square_x(d, 2 * l + 1, groups)
                norm_hi(2 * l + 1)
                for part, n in enumerate(PARTS):
                    pair0 = l * FF_TILES + sum(PARTS[:part])

                    A(act_scrap[:, :], sm[:, 0:1], ACT.Silu)

                    def pairs(i, part=part, pair0=pair0, groups=groups, T=T, l=l):
                        for half in range(2):
                            for gv, buf in enumerate((conv_g, conv_v)):
                                c = up_unit(l, part) + 2 * half + gv
                                wcol = S_CONV + (l * 2 * FF_TILES + gv * FF_TILES + sum(PARTS[:part]) + half) * 4
                                wait_unit(act, c, i)
                                act.wait_ge(a_lo_done, 2 * i + (pair0 + half + 1))
                                for g, (t0, t1) in enumerate(groups):
                                    ins = A(buf[:, t0:t1], ps[:, 2 * (c % 4) + g, 0:t1 - t0], ACT.Identity,
                                            bias=sm[:, bass.ds(8 * i + (wcol + 3), 1)],
                                            scale=sm[:, bass.ds(8 * i + (wcol + 1), 1)])
                                ins.then_inc(conv_started, 1)
                                unit_hi(c + RING, i)
                            act.wait_ge(bank_read, 4 * i + (evac_index(up_unit(l, part) + 2 * half) + 1))
                            A(conv_g[:, 0:T], conv_g[:, 0:T], ACT.Silu).then_inc(silu_done, 1)
                            act.wait_ge(prod_done, 2 * i + (pair0 + half + 1))
                            A(a_hi[:, 2 * i + half, 0:T], conv_g[:, 0:T], ACT.Copy).then_inc(a_hi_done, 1)

                    step.loop(n // 2, 0, pairs)
                    last_part = part == len(PARTS) - 1
                    for d in range(KT):
                        c = down_unit(l, part) + d
                        if c + RING < N_UNITS:
                            unit_hi(c + RING)
                        if last_part:
                            act.wait_ge(bank_read, evac_index(c) + 1)
                            square_x(d, 2 * l + 2, norms[2 * l + 2])
                if l == 0:
                    act.wait_ge(bank_read, evac_index(down_unit(0, len(PARTS) - 1) + KT - 1) + 1)
                    act.dma_start(x_spill, x_sb[:, :, 0:SEQ]).then_inc(x_spilled, 16)
                norm_hi(2 * l + 2)
                if l == 0:
                    act.wait_ge(x_spilled, 16)
            for k in range(KT):
                act.wait_ge(y_done, k + 1)
                act.dma_start(out[:, k, :], y_sb[:, k, :]).then_inc(stored, 16)
            act.wait_ge(stored, 16 * KT)

        @block.vector
        def _(dve):
            V = nc.vector
            step = Steps(dve, dve_step)

            def ada_tile(c, streams, i, dst):
                if isinstance(i, int) and c < FIRST_ADA:
                    dve.wait_ge(first_ada_loaded[c // ADA_GROUP], 16)
                    w = ada_first[:, c, :]
                else:
                    dve.wait_ge(ada_loaded[c % 2], 32 * i + 16 * ((c - FIRST_ADA) // 2 + 1))
                    w = ada_b[c % 2][:, :]
                if not isinstance(i, int) or c > 0:
                    dve.wait_ge(ada_used, 4 * i + c)
                for s in range(streams):
                    ins = V.tensor_tensor_reduce(ada_junk[:, :], w, c_bc[:, s, :], 1.0, 0.0, ALU.mult, ALU.add,
                                                 dst(s))
                    if s == streams - 1:
                        ins.then_inc(ada_used, 1)
                    else:
                        step(ins)

            def ada_straight(a, b, streams=2):
                for c in range(a, b):
                    ada_tile(c, streams, 0, lambda s: mod[:, s, c:c + 1])

            def add_bias(a, b, streams=2):
                dve.wait_ge(ada_used, b)
                for s in range(streams):
                    step(V.tensor_tensor(mod[:, s, a:b], mod[:, s, a:b], sm[:, S_BADA + a:S_BADA + b], ALU.add))

            def norm_gains(gs, scale_at, gain, streams=2):
                for s in range(streams):
                    step(V.scalar_tensor_tensor(gs[:, s, :], mod[:, s, scale_at:scale_at + KT], 1.0,
                                                sm[:, gain:gain + KT], ALU.add, ALU.mult))

            cos = sm[:, S_COS:S_COS + 4 * HD].rearrange("p (t d) -> p t d", t=4)
            sin = sm[:, S_SIN:S_SIN + 4 * HD].rearrange("p (t d) -> p t d", t=4)

            def rope_tables(l):
                for n, col in enumerate((S_GQ, S_GK)):
                    g = sm[:, col + l * HD:col + (l + 1) * HD]
                    step(V.tensor_tensor(tabs[:, 2 * n, :, :], cos, g.unsqueeze(1).broadcast_to([P, 4, HD]), ALU.mult))
                    gv = g.rearrange("p (a b d) -> p a b d", a=2, b=2)
                    for t in range(4):
                        sv = sm[:, S_SIN + t * HD:S_SIN + (t + 1) * HD].rearrange("p (a b d) -> p a b d", a=2, b=2)
                        ov = tabs[:, 2 * n + 1, t, :].rearrange("p (a b d) -> p a b d", a=2, b=2)
                        for b in range(2):
                            step(V.tensor_tensor(ov[:, :, b, :], sv[:, :, b, :], gv[:, :, 1 - b, :], ALU.mult))

            def stats_scales(s, cols, banks_of):
                no = stat_index(s) + 1
                dve.wait_ge(sd_done, no)
                step(V.reciprocal(n_r[:, 0:cols], n_sd[:, 0:cols]))

            def diag(s, k):
                g = stat_base(s) + k
                dg = dgo if s[0] == "sub" else dgn
                if k >= 4:
                    dve.wait_ge(spread_done, g - 3)
                V.tensor_scalar(dg[:, k % 4, :], ident, n_r[:, k:k + 1], None, ALU.mult).then_inc(diag_done, 1)

            def add_squares(d, j, groups, i=0):
                T = groups[-1][1]
                dve.wait_ge(sq_done, 4 * i + (KT * j + d + 1))
                if not (isinstance(i, int) and d == 0):
                    dve.wait_ge(sqsum_done, KT * j + d)
                    V.tensor_tensor(sqsum[:, 0:T], sqsum[:, 0:T], sqt[:, d % 2, 0:T], ALU.add).then_inc(sqsum_done, 1)
                else:
                    V.tensor_copy(sqsum[:, 0:T], sqt[:, d % 2, 0:T]).then_inc(sqsum_done, 1)

            def norm(j):
                groups = norms[j]
                s = ("norm", j)
                nt = n_tiles(groups)
                _, hs = norm_counts(j)
                l = j // 2
                gs = gs1 if j % 2 == 0 else gs2
                sh = 0 if j % 2 == 0 else 3 * KT
                final = j == len(norms) - 1
                stats_scales(s, nt, None)
                for t in range(nt):
                    diag(s, t)

                def lo(k, g):
                    t0, t1 = groups[g]
                    dve.wait_ge(h_hi_done, hs + k * len(groups) + g + 1)
                    V.scalar_tensor_tensor(h_lo[:, k, t0:t1], ht[:, k % 2, t0:t1], mod[:, g, l * N_ADA + sh + k:l * N_ADA + sh + k + 1],
                                           h_hi[:, k, t0:t1].bitcast(f32), ALU.add, ALU.subtract).then_inc(h_lo_done, 1)

                dve.wait_ge(spread_done, stat_base(s) + nt)
                for k in range(KT):
                    for g, (t0, t1) in enumerate(groups):
                        scale = sm[:, S_GFIN + k:S_GFIN + k + 1] if final else gs[:, g, k:k + 1]
                        if final:
                            dst, done = y_sb[:, k, t0:t1], y_done
                        else:
                            dst, done = ht[:, k % 2, t0:t1], ht_done
                            if k >= 2:
                                dve.wait_ge(h_lo_done, hs + (k - 2) * len(groups) + g + 1)
                        V.scalar_tensor_tensor(dst, x_sb[:, k, t0:t1], scale, ps[:, 6 + g, 0:t1 - t0],
                                               ALU.mult, ALU.mult).then_inc(done, 1)
                    if k >= 1 and not final:
                        for g in range(len(groups)):
                            lo(k - 1, g)
                if not final:
                    for g in range(len(groups)):
                        lo(KT - 1, g)

            def head_norms(ch):
                k = 2 * ch["l"] + ch["c"]
                dve.wait_ge(raw_squared, k + 1)
                nt = len(ch["tiles"])
                rows = [(0, nt, 0, 6)] if ch["tiles"][-1]["cols"][1] == CHUNK else [(0, 4, 0, 6), (4, 6, 0, 4)]
                sq = rawsq[:, :, :].rearrange("p t (s d) -> p t s d", d=HD)
                ssv = head_ss[:, :].rearrange("p (t s) -> p t s", s=6)
                if len(rows) > 1:
                    step(V.memset(head_ss[:, :], 1.0))
                for n, (a, b, s0, s1) in enumerate(rows):
                    ins = V.tensor_reduce(ssv[:, a:b, s0:s1], sq[:, a:b, s0:s1, :], AX.X, ALU.add)
                    if n == len(rows) - 1:
                        ins.then_inc(head_ss_done, 1)
                dve.wait_ge(head_sd_done, k + 1)
                n = 36 if nt == 6 else 24
                step(V.reciprocal(head_r[:, 0:n], head_sd[:, 0:n]))

            def rope_tile(ch, x):
                t, i = x["t"], x["tile"] % 2
                if x["tile"] >= 1:
                    dve.wait_ge(rope_done, x["tile"])
                if x["tile"] >= 2:
                    dve.wait_ge(split_lo_done, x["prev2_his"])
                p = ch["p"]
                last = len(x["maps"]) - 1
                for n, (s0, m, kind, _) in enumerate(x["maps"]):
                    src = raw_of(ch, t)[:, s0 * HD:(s0 + m) * HD].rearrange("p (m d) -> p m d", m=m)
                    if p == 0:
                        r = head_r[:, 6 * t + s0:6 * t + s0 + m].unsqueeze(2).broadcast_to([P, m, HD])
                        step(V.tensor_tensor(src, src, r, ALU.mult))
                    dst = roped[:, i, s0:s0 + m, :]
                    if t >= SEQ // P:
                        if p == 0:
                            col = (S_GQ if kind == "q" else S_GK) + ch["l"] * HD
                            ins = V.tensor_tensor(dst, src, sm[:, col:col + HD].unsqueeze(1).broadcast_to([P, m, HD]),
                                                  ALU.mult)
                        else:
                            ins = V.tensor_copy(dst, src)
                    else:
                        if p == 0:
                            w = 0 if kind == "q" else 2
                            ct, st = tabs[:, w, t, :], tabs[:, w + 1, t, :]
                        else:
                            ct, st = cos[:, t, :], sin[:, t, :]
                        r1 = rope1[:, s0:s0 + m, :]
                        step.mark(V.tensor_tensor(r1, src, ct.unsqueeze(1).broadcast_to([P, m, HD]), ALU.mult))
                        sv = src.rearrange("p m (a b d) -> p m a b d", a=2, b=2)
                        tv = st.rearrange("p (a b d) -> p a b d", a=2, b=2)
                        ov = rope2[:, s0:s0 + m, :].rearrange("p m (a b d) -> p m a b d", a=2, b=2)
                        for b in range(2):
                            step.mark(V.tensor_tensor(ov[:, :, :, b, :], sv[:, :, :, 1 - b, :],
                                                      tv[:, :, b, :].unsqueeze(1).broadcast_to([P, m, 2, 16]),
                                                      ALU.mult))
                        step.wait()
                        ins = V.tensor_tensor(dst, r1, rope2[:, s0:s0 + m, :], ALU.add)
                    if n == last:
                        ins.then_inc(rope_done, 1)
                    else:
                        step.mark(ins)

            def tile_lo(x):
                i = x["tile"] % 2
                b = 0
                for n, (s0, m, kind, _) in enumerate(x["maps"]):
                    dve.wait_ge(split_hi_done, x["his"] - len(x["maps"]) + n + 1)
                    u = roped[:, i, s0:s0 + m, :]
                    if kind == "q":
                        ins = V.scalar_tensor_tensor(split[:, i, b:b + m, 1, :], u, SCALE, split[:, i, b:b + m, 0, :],
                                                     ALU.mult, ALU.subtract)
                        b += m
                    else:
                        ins = V.tensor_tensor(split[:, i, b + 1:b + 2 * m:2, :, :],
                                              u.unsqueeze(2).broadcast_to([P, m, 2, HD]),
                                              split[:, i, b:b + 2 * m:2, :, :], ALU.subtract)
                        b += 2 * m
                    ins.then_inc(split_lo_done, 1)

            def values_lo(ch, x):
                s0, n = x["v"]
                t = x["t"]
                dve.wait_ge(v_hi_done, x["vn"] + 1)
                if n == 2:
                    src = raw_of(ch, t)[:, s0 * HD:(s0 + 2) * HD].rearrange("p (k d) -> p k d", k=2)
                    hv = v_hi[:, t, :].bitcast(f32).rearrange("p (k a d) -> p k a d", k=2, a=2)
                    lv = v_lo[:, t, :].rearrange("p (k a d) -> p k a d", k=2, a=2)
                    for a in range(2):
                        ins = V.tensor_tensor(lv[:, :, a, :], src, hv[:, :, a, :], ALU.subtract)
                else:
                    ins = V.tensor_tensor(v_lo[:, t, :], raw_of(ch, t)[:, s0 * HD:(s0 + n) * HD],
                                          v_hi[:, t, :].bitcast(f32), ALU.subtract)
                ins.then_inc(v_lo_done, 1)

            tiles = [x for ch in chunks for x in ch["tiles"] if "tile" in x]
            for n, x in enumerate(tiles):
                if n >= 2:
                    x["prev2_his"] = tiles[n - 2]["his"]

            def turn_chunk(ch):
                p = ch["p"]
                if p == 0:
                    head_norms(ch)
                before = None
                for x in ch["tiles"]:
                    if "tile" in x:
                        if p > 0:
                            dve.wait_ge(acc_copied, x["acc"] + 1)
                        rope_tile(ch, x)
                    if before:
                        tile_lo(before)
                    before = x if "tile" in x else None
                    if x["v"]:
                        values_lo(ch, x)
                if before:
                    tile_lo(before)

            def project(l, p, c):
                ch = chunk_of(l, p, c)
                if ch["after"] is not None:
                    dve.wait_ge(pv_done, phase_of(l, ch["after"])["items"][-1]["T"][-1]["tid"] + 1)
                if ch["prev"]:
                    turn_chunk(ch["prev"])
                elif l == 0:
                    ada_straight(2 * KT, 3 * KT)
                    add_bias(2 * KT, 3 * KT)
                if (p, c) == (2, 1):
                    turn_chunk(ch)

            def attend(l, p):
                def finish(s):
                    it, sid = s["item"], s["sid"]
                    k = it["k1"] - it["k0"]
                    c = slice(sid % 8, sid % 8 + 1)
                    dve.wait_ge(exp_done, sid + 1)
                    ins = V.reciprocal(ri[:, c], rs[:, c])
                    ins.then_inc(recip_done, 1)
                    if s["m"] == 1:
                        dve.wait_ge(recip_done, sid + 1)
                        step(V.tensor_scalar(rl[:, c], ri[:, c], nlam[:, l:l + 1], None, ALU.mult))
                        dve.wait_ge(scaled_done, scaled_no[sid - 1])
                        buf = p_sb[:, it["slots"][s["qi"]], 0:k]
                        V.scalar_tensor_tensor(buf, ptmp[:, 0:k], rl[:, c], buf, ALU.mult, ALU.add) \
                            .then_inc(probs_done, 1)

                def pt_rest(s):
                    tid = s["tid"]
                    nq = s["item"]["t1"] - s["item"]["t0"]
                    dve.wait_ge(pt_hi_done, tid + 1)
                    V.tensor_tensor(pt_lo[s["buf"]][:, 0:nq], ps[:, 4 + tid % TURNS, 0:nq],
                                    pt_hi[s["buf"]][:, 0:nq].bitcast(f32), ALU.subtract).then_inc(pt_lo_done, 1)

                sums, rests = [], []
                for kind, s in phase_of(l, p)["order"]:
                    it = s["item"]
                    if kind == "S":
                        sid = s["sid"]
                        k = it["k1"] - it["k0"]
                        dve.wait_ge(scores_done, sid + 1)
                        src = ps[:, 2 * (sid % 2):2 * (sid % 2) + 2, :].rearrange("p a b -> p (a b)")[:, 0:k]
                        V.tensor_reduce(nb[:, sid % 8:sid % 8 + 1], src, AX.X, ALU.max, negate=True) \
                            .then_inc(bias_done, 1)
                        while rests:
                            pt_rest(rests.pop(0))
                        while sums:
                            finish(sums.pop(0)[0])
                        sums.append([s, 0])
                    elif kind == "T":
                        while sums and (sums[0][0]["item"] is it or sums[0][1]):
                            finish(sums.pop(0)[0])
                        for r in sums:
                            r[1] += 1
                        while rests:
                            pt_rest(rests.pop(0))
                        rests.append(s)
                    elif rests and rests[0] is s:
                        pt_rest(rests.pop(0))
                assert not sums and not rests

            step.mark(V.memset(eps[:, :], EPS))
            V.memset(zero[:, :], 0.0).then_inc(a_lo_done, 1)
            dve.wait_ge(small_loaded, 32)
            for l in range(DEPTH):
                for n in range(2):
                    step(V.tensor_tensor_reduce(ht[:, 0, 0:HD],
                                                lamv[:, l, 2 * n, :], lamv[:, l, 2 * n + 1, :], 1.0, 0.0,
                                                ALU.mult, ALU.add, lamw[:, 2 * l + n:2 * l + n + 1]))
            V.tensor_scalar(gsub[:, 0:1], sm[:, S_GSUB:S_GSUB + 1], 1.0 - LAM_INIT[0], None, ALU.mult) \
                .then_inc(lam_sum, 1)
            step(V.tensor_scalar(gsub[:, 1:2], sm[:, S_GSUB + 1:S_GSUB + 2], 1.0 - LAM_INIT[1], None, ALU.mult))
            dve.wait_ge(c_ready, 1)
            ada_straight(0, FIRST_ADA)
            add_bias(0, FIRST_ADA)
            norm_gains(gs1, KT, S_GATTN)
            rope_tables(0)
            dve.wait_ge(lam_exp, 1)
            for l in range(DEPTH):
                step(V.tensor_tensor(nlam[:, l:l + 1], lamw[:, 2 * l + 1:2 * l + 2], lamw[:, 2 * l:2 * l + 1],
                                     ALU.subtract))
                step(V.tensor_scalar(nlam[:, l:l + 1], nlam[:, l:l + 1], -LAM_INIT[l], None, ALU.add))
            for d in range(KT):
                add_squares(d, 0, norms[0])
            norm(0)
            for l in range(DEPTH):
                groups = token_groups(l)
                T = groups[-1][1]
                nt = n_tiles(groups)
                for what, *args in LAYER_STEPS:
                    (project if what == "project" else attend)(l, *args)
                s = ("sub", l)
                stats_scales(s, B_HEADS * nt, None)

                def o_lo(k):
                    for g, (t0, t1) in enumerate(groups):
                        dve.wait_ge(o_hi_done, sub_oh[l] + k * len(groups) + g + 1)
                        V.tensor_tensor(ol[:, k, t0:t1], o_sb[:, k, t0:t1], oh[:, k, t0:t1].bitcast(f32),
                                        ALU.subtract).then_inc(o_lo_done, 1)

                for b in range(B_HEADS):
                    for t in range(nt):
                        diag(s, b * nt + t)
                    dve.wait_ge(spread_done, stat_base(s) + (b + 1) * nt)
                    for g, (t0, t1) in enumerate(groups):
                        ins = V.scalar_tensor_tensor(o_sb[:, 4 + b, t0:t1], o_sb[:, 4 + b, t0:t1], gsub[:, l:l + 1],
                                                     ps[:, 6 + g, 0:t1 - t0], ALU.mult, ALU.mult)
                    ins.then_inc(o_normed, 1)
                for k in range(KT):
                    o_lo(k)

                def update(c, gate, x_col):
                    wait_unit(dve, c)
                    for g, (t0, t1) in enumerate(groups):
                        xs = x_sb[:, x_col, t0:t1]
                        ins = V.scalar_tensor_tensor(xs, ps[:, 2 * (c % 4) + g, 0:t1 - t0],
                                                     mod[:, g, l * N_ADA + gate + x_col:l * N_ADA + gate + x_col + 1],
                                                     xs, ALU.mult, ALU.add)
                    ins.then_inc(bank_read, 1)

                dve.wait_ge(x_loaded, 16 * (l + 2))
                for d in range(KT):
                    update(wo_unit(l) + d, 2 * KT, d)
                    add_squares(d, 2 * l + 1, groups)
                    if l == 0:
                        if d == 0:
                            dve.wait_ge(c_ready, 2)
                        ada_straight(3 * KT + 2 * d, 3 * KT + 2 * d + 2)
                if l == 0:
                    add_bias(3 * KT, 5 * KT)
                    norm_gains(gs2, 4 * KT, S_GFFN)
                norm(2 * l + 1)
                for part, n in enumerate(PARTS):
                    pair0 = l * FF_TILES + sum(PARTS[:part])
                    ada0 = 5 * KT + 2 * sum(PARTS[:part]) + (KT if part else 0)

                    def pairs(i, part=part, pair0=pair0, l=l, groups=groups, T=T, ada0=ada0):
                        for half in range(2):
                            for gv, buf in enumerate((conv_g, conv_v)):
                                c = up_unit(l, part) + 2 * half + gv
                                wcol = S_CONV + (l * 2 * FF_TILES + gv * FF_TILES + sum(PARTS[:part]) + half) * 4
                                dve.wait_ge(conv_started, 4 * i + (2 * (pair0 + half) + gv + 1))
                                for tap in range(2):
                                    w = wcol + 2 * tap
                                    for g, (t0, t1) in enumerate(groups):
                                        dst = buf[:, t0 + 1:t1] if tap == 0 else buf[:, t0:t1 - 1]
                                        n_ = t1 - t0
                                        src = ps[:, 2 * (c % 4) + g, 0:n_ - 1] if tap == 0 else \
                                            ps[:, 2 * (c % 4) + g, 1:n_]
                                        ins = V.scalar_tensor_tensor(dst, src, sm[:, bass.ds(8 * i + w, 1)], dst,
                                                                     ALU.mult, ALU.add)
                                        if tap == 0 or g < len(groups) - 1:
                                            step.mark(ins)
                                    if tap == 0:
                                        step.wait()
                                ins.then_inc(bank_read, 1)
                            dve.wait_ge(silu_done, 2 * i + (pair0 + half + 1))
                            dve.wait_ge(bank_read, 4 * i + (evac_index(c) + 1))
                            V.tensor_tensor(conv_g[:, 0:T], conv_g[:, 0:T], conv_v[:, 0:T], ALU.mult) \
                                .then_inc(prod_done, 1)
                            dve.wait_ge(a_hi_done, 2 * i + (pair0 + half + 1))
                            V.tensor_tensor(a_lo[:, 2 * i + half, 0:T], conv_g[:, 0:T],
                                            a_hi[:, 2 * i + half, 0:T].bitcast(f32), ALU.subtract).then_inc(a_lo_done, 1)
                            if l == 0:
                                for j in range(2):
                                    a = ada0 + 2 * half + j
                                    ada_tile(a, 2 if part == 0 else 1, i,
                                             lambda s: ada_sum[:, s, 2 * half + j:2 * half + j + 1])
                        if l == 0:
                            dve.wait_ge(ada_used, 4 * i + (ada0 + 4))
                            for s in range(2 if part == 0 else 1):
                                step(V.tensor_copy(mod[:, s, bass.ds(4 * i + ada0, 4)], ada_sum[:, s, :]))

                    per = 2 * 2 * (len(groups) + len(groups) - 1)
                    if l == 0:
                        per += 6 if part == 0 else 1
                    step.loop(n // 2, per, pairs)
                    if l == 0 and part == 0:
                        add_bias(5 * KT, N_ADA)
                    for d in range(KT):
                        c = down_unit(l, part) + d
                        update(c, 5 * KT, d)
                        if l == 0 and part == 0:
                            ada_straight(ada0 + 2 * n + d, ada0 + 2 * n + d + 1)
                        if part == len(PARTS) - 1:
                            add_squares(d, 2 * l + 2, norms[2 * l + 2])
                            if l == 0 and d % 2 == 1:
                                ada_straight(ada0 + 2 * n + d // 2, ada0 + 2 * n + d // 2 + 1, streams=1)
                if l == 0:
                    add_bias(N_ADA, N_ADA + 2 * KT)
                    add_bias(N_ADA + 2 * KT, 2 * N_ADA, streams=1)
                    norm_gains(gs1, N_ADA + KT, S_GATTN + KT)
                    norm_gains(gs2, N_ADA + 4 * KT, S_GFFN + KT, streams=1)
                    rope_tables(1)
                norm(2 * l + 2)


_OUT_SHAPE = (P, KT, SEQ)


def kernel(x, c, ctx, c_ctx, w_ada, b_ada, g_attn, w_in, g_qa, g_ka, lam_q1, lam_k1, lam_q2, lam_k2,
           g_sub, w_o, g_ffn, w_up, conv_w, conv_b, w_down, g_final):
    import numpy as np
    import concourse.bacc as bacc
    from concourse import mybir as mb
    from concourse.bass_utils import run_bass_kernel_spmd

    f = np.float32

    def feature_cols(v):
        v = np.asarray(v)
        return np.moveaxis(v.reshape(v.shape[:-1] + (-1, P)), -1, 0)

    def tiles(w):
        k, n = w.shape
        return w.reshape(k // P, P, n // P, P).transpose(2, 1, 0, 3).reshape(n // P, P, k)

    tok = np.concatenate([np.asarray(x)[0], np.asarray(ctx)[0]], axis=0)
    x_arr = np.ascontiguousarray(tok.T.reshape(KT, P, TOK).transpose(1, 0, 2))
    cc = np.concatenate([np.asarray(c)[0], np.asarray(c_ctx)])
    pos = np.arange(SEQ)
    quarter = HD // 4
    inv = (f(10000.0) ** (-np.arange(quarter, dtype=f) / f(quarter))).astype(f)
    ang_r = (pos // GRID_W).astype(f)[:, None] * inv[None]
    ang_c = (pos % GRID_W).astype(f)[:, None] * inv[None]
    cos = np.concatenate([np.cos(ang_r)] * 2 + [np.cos(ang_c)] * 2, -1).astype(f)
    sin = np.concatenate([-np.sin(ang_r), np.sin(ang_r), -np.sin(ang_c), np.sin(ang_c)], -1).astype(f)

    sm = np.zeros((P, S_END), f)
    sm[:, S_IDENT:S_IDENT + P] = np.eye(P, dtype=f)
    sm[:, S_ONES:S_ONES + P] = 1
    sm[:, S_COS:S_COS + 4 * HD] = cos.reshape(4, P, HD).transpose(1, 0, 2).reshape(P, -1)
    sm[:, S_SIN:S_SIN + 4 * HD] = sin.reshape(4, P, HD).transpose(1, 0, 2).reshape(P, -1)
    sm[:, S_BADA:S_GATTN] = feature_cols(b_ada).reshape(P, -1)
    sm[:, S_GATTN:S_GFFN] = feature_cols(g_attn).reshape(P, -1)
    sm[:, S_GFFN:S_GFIN] = feature_cols(g_ffn).reshape(P, -1)
    sm[:, S_GFIN:S_CONV] = feature_cols(g_final).reshape(P, -1)
    conv = np.concatenate([np.asarray(conv_w), np.asarray(conv_b)[:, None]], axis=1)
    sm[:, S_CONV:S_GSUB] = feature_cols(conv).transpose(0, 1, 3, 2).reshape(P, -1)
    sm[:, S_GSUB:S_GQ] = np.asarray(g_sub).T
    sm[:, S_GQ:S_GK] = np.asarray(g_qa).reshape(1, -1)
    sm[:, S_GK:S_END] = np.asarray(g_ka).reshape(1, -1)
    lam = np.stack([np.asarray(v) for v in (lam_q1, lam_k1, lam_q2, lam_k2)], axis=1).reshape(1, -1)
    lam = np.ascontiguousarray(np.broadcast_to(lam, (P, LAM_COLS)))
    ada = np.ascontiguousarray(np.asarray(w_ada).transpose(0, 2, 1).reshape(DEPTH * N_ADA, P, D))

    w_in, w_o, w_up, w_down = (np.asarray(w) for w in (w_in, w_o, w_up, w_down))
    stream = np.zeros((N_UNITS, P, UNIT), f)
    aq, ak, av, bq, bk, bv = 0, 512, 640, 768, 1280, 1792
    for l in range(DEPTH):
        for p in range(3):
            if p == 0:
                cols = [[(ak, 128), (av, 128), (aq, 128)], [(aq + 128, 384)]]
            else:
                o = 256 * (p - 1)
                cols = [[(bk + o, 256), (bq + o, 128)], [(bq + o + 128, 128), (bv + o, 256)]]
            for c_ in range(2):
                w = np.concatenate([w_in[l][:, a:a + n] for a, n in cols[c_]], axis=1)
                u = in_unit(l, p, c_)
                stream[u:u + IN_UNITS, :, :UNIT_K * CHUNK] = \
                    w.reshape(IN_UNITS, UNIT_K, P, CHUNK).transpose(0, 2, 1, 3).reshape(IN_UNITS, P, -1)
        stream[wo_unit(l):wo_unit(l) + KT] = tiles(w_o[l])
        up = tiles(w_up[l])
        for part, n in enumerate(PARTS):
            k0 = sum(PARTS[:part])
            u = up_unit(l, part)
            stream[u:u + 2 * n:2] = up[k0:k0 + n]
            stream[u + 1:u + 2 * n:2] = up[FF_TILES + k0:FF_TILES + k0 + n]
            d = down_unit(l, part)
            stream[d:d + KT, :, :n * P] = tiles(w_down[l][k0 * P:(k0 + n) * P])

    nc = bacc.Bacc("TRN2", target_bir_lowering=False, num_devices=1)
    arrays = dict(x_d=x_arr, cc_d=cc, small_d=sm, lam_d=lam, ada_d=ada, w_d=stream)
    aps = [nc.dram_tensor(n, a.shape, mb.dt.from_np(a.dtype), kind="ExternalInput").ap() for n, a in arrays.items()]
    out = nc.dram_tensor("out_d", _OUT_SHAPE, mb.dt.float32, kind="ExternalOutput").ap()
    spill = nc.dram_tensor("x_spill_d", _OUT_SHAPE, mb.dt.float32, kind="Internal").ap()
    backbone(nc, *aps, out, spill)
    r = run_bass_kernel_spmd(nc, [arrays], core_ids=[0])
    y = r.results[0]["out_d"]
    return y.transpose(1, 0, 2).reshape(D, SEQ).T.reshape(1, SEQ, D)
```

```python
import math
from contextlib import ExitStack

import concourse.bass as bass
from concourse import mybir

D = 1024
DEPTH = 2
SEQ, CTX = 512, 256
TOK = SEQ + CTX
GRID_W = 64
P = 128
HD = 64
KT = D // P
A_HEADS, A_KV, B_HEADS = D // 128, D // 512, D // 256
FF_TILES = ((8 * D // 3 + 127) // 128)
EPS = 1e-6
SCALE = HD ** -0.5
N_ADA = 6 * KT

CHUNK = 384
UNIT = 1024
UNIT_K = 2
IN_UNITS = KT // UNIT_K
PARTS = [8, 8, FF_TILES - 16]
LAYER_UNITS = 6 * IN_UNITS + KT + 2 * FF_TILES + len(PARTS) * KT
N_UNITS = DEPTH * LAYER_UNITS
RAW, RING = 2, 4
PROBS = 8
TURNS = 3
FIRST_ADA = 2 * KT
FIRST_GROUP = 4
ADA_GROUP = 2
MID_ADA, MID_END = 4 * KT, 5 * KT

LAYER_STEPS = [("project", 0, 0), ("project", 0, 1), ("project", 1, 0), ("attend", 0),
               ("project", 1, 1), ("project", 2, 0), ("attend", 1), ("project", 2, 1), ("attend", 2)]
SPREAD = 6
LEADS = (0, 4)

LAM_INIT = [0.8 - 0.6 * math.exp(-0.3 * l) for l in range(DEPTH)]

S_IDENT, S_ONES = 0, 128
S_COS, S_SIN = 256, 512
S_BADA = 768
S_GATTN = S_BADA + DEPTH * N_ADA
S_GFFN = S_GATTN + DEPTH * KT
S_GFIN = S_GFFN + DEPTH * KT
S_CONV = S_GFIN + KT
S_GSUB = S_CONV + DEPTH * 2 * FF_TILES * 4
S_GQ = S_GSUB + DEPTH
S_GK = S_GQ + DEPTH * HD
S_C = S_GK + DEPTH * HD
S_END = S_C + 2 * KT
LAM_COLS = DEPTH * 4 * HD


def token_groups(l):
    return [(0, SEQ), (SEQ, TOK)] if l < DEPTH - 1 else [(0, SEQ)]


def unit0(l):
    return l * LAYER_UNITS


def in_unit(l, p, c):
    return unit0(l) + (2 * p + c) * IN_UNITS


def wo_unit(l):
    return unit0(l) + 6 * IN_UNITS


def up_unit(l, part):
    return wo_unit(l) + KT + sum(2 * n + KT for n in PARTS[:part])


def down_unit(l, part):
    return up_unit(l, part) + 2 * PARTS[part]


def turn_schedule(chunks, ch):
    prev = ch["prev"]
    after = [[] for _ in range(IN_UNITS + 1)]
    if prev and prev["p"] == 0:
        xs = [(prev, x) for x in prev["tiles"]]
        after[2], after[3] = xs[:1], xs[1:3]
        if ch["p"] == 1:
            older = prev["prev"]
            after[0] = [(older, x) for x in older["tiles"][3:]]
            after[4] = xs[3:]
    elif prev:
        for u in range(1, IN_UNITS):
            after[u] = [(prev, x) for x in prev["tiles"][2 * u - 2:2 * u]]
    return after


def unit_width(n):
    return UNIT_K * CHUNK if n % LAYER_UNITS < 6 * IN_UNITS else UNIT


def unit_runs(a, b):
    cuts = [a] + [c for l in range(DEPTH) for c in (unit0(l), wo_unit(l)) if a < c < b] + [b]
    return [(c, d) for c, d in zip(cuts, cuts[1:]) if d > c]


def evac_index(n):
    l, r = divmod(n, LAYER_UNITS)
    return l * (LAYER_UNITS - 6 * IN_UNITS) + r - 6 * IN_UNITS


def chunk_plan():
    plan = []
    for l in range(DEPTH):
        last = l == DEPTH - 1
        for p in range(3):
            for c in range(2):
                ch = dict(l=l, p=p, c=c, q=len(plan), unit=in_unit(l, p, c), tiles=[])
                for t in range(TOK // P):
                    full = not (last and t >= SEQ // P)
                    if p == 0:
                        maps = [(0, 2, "k", 8), (4, 2, "q", 0)] if c == 0 else [(0, 6, "q", 2)]
                        v = (2, 2) if c == 0 else None
                    else:
                        maps = [(0, 4, "k", 4), (4, 2, "q", 0)] if c == 0 else [(0, 2, "q", 2)]
                        v = (2, 4) if c == 1 else None
                    cols = (0, CHUNK)
                    if not full:
                        maps = [m for m in maps if m[2] == "k"]
                        if c == 0:
                            cols = (0, 256)
                        elif p == 0:
                            continue
                        else:
                            cols = (128, CHUNK)
                    ch["tiles"].append(dict(t=t, maps=maps, v=v, cols=cols))
                plan.append(ch)
    n_acc = n_tile = n_v = n_group = n_hi = 0
    for ch in plan:
        ch["prev"] = plan[ch["q"] - 1] if ch["q"] % 6 else None
        ch["after"] = {(1, 1): 0, (2, 1): 1}.get((ch["p"], ch["c"]))
        for x in ch["tiles"]:
            x["acc"] = n_acc
            n_acc += 1
            if x["maps"]:
                x["tile"] = n_tile
                n_tile += 1
                x["groups"] = []
                b = 0
                for s0, n, kind, store in x["maps"]:
                    blocks = n * (2 if kind == "k" else 1)
                    for g in range(0, blocks, 4):
                        m = min(4, blocks - g)
                        x["groups"].append((n_group, b + g, m, store + g))
                        n_group += 1
                    b += blocks
                x["his"] = n_hi + len(x["maps"])
                n_hi += len(x["maps"])
            if x["v"]:
                x["vn"] = n_v
                n_v += 1
    return plan


def attention_plan(chunks):
    phases = []
    sid = tid = item_id = 0
    buf_user = {}
    for l in range(DEPTH):
        for p in range(3):
            items = []
            for g, (t0, t1) in enumerate(token_groups(l)):
                keys = range(TOK // P) if g == 0 else range(SEQ // P, TOK // P)
                for h in range(A_HEADS if p == 0 else 2):
                    it = dict(id=item_id, l=l, p=p, g=g, h=h, t0=t0, t1=t1, qt=list(range(t0 // P, t1 // P)),
                              kt=list(keys), maps=1 if p == 0 else 2, first=not items)
                    it["k0"], it["k1"] = keys[0] * P, (keys[-1] + 1) * P
                    it["S"] = []
                    for qi, q in enumerate(it["qt"]):
                        for m in range(it["maps"]):
                            it["S"].append(dict(sid=sid, q=q, qi=qi, m=m, item=it))
                            sid += 1
                    it["T"] = [dict(tid=tid + j, j=j, kt=kt, item=it) for j, kt in enumerate(it["kt"])]
                    for x in it["T"]:
                        x["buf"] = x["tid"] % (2 if p == 1 else TURNS)
                        x["buf_before"] = buf_user.get(x["buf"])
                        buf_user[x["buf"]] = x["tid"]
                    tid += len(it["kt"])
                    item_id += 1
                    items.append(it)
            slot = 0
            users = {}
            for n, it in enumerate(items):
                it["slots"], it["freed_by"] = [], []
                for _ in it["qt"]:
                    it["slots"].append(slot)
                    it["freed_by"].append(users.get(slot))
                    users[slot] = it
                    slot = (slot + 1) % PROBS

            order = []
            tiles = chunks[6 * l + 5]["tiles"] if p == 2 else []
            first = items[0]["S"]
            for n in range(max(len(first), len(tiles) + 2)):
                order += [("S", s) for s in first[n:n + 1]]
                order += [("turn", x) for x in tiles[n - 2:n - 1] if n >= 2]
                order += [("split", x) for x in tiles[n:n + 1]]
            n_front = 1
            for i, it in enumerate(items):
                T = it["T"]
                back = []
                for j in range(len(T)):
                    back.append(("T", T[j]))
                    if j >= 2:
                        back.append(("V", T[j - 2]))
                back += [("V", x) for x in T[-2:]]
                upto = i + 2
                if upto < len(items) and items[upto]["g"] == 1 and it not in items[upto]["freed_by"]:
                    upto += 1
                rest = [("S", s) for x in items[n_front:upto] for s in x["S"]]
                n_front = max(n_front, min(upto, len(items)))
                lead = LEADS[p > 0]
                order += rest[:lead]
                rest = rest[lead:]
                per_t = -(-len(rest) // SPREAD)
                for kind, x in back:
                    if kind == "T":
                        order += rest[:per_t]
                        rest = rest[per_t:]
                    order.append((kind, x))
                order += rest
            phases.append(dict(l=l, p=p, items=items, order=order))
    return phases


def backbone(nc, x_in, cc_in, small_in, lam_in, first_in, ada_in, w_in, out, x_spill):
    f32, f32r, bf16 = mybir.dt.float32, mybir.dt.float32r, mybir.dt.bfloat16
    ALU = mybir.AluOpType
    ACT = mybir.ActivationFunctionType
    AX = mybir.AxisListType

    chunks = chunk_plan()
    phases = attention_plan(chunks)

    def chunk_of(l, p, c):
        return chunks[6 * l + 2 * p + c]

    def phase_of(l, p):
        return phases[3 * l + p]

    base = -(-nc.sbuf_base // 64) * 64
    KB = 1024
    R_X = base
    R_H = R_X + 35 * KB
    R_QKV = R_H + 48 * KB
    R_O = R_QKV + 48 * KB
    R_W = R_O + 24 * KB
    R_TAB = R_W + 40 * KB
    R_SMALL = R_TAB + 4 * KB
    at = [R_SMALL]

    def place(name, shape, dt, offset):
        return nc.alloc_sbuf_tensor_at(name, shape, dt, offset=offset)

    def small(name, shape, dt=f32):
        n = 4
        for s in shape[1:]:
            n *= s
        a = place(name, shape, dt, at[0])
        at[0] += -(-n // 32) * 32
        return a

    x_sb = place("x_sb", [P, KT, TOK], f32, R_X)
    p_sb = place("p_sb", [P, PROBS, TOK], f32, R_X)
    ptmp = place("ptmp", [P, TOK], f32, R_X + 24 * KB)
    pt_at = [R_X + 27 * KB, R_X + 31 * KB, R_TAB]
    pt_hi = [place(f"pt_hi{i}", [P, SEQ], f32r, pt_at[i]) for i in range(TURNS)]
    pt_lo = [place(f"pt_lo{i}", [P, SEQ], f32r, pt_at[i] + 2 * KB) for i in range(TURNS)]
    raw = place("raw", [P, 6, CHUNK], f32, R_X)
    raw_01 = place("raw_01", [P, 6, CHUNK], f32, R_O)
    raw_10 = place("raw_10", [P, 6, CHUNK], f32, R_O + 12 * KB)
    raw_20 = place("raw_20", [P, 4, CHUNK], f32, R_O + 18 * KB)
    raw_20c = place("raw_20c", [P, 2, CHUNK], f32, R_TAB)
    rawsq = place("rawsq", [P, 6, CHUNK], f32, R_X + 9 * KB)
    split = place("split", [P, 2, 10, 2, HD], f32, R_X + 18 * KB)
    rope1 = place("rope1", [P, 6, HD], f32, R_X + 28 * KB)
    rope2 = place("rope2", [P, 6, HD], f32, R_X + 28 * KB + 1536)
    roped = place("roped", [P, 2, 6, HD], f32, R_X + 31 * KB)
    c_bc = place("c_bc", [P, 2, D], f32, R_X + 24 * KB)
    sqsum = place("sqsum", [P, TOK], f32, R_X + 32 * KB)
    h_hi = place("h_hi", [P, KT, TOK], f32r, R_H)
    h_lo = place("h_lo", [P, KT, TOK], f32r, R_H + 24 * KB)
    y_sb = place("y_sb", [P, KT, SEQ], f32, R_H)
    osq = place("osq", [P, 2, TOK], f32, R_H)
    dgo = place("dgo", [P, 4, P], f32, R_H + 6 * KB)
    qk = place("qk", [P, 12, TOK], f32r, R_QKV)
    v_hi = place("v_hi", [P, 6, 256], f32r, R_QKV + 36 * KB)
    v_lo = place("v_lo", [P, 6, 256], f32r, R_QKV + 42 * KB)
    oh = place("oh", [P, KT, TOK], f32r, R_QKV)
    ol = place("ol", [P, KT, TOK], f32r, R_QKV + 24 * KB)
    a_hi = place("a_hi", [P, 8, TOK], f32r, R_QKV)
    a_lo = place("a_lo", [P, 8, TOK], f32r, R_QKV + 24 * KB)
    o_sb = place("o_sb", [P, KT, TOK], f32, R_O)
    conv_g = place("conv_g", [P, TOK], f32, R_O)
    conv_v = place("conv_v", [P, TOK], f32, R_O + 3 * KB)
    sqt = place("sqt", [P, 2, TOK], f32, R_O)
    ht = place("ht", [P, 2, TOK], f32, R_O + 6 * KB)
    ada_first = place("ada_first", [P, FIRST_ADA, D], f32, R_H)
    mod_row = place("mod_row", [2, FIRST_ADA * P], f32, R_QKV + 20 * KB)
    ada_b = [place(f"ada_b{i}", [P, D], f32, R_O + (14 + 4 * i) * KB) for i in range(2)]
    ada_junk = place("ada_junk", [P, D], bf16, R_O + 12 * KB)
    c_inner = place("c_inner", [P, 2, D], f32, R_X + 9 * KB)
    ada_early = [place("ada_early0", [P, D], f32, R_X + 4608), place("ada_early1", [P, D], f32, R_TAB)]
    junk_early = place("junk_early", [P, D], bf16, R_O + 21 * KB)
    ada_inner = [place("ada_inner0", [P, D], f32, R_O + 12 * KB), place("ada_inner1", [P, D], f32, R_TAB)]
    junk_inner = place("junk_inner", [P, D], bf16, R_O + 16 * KB)
    dgn = place("dgn", [P, 4, P], f32, R_O + 22 * KB)
    lamv = place("lamv", [P, DEPTH, 4, HD], f32, R_O)
    w_raw = place("w_raw", [P, RAW, UNIT], f32, R_W)
    w_hi = place("w_hi", [P, RING, UNIT], f32r, R_W + 8 * KB)
    w_lo = place("w_lo", [P, RING, UNIT], f32r, R_W + 24 * KB)
    tabs = place("tabs", [P, 4, 4, HD], f32, R_TAB)
    sm = small("sm", [P, S_END])
    mod = small("mod", [P, 2, DEPTH * N_ADA])
    ada_sum = small("ada_sum", [P, 2, 4])
    gs1 = small("gs1", [P, 2, KT])
    gs2 = small("gs2", [P, 2, KT])
    silu_cols = small("silu_cols", [P, KT, 2])
    eps = small("eps", [P, 1])
    zero = small("zero", [P, 1])
    act_scrap = small("act_scrap", [P, 1])
    lamw = small("lamw", [P, 4])
    nlam = small("nlam", [P, DEPTH])
    gsub = small("gsub", [P, DEPTH])
    head_ss = small("head_ss", [P, 36])
    head_sd = small("head_sd", [P, 36])
    head_r = small("head_r", [P, 36])
    nb = small("nb", [P, 8])
    rs = small("rs", [P, 8])
    ri = small("ri", [P, 8])
    rl = small("rl", [P, 8])
    n_sd = small("n_sd", [P, 24])
    n_r = small("n_r", [P, 24])
    assert at[0] <= nc.sbuf_usable_end, (at[0], nc.sbuf_usable_end)

    raw_21 = place("raw_21", [P, 6, CHUNK], f32, R_H)
    split_21 = place("split_21", [P, 2, 10, 2, HD], f32, R_H + 24 * KB)
    rope1_21 = place("rope1_21", [P, 6, HD], f32, R_H + 34 * KB)
    rope2_21 = place("rope2_21", [P, 6, HD], f32, R_H + 34 * KB + 1536)
    roped_21 = place("roped_21", [P, 2, 6, HD], f32, R_H + 37 * KB)

    def turn_buffers(ch):
        return (split_21, rope1_21, rope2_21, roped_21) if (ch["p"], ch["c"]) == (2, 1) \
            else (split, rope1, rope2, roped)

    def ada_place(c, i=0):
        if isinstance(i, int) and 3 * KT <= c < 3 * KT + 4:
            return ada_early[c % 2], c_inner, junk_early
        if isinstance(i, int) and 3 * KT + 4 <= c < 4 * KT:
            return ada_inner[c % 2], c_inner, junk_inner
        return ada_b[c % 2], c_bc, ada_junk

    def raw_of(ch, t):
        if (ch["p"], ch["c"]) == (0, 1):
            return raw_01[:, t, :]
        if (ch["p"], ch["c"]) == (1, 0):
            return raw_10[:, t, :]
        if (ch["p"], ch["c"]) == (2, 0):
            return raw_20[:, t, :] if t < 4 else raw_20c[:, t - 4, :]
        if (ch["p"], ch["c"]) == (2, 1):
            return raw_21[:, t, :]
        return raw[:, t, :]

    ident = sm[:, S_IDENT:S_IDENT + P]
    ones = sm[:, S_ONES:S_ONES + P]

    ctx = ExitStack()
    with ctx:
        ps = ctx.enter_context(nc.psum_tensor("ps", [P, 8, 512], f32))

        def sem(name):
            return ctx.enter_context(nc.semaphore(name))

        small_loaded = sem("small_loaded")
        x_loaded = sem("x_loaded")
        c_loaded = sem("c_loaded")
        c_ready = sem("c_ready")
        silu_cols_done = sem("silu_cols_done")
        mod_row_done = sem("mod_row_done")
        mod_row_copied = sem("mod_row_copied")
        first_mod_done = sem("first_mod_done")
        ada_loaded = [sem("ada_loaded0"), sem("ada_loaded1")]
        first_ada_loaded = [sem(f"first_ada_loaded{i}") for i in range(FIRST_ADA // FIRST_GROUP)]
        ada_used = sem("ada_used")
        w_loaded = [sem("w_loaded0"), sem("w_loaded1")]
        w_hi_done = sem("w_hi_done")
        w_lo_done = sem("w_lo_done")
        unit_done = sem("unit_done")
        acc_done = sem("acc_done")
        acc_copied = sem("acc_copied")
        raw_squared = sem("raw_squared")
        head_ss_done = sem("head_ss_done")
        head_sd_done = sem("head_sd_done")
        rope_done = sem("rope_done")
        split_hi_done = sem("split_hi_done")
        split_lo_done = sem("split_lo_done")
        v_hi_done = sem("v_hi_done")
        v_lo_done = sem("v_lo_done")
        qk_turned = sem("qk_turned")
        qk_stored = sem("qk_stored")
        scores_done = sem("scores_done")
        bias_done = sem("bias_done")
        exp_done = sem("exp_done")
        recip_done = sem("recip_done")
        scaled_done = sem("scaled_done")
        probs_done = sem("probs_done")
        turned = sem("turned")
        pt_hi_done = sem("pt_hi_done")
        pt_lo_done = sem("pt_lo_done")
        pv_done = sem("pv_done")
        o_done = sem("o_done")
        osq_done = sem("osq_done")
        o_normed = sem("o_normed")
        o_hi_done = sem("o_hi_done")
        o_lo_done = sem("o_lo_done")
        sq_done = sem("sq_done")
        sqsum_done = sem("sqsum_done")
        ss_done = sem("ss_done")
        sd_done = sem("sd_done")
        diag_done = sem("diag_done")
        spread_done = sem("spread_done")
        ht_done = sem("ht_done")
        h_hi_done = sem("h_hi_done")
        h_lo_done = sem("h_lo_done")
        bank_read = sem("bank_read")
        conv_started = sem("conv_started")
        silu_done = sem("silu_done")
        prod_done = sem("prod_done")
        a_hi_done = sem("a_hi_done")
        a_lo_done = sem("a_lo_done")
        lam_sum = sem("lam_sum")
        lam_exp = sem("lam_exp")
        x_spilled = sem("x_spilled")
        y_done = sem("y_done")
        stored = sem("stored")
        dve_step = sem("dve_step")
        act_step = sem("act_step")

        class Steps:

            def __init__(self, eng, s):
                self.eng, self.s, self.n, self.i, self.per, self.k = eng, s, 0, 0, 0, 0

            def mark(self, ins):
                self.k += 1
                ins.then_inc(self.s, 1)

            def wait(self):
                self.eng.wait_ge(self.s, self.i * self.per + (self.n + self.k))

            def __call__(self, ins):
                self.mark(ins)
                self.wait()

            def loop(self, n, per, body):
                self.n, self.k = self.n + self.k, 0
                self.per = per
                with self.eng.Fori(0, n) as i:
                    self.i = i
                    body(i)
                    assert self.k == per, (self.k, per)
                self.n, self.i, self.k, self.per = self.n + n * per, 0, 0, 0

        def wait_unit(e, c, i=0):
            l, r = divmod(c, LAYER_UNITS)
            done_in = l * 6 + min(r, 6 * IN_UNITS) // IN_UNITS
            if r < 6 * IN_UNITS and r % IN_UNITS == IN_UNITS - 1:
                e.wait_ge(acc_done, chunks[l * 6 + r // IN_UNITS]["tiles"][-1]["acc"] + 1)
            else:
                e.wait_ge(unit_done, 4 * i + (c + 1 - done_in))

        norms = []
        for l in range(DEPTH):
            norms += [[(0, SEQ), (SEQ, TOK)], token_groups(l)]
        norms.append([(0, SEQ)])

        def n_tiles(groups):
            return sum((b - a) // P for a, b in groups)

        def norm_counts(j):
            tiles = sum(n_tiles(g) for g in norms[:j])
            hs = sum(len(g) * KT for g in norms[:j])
            return tiles, hs

        stat_order = [("norm", 0)]
        for l in range(DEPTH):
            stat_order += [("sub", l), ("norm", 2 * l + 1), ("norm", 2 * l + 2)]

        def stat_tiles(s):
            kind, j = s
            return 4 * n_tiles(token_groups(j)) if kind == "sub" else n_tiles(norms[j])

        def stat_index(s):
            return stat_order.index(s)

        def stat_base(s):
            return sum(stat_tiles(r) for r in stat_order[:stat_index(s)])

        sub_oh = [sum(KT * len(token_groups(k)) for k in range(l)) for l in range(DEPTH)]
        sub_sq = [sum(4 for k in range(l)) for l in range(DEPTH)]

        scaled_no, comb_no = {}, {}
        divided = {}
        for ph in phases:
            for kind, s in ph["order"]:
                if kind == "S" and s["m"] == s["item"]["maps"] - 1:
                    scaled_no[s["sid"]] = len(scaled_no) + 1
                    divided[s["sid"] - s["m"]] = len(scaled_no)
                if kind == "S" and s["m"] == 1:
                    comb_no[s["sid"]] = len(comb_no) + 1

        block = ctx.enter_context(nc.Block())

        @block.sync
        def _(sp):
            def load_unit(c, i=0, first=False):
                if not first:
                    sp.wait_ge(w_lo_done, 4 * i + (c - RAW + 1))
                n = unit_width(c)
                sp.dma_start(w_raw[:, c % RAW, 0:n], w_in[4 * i + c, :, 0:n]).then_inc(w_loaded[c % RAW], 16)

            def load_ada(c, i=0, first=False):
                if not first:
                    sp.wait_ge(ada_used, 4 * i + (c - 1))
                sp.dma_start(ada_place(c, i)[0][:, :], ada_in[4 * i + c, :, :]).then_inc(ada_loaded[c % 2], 16)

            def load_c(dst=c_bc):
                sp.dma_start(dst[:, :, :].rearrange("p a k -> p (a k)"),
                             cc_in.partition_broadcast(P)).then_inc(c_loaded, 16)

            def units(a, b):
                for c, d in unit_runs(a, b):
                    with sp.Fori(0, (d - c) // RING) as i:
                        for j in range(RING):
                            load_unit(c + j, i)

            sp.dma_start(sm[:, :], small_in).then_inc(small_loaded, 16)
            sp.dma_start(lamv[:, :, :, :].rearrange("p l a k -> p (l a k)"), lam_in).then_inc(small_loaded, 16)
            sp.dma_start(x_sb[:, :, :], x_in).then_inc(x_loaded, 16)
            for n in range(RAW):
                load_unit(n, first=True)
            n_first = FIRST_ADA // FIRST_GROUP
            for g in range(n_first):
                if g == n_first - 1:
                    for n in range(RAW, RING):
                        load_unit(n)
                sp.dma_start(ada_first[:, g * FIRST_GROUP:(g + 1) * FIRST_GROUP, :].rearrange("p a k -> p (a k)"),
                             first_in[g, :, :]).then_inc(first_ada_loaded[g], 16)
            load_c()
            a = FIRST_ADA
            for j in range(2):
                load_ada(a + j, first=True)
            for j in range(RING):
                load_unit(RING + j)
                if j:
                    load_ada(a + 2 * j)
                    load_ada(a + 2 * j + 1)
            u = in_unit(0, 1, 1)
            units(2 * RING, u + RING)
            sp.wait_ge(pv_done, phase_of(0, 0)["items"][-1]["T"][-1]["tid"] + 1)
            load_c(c_inner)
            a = 3 * KT
            for j in range(2):
                load_ada(a + j, first=True)
            for j in range(RING):
                load_unit(u + RING + j)
            load_ada(a + 2)
            load_ada(a + 3)
            sp.wait_ge(split_lo_done, chunk_of(0, 1, 0)["tiles"][-1]["his"])
            load_ada(a + 4)
            load_ada(a + 5)
            u = in_unit(0, 2, 0)
            load_unit(u + RING)
            load_ada(a + 6)
            load_ada(a + 7)
            for j in range(1, RING):
                load_unit(u + RING + j)
            units(u + 2 * RING, wo_unit(0) + RING)
            sp.wait_ge(o_lo_done, sub_oh[1])
            load_c()
            def load_mid(g):
                b = slice(g * ADA_GROUP, (g + 1) * ADA_GROUP)
                a = slice(MID_ADA + g * ADA_GROUP, MID_ADA + (g + 1) * ADA_GROUP)
                sp.dma_start(ada_first[:, b, :], ada_in[a, :, :].rearrange("a p k -> p a k")) \
                    .then_inc(first_ada_loaded[g], 16)

            for g in range((MID_END - MID_ADA) // ADA_GROUP):
                load_mid(g)
                if g:
                    load_unit(wo_unit(0) + RING + g - 1)
            for d in range(g, KT):
                load_unit(wo_unit(0) + RING + d)
            a = 5 * KT
            for part, n in enumerate(PARTS):
                u = up_unit(0, part) + RING
                with sp.Fori(0, n // 2) as i:
                    for j in (0, 2):
                        for unit in (u + j, u + j + 1):
                            load_unit(unit, i)
                        for tile in (a + j, a + j + 1):
                            load_ada(tile, i)
                a += 2 * n
                u = down_unit(0, part) + RING
                if part == 1:
                    units(u, u + KT)
                else:
                    for j in range(KT):
                        load_unit(u + j)
                        if part == 0 or j % 2 == 0:
                            load_ada(a)
                            a += 1
            assert a == DEPTH * N_ADA
            units(down_unit(0, len(PARTS) - 1) + KT + RING, N_UNITS)

        @block.gpsimd
        def _(pool):
            def split_unit(c, i=0):
                pool.wait_ge(w_hi_done, 4 * i + (c + 1))
                n = unit_width(c)
                nc.gpsimd.tensor_tensor(w_lo[:, c % RING, 0:n], w_raw[:, c % RAW, 0:n],
                                        w_hi[:, c % RING, 0:n].bitcast(f32), ALU.subtract).then_inc(w_lo_done, 1)

            def units(a, b):
                for c, d in unit_runs(a, b):
                    with pool.Fori(0, (d - c) // RING) as i:
                        for j in range(RING):
                            split_unit(c + j, i)

            for n in range(RING):
                split_unit(n)
            done = RING
            for l in range(DEPTH):
                for at_step, (what, p, *c) in enumerate(LAYER_STEPS):
                    if what == "project":
                        if LAYER_STEPS[at_step + 1][0] == "attend":
                            upto = in_unit(l, p, c[0]) + IN_UNITS + RING
                            units(done, upto)
                            done = upto
                        continue
                    for kind, s in phase_of(l, p)["order"]:
                        if kind != "S" or s["m"] != s["item"]["maps"] - 1:
                            continue
                        it, sid = s["item"], s["sid"]
                        k = it["k1"] - it["k0"]
                        pool.wait_ge(recip_done, sid + 1)
                        if s["m"]:
                            pool.wait_ge(probs_done, comb_no[sid])
                        buf = p_sb[:, it["slots"][s["qi"]], 0:k]
                        r = (sid - s["m"]) % 8
                        nc.gpsimd.tensor_tensor(buf, buf, ri[:, r:r + 1].broadcast_to([P, k]),
                                                ALU.mult).then_inc(scaled_done, 1)
                upto = min(up_unit(l, 0) + RING, N_UNITS)
                units(done, upto)
                end = min(unit0(l + 1) + RING, N_UNITS)
                units(upto, end)
                done = end

        def wait_probs(e, it):
            e.wait_ge(scaled_done, scaled_no[it["S"][-1]["sid"]])

        @block.tensor
        def _(pe):
            def spread_stats(s, cols, pieces):
                for k, (bank, col) in enumerate(pieces):
                    g = stat_base(s) + cols + k
                    dg = dgo if s[0] == "sub" else dgn
                    pe.wait_ge(diag_done, g + 1)
                    nc.tensor.matmul(ps[:, bank, col:col + P], ones, dg[:, (cols + k) % 4, :],
                                     start=True, stop=True).then_inc(spread_done, 1)

            def norm_stats(j):
                groups = norms[j]
                pe.wait_ge(sqsum_done, KT * (j + 1))
                for t in range(n_tiles(groups)):
                    mm = nc.tensor.matmul(ps[:, 5, t:t + 1], sqsum[:, t * P:(t + 1) * P], ones[:, 0:1],
                                          start=True, stop=True)
                mm.then_inc(ss_done, 1)
                spread_stats(("norm", j), 0, [(6 + t // 4, (t % 4) * P) for t in range(n_tiles(groups))])

            def three(out, lhs, rhs, first, last):
                (lh, ll), (rh, rl_) = lhs, rhs
                nc.tensor.matmul(out, lh, rh, start=first, stop=False)
                nc.tensor.matmul(out, lh, rl_, start=False, stop=False)
                return nc.tensor.matmul(out, ll, rh, start=False, stop=last)

            def turn_tile(ch, x, last_item=None):
                if "tile" not in x:
                    return
                split = turn_buffers(ch)[0]
                pe.wait_ge(split_lo_done, x["his"])
                for g, b, m, store in x["groups"]:
                    if g >= 2:
                        pe.wait_ge(qk_stored, g - 1)
                    if last_item is not None:
                        pe.wait_ge(pt_lo_done, last_item["T"][-1]["tid"] + 1)
                        pe.wait_ge(o_done, last_item["id"] + 1)
                        last_item = None
                    for k in range(m):
                        mm = nc.tensor.transpose(ps[:, 6 + g % 2, k * P:(k + 1) * P],
                                                 split[:, x["tile"] % 2, b + k, :, :].rearrange("p a d -> p (a d)"),
                                                 ident)
                    mm.then_inc(qk_turned, 1)

            def project(l, p, c):
                ch = chunk_of(l, p, c)
                prev = ch["prev"]
                last_item = None if ch["after"] is None else phase_of(l, ch["after"])["items"][-1]
                after = turn_schedule(chunks, ch)
                for u in range(IN_UNITS):
                    n = ch["unit"] + u
                    pe.wait_ge(w_lo_done, n + 1)
                    if p == 0 and c == 0:
                        _, hs = norm_counts(2 * l)
                        pe.wait_ge(h_lo_done, hs + 2 * (UNIT_K * u + UNIT_K))
                    for x in ch["tiles"]:
                        t = x["t"]
                        if u == 0:
                            if last_item is not None:
                                if t == 0:
                                    pe.wait_ge(exp_done, last_item["S"][-1]["sid"] + 1)
                                elif t == 4:
                                    pe.wait_ge(pt_lo_done, last_item["T"][-1]["tid"] + 1)
                            elif prev:
                                pe.wait_ge(acc_copied, [y["acc"] for y in prev["tiles"] if y["t"] <= t][-1] + 1)
                        c0, c1 = x["cols"]
                        for kk in range(UNIT_K):
                            k = UNIT_K * u + kk
                            tok = slice(t * P, (t + 1) * P)
                            col = slice(kk * CHUNK + c0, kk * CHUNK + c1)
                            mm = three(ps[:, t, c0:c1], (h_hi[:, k, tok], h_lo[:, k, tok]),
                                       (w_hi[:, n % RING, col], w_lo[:, n % RING, col]), k == 0, k == KT - 1)
                        if u == IN_UNITS - 1:
                            mm.then_inc(acc_done, 1)
                    if u < IN_UNITS - 1:
                        mm.then_inc(unit_done, 1)
                    for y, x in after[u]:
                        turn_tile(y, x, last_item if x["t"] == 0 else None)
                for y, x in after[IN_UNITS]:
                    turn_tile(y, x)

            def attend(l, p):
                ph = phase_of(l, p)
                a, b = chunk_of(l, p, 0), chunk_of(l, p, 1)
                stored = [x["groups"][-1][0] + 1 for x in a["tiles"] + b["tiles"] if "tile" in x]
                stored_a = [x["groups"][-1][0] + 1 for x in a["tiles"] if "tile" in x]
                v_all = [x["vn"] + 1 for ch in (a, b) for x in ch["tiles"] if x["v"]][-1]
                pe.wait_ge(qk_stored, stored_a[-1])
                left = b if p == 2 else chunk_of(l, p + 1, 0)
                pe.wait_ge(acc_copied, left["tiles"][-1]["acc"] + 1)
                complete = False
                for kind, s in ph["order"]:
                    if kind == "turn":
                        turn_tile(b, s)
                    if kind in ("split", "turn"):
                        continue
                    it = s["item"]
                    if not complete and (kind != "S" or it is not ph["items"][0]):
                        pe.wait_ge(qk_stored, stored[-1])
                        pe.wait_ge(v_lo_done, v_all)
                        complete = True
                    if kind == "S":
                        sid, m = s["sid"], s["m"]
                        if p == 0:
                            qs, ks = it["h"], 8 + 2 * (it["h"] // (A_HEADS // A_KV))
                        else:
                            qs, ks = 2 * it["h"] + m, 4 + 2 * (2 * it["h"] + m)
                        if sid >= 2:
                            pe.wait_ge(exp_done, sid - 1)
                        lhs = qk[:, qs, s["q"] * P:(s["q"] + 1) * P]
                        k0 = it["k0"]
                        while k0 < it["k1"]:
                            k1 = min(k0 + 512, it["k1"])
                            at0 = k0 - it["k0"]
                            dst = ps[:, 2 * (sid % 2) + at0 // 512, 0:k1 - k0]
                            nc.tensor.matmul(dst, lhs, qk[:, ks, k0:k1], start=True, stop=False)
                            mm = nc.tensor.matmul(dst, lhs, qk[:, ks + 1, k0:k1], start=False, stop=True)
                            k0 = k1
                        mm.then_inc(scores_done, 1)
                    elif kind == "T":
                        tid, j = s["tid"], s["j"]
                        if j == 0:
                            wait_probs(pe, it)
                        if tid >= TURNS:
                            pe.wait_ge(pt_lo_done, tid - TURNS + 1)
                        for qi in range(len(it["qt"])):
                            mm = nc.tensor.transpose(ps[:, 4 + tid % TURNS, qi * P:(qi + 1) * P],
                                                     p_sb[:, it["slots"][qi], j * P:(j + 1) * P], ident)
                        mm.then_inc(turned, 1)
                    else:
                        tid, j = s["tid"], s["j"]
                        nq = it["t1"] - it["t0"]
                        if j == 0 and it["id"] >= 1:
                            pe.wait_ge(o_done, it["id"])
                        pe.wait_ge(pt_lo_done, tid + 1)
                        vc = slice(P * (it["h"] // (A_HEADS // A_KV)), P * (it["h"] // (A_HEADS // A_KV)) + P) \
                            if p == 0 else slice(P * it["h"], P * it["h"] + P)
                        mm = three(ps[:, 7, 0:nq], (v_hi[:, s["kt"], vc], v_lo[:, s["kt"], vc]),
                                   (pt_hi[s["buf"]][:, 0:nq], pt_lo[s["buf"]][:, 0:nq]), j == 0, j == len(it["T"]) - 1)
                        mm.then_inc(pv_done, 1)

            def sub_stats(l):
                nt = n_tiles(token_groups(l))
                for b in range(B_HEADS):
                    pe.wait_ge(osq_done, sub_sq[l] + b + 1)
                    for t in range(nt):
                        mm = nc.tensor.matmul(ps[:, 5, b * nt + t:b * nt + t + 1], osq[:, b % 2, t * P:(t + 1) * P],
                                              ones[:, 0:1], start=True, stop=True)
                    mm.then_inc(ss_done, 1)
                for j in range(2):
                    output_part(wo_unit(l) + j, token_groups(l), range(4), sub_oh[l])
                for b in range(B_HEADS):
                    if b >= 1:
                        pe.wait_ge(o_normed, sub_sq[l] + b)
                    spread_stats(("sub", l), b * nt, [(6 + t // 4, (t % 4) * P) for t in range(nt)])

            def output_part(c, groups, ks, base):
                pe.wait_ge(w_lo_done, c + 1)
                for k in ks:
                    pe.wait_ge(o_lo_done, base + (k + 1) * len(groups))
                    for g, (t0, t1) in enumerate(groups):
                        col = slice(k * P, (k + 1) * P)
                        mm = three(ps[:, 2 * (c % 4) + g, 0:t1 - t0], (w_hi[:, c % RING, col], w_lo[:, c % RING, col]),
                                   (oh[:, k, t0:t1], ol[:, k, t0:t1]), k == 0, k == KT - 1)
                if ks[-1] == KT - 1:
                    mm.then_inc(unit_done, 1)

            def feature_unit(c, i, groups, kn, moving, wait_bank):
                pe.wait_ge(w_lo_done, 4 * i + (c + 1))
                if wait_bank:
                    pe.wait_ge(bank_read, 4 * i + (evac_index(c) - 3))
                mh, ml = moving
                for g, (t0, t1) in enumerate(groups):
                    for k in range(kn):
                        col = slice(k * P, (k + 1) * P)
                        mm = three(ps[:, 2 * (c % 4) + g, 0:t1 - t0], (w_hi[:, c % RING, col], w_lo[:, c % RING, col]),
                                   (mh[:, k, t0:t1], ml[:, k, t0:t1]), k == 0, k == kn - 1)
                mm.then_inc(unit_done, 1)

            def first_units(c, n, groups, base):
                for j in range(n):
                    pe.wait_ge(w_lo_done, c + j + 1)
                    pe.wait_ge(bank_read, evac_index(c + j) - 3)
                for k in range(KT):
                    pe.wait_ge(h_lo_done, base + (k + 1) * len(groups))
                    for j in range(n):
                        for g, (t0, t1) in enumerate(groups):
                            w = ((c + j) % RING, slice(k * P, (k + 1) * P))
                            mm = three(ps[:, 2 * ((c + j) % 4) + g, 0:t1 - t0],
                                       (w_hi[:, w[0], w[1]], w_lo[:, w[0], w[1]]),
                                       (h_hi[:, k, t0:t1], h_lo[:, k, t0:t1]), k == 0, k == KT - 1)
                        if k == KT - 1:
                            mm.then_inc(unit_done, 1)

            def first_modulation():
                pe.wait_ge(silu_cols_done, 1)
                width = FIRST_GROUP * P

                def columns(g):
                    pe.wait_ge(mod_row_copied, g + 1)
                    for c in range(g * FIRST_GROUP, (g + 1) * FIRST_GROUP):
                        mm = nc.tensor.transpose(ps[:, 4, 2 * c:2 * c + 2], mod_row[:, c * P:(c + 1) * P],
                                                 ident[0:2, 0:2])
                    mm.then_inc(first_mod_done, 1)

                for g in range(FIRST_ADA // FIRST_GROUP):
                    pe.wait_ge(first_ada_loaded[g], 16)
                    w = ada_first[:, g * FIRST_GROUP:(g + 1) * FIRST_GROUP, :].rearrange("p a k -> p (a k)")
                    for k in range(KT):
                        mm = nc.tensor.matmul(ps[0:2, g, 0:width], silu_cols[:, k, :],
                                              w[:, k * width:(k + 1) * width], start=k == 0, stop=k == KT - 1)
                    mm.then_inc(mod_row_done, 1)
                    if g:
                        columns(g - 1)
                columns(g)

            def down_start(c, groups, n, pair_end):
                for ks in (range(n - 2), range(n - 2, n)):
                    pe.wait_ge(a_lo_done, pair_end - n + ks[-1] + 1)
                    for j in range(2):
                        if ks[0] == 0:
                            pe.wait_ge(w_lo_done, c + j + 1)
                            pe.wait_ge(bank_read, evac_index(c + j) - 3)
                        for g, (t0, t1) in enumerate(groups):
                            for k in ks:
                                w = ((c + j) % RING, slice(k * P, (k + 1) * P))
                                mm = three(ps[:, 2 * ((c + j) % 4) + g, 0:t1 - t0],
                                           (w_hi[:, w[0], w[1]], w_lo[:, w[0], w[1]]),
                                           (a_hi[:, k, t0:t1], a_lo[:, k, t0:t1]), k == 0, k == n - 1)
                        if ks[0] > 0:
                            mm.then_inc(unit_done, 1)

            pe.wait_ge(small_loaded, 32)
            for l in range(DEPTH):
                groups = token_groups(l)
                if l == 0:
                    norm_stats(0)
                    first_modulation()
                for what, *args in LAYER_STEPS:
                    (project if what == "project" else attend)(l, *args)
                sub_stats(l)
                first = wo_unit(l)
                for j in range(2):
                    output_part(first + j, groups, range(4, KT), sub_oh[l])
                for j in range(2, RING):
                    feature_unit(first + j, 0, groups, KT, (oh, ol), False)
                for j in range(RING):
                    feature_unit(first + RING + j, 0, groups, KT, (oh, ol), True)
                norm_stats(2 * l + 1)
                _, hs = norm_counts(2 * l + 1)
                for part, n in enumerate(PARTS):
                    turns, c = n // 2, up_unit(l, part)
                    if part == 0:
                        first_units(c, RING - 1, groups, hs)
                        feature_unit(c + RING - 1, 0, groups, KT, (h_hi, h_lo), True)
                        turns, c = turns - 1, c + RING
                    with pe.Fori(0, turns) as i:
                        for j in range(RING):
                            feature_unit(c + j, i, groups, KT, (h_hi, h_lo), True)
                    pair_end = 1 + l * FF_TILES + sum(PARTS[:part + 1])
                    c = down_unit(l, part)
                    down_start(c, groups, n, pair_end)
                    for j in range(2, KT):
                        feature_unit(c + j, 0, groups, n, (a_hi, a_lo), True)
                norm_stats(2 * l + 2)

        @block.scalar
        def _(act):
            A = nc.scalar.activation
            step = Steps(act, act_step)

            def unit_hi(c, i=0):
                half = (c - c % RING) // 2
                if c >= RING:
                    wait_unit(act, c - RING, i)
                act.wait_ge(w_loaded[c % RAW], 32 * i + 16 * (c // RAW + 1))
                n = unit_width(c)
                A(w_hi[:, c % RING, 0:n], w_raw[:, c % RAW, 0:n], ACT.Copy).then_inc(w_hi_done, 1)

            def stats_sd(s, cols, width, n):
                ss_no = {("norm", 0): 1}
                k = 1
                for r in stat_order[1:]:
                    k += B_HEADS if r[0] == "sub" else 1
                    ss_no[r] = k
                act.wait_ge(ss_done, ss_no[s])
                A(n_sd[:, 0:cols], ps[:, 5, 0:cols], ACT.Sqrt, bias=eps[:, :], scale=1.0 / width).then_inc(sd_done, 1)

            def norm_hi(j):
                groups = norms[j]
                _, hs = norm_counts(j)
                l = j // 2
                sh = 0 if j % 2 == 0 else 3 * KT
                stats_sd(("norm", j), n_tiles(groups), D, j)
                if j == len(norms) - 1:
                    return
                if j == 0:
                    for n in range(RAW, RING):
                        unit_hi(n)
                    for g in range(FIRST_ADA // FIRST_GROUP):
                        act.wait_ge(mod_row_done, g + 1)
                        width = FIRST_GROUP * P
                        A(mod_row[:, g * width:(g + 1) * width], ps[0:2, g, 0:width], ACT.Copy) \
                            .then_inc(mod_row_copied, 1)
                for k in range(KT):
                    for g, (t0, t1) in enumerate(groups):
                        n = hs + k * len(groups) + g
                        act.wait_ge(ht_done, n + 1)
                        A(h_hi[:, k, t0:t1], ht[:, k % 2, t0:t1], ACT.Identity,
                          bias=mod[:, g, l * N_ADA + sh + k:l * N_ADA + sh + k + 1]).then_inc(h_hi_done, 1)

            def square_x(d, j, groups, i=0):
                T = groups[-1][1]
                n = KT * j + d
                if not (isinstance(i, int) and n < 2):
                    act.wait_ge(sqsum_done, 4 * i + (n - 1))
                A(sqt[:, d % 2, 0:T], x_sb[:, 4 * i + d, 0:T], ACT.Square).then_inc(sq_done, 1)

            def tile_hi(ch, x):
                if x["v"]:
                    s0, n = x["v"]
                    act.wait_ge(acc_copied, x["acc"] + 1)
                    if n == 2:
                        src = raw_of(ch, x["t"])[:, s0 * HD:(s0 + 2) * HD].rearrange("p (k d) -> p k d", k=2) \
                            .unsqueeze(2).broadcast_to([P, 2, 2, HD])
                        dst = v_hi[:, x["t"], :].rearrange("p (k a d) -> p k a d", k=2, a=2)
                    else:
                        src = raw_of(ch, x["t"])[:, s0 * HD:(s0 + n) * HD]
                        dst = v_hi[:, x["t"], :]
                    A(dst, src, ACT.Copy).then_inc(v_hi_done, 1)
                if "tile" not in x:
                    return
                b = 0
                i = x["tile"] % 2
                split, _, _, roped = turn_buffers(ch)
                act.wait_ge(rope_done, x["tile"] + 1)
                if x["tile"] >= 2:
                    act.wait_ge(qk_turned, x["prev2"])
                for s0, n, kind, _ in x["maps"]:
                    u = roped[:, i, s0:s0 + n, :]
                    if kind == "q":
                        ins = A(split[:, i, b:b + n, 0, :].bitcast(f32r), u, ACT.Copy, scale=SCALE)
                        b += n
                    else:
                        dst = split[:, i, b:b + 2 * n:2, :, :].bitcast(f32r)
                        ins = A(dst, u.unsqueeze(2).broadcast_to([P, n, 2, HD]), ACT.Copy)
                        b += 2 * n
                    ins.then_inc(split_hi_done, 1)

            def tile_store(x):
                for g, b, m, store in x.get("groups", []):
                    act.wait_ge(qk_turned, g + 1)
                    A(qk[:, store:store + m, x["t"] * P:(x["t"] + 1) * P],
                      ps[:, 6 + g % 2, 0:m * P].rearrange("p (m t) -> p m t", m=m), ACT.Copy).then_inc(qk_stored, 1)

            tiles = [x for ch in chunks for x in ch["tiles"] if "tile" in x]
            for n, x in enumerate(tiles):
                if n >= 2:
                    x["prev2"] = tiles[n - 2]["groups"][-1][0] + 1

            def chunk_copies(ch):
                q, l, p, c = ch["q"], ch["l"], ch["p"], ch["c"]
                for x in ch["tiles"]:
                    act.wait_ge(acc_done, x["acc"] + 1)
                    if l == 0 and (p, c) == (1, 1) and x["t"] == 3:
                        act.wait_ge(ada_used, 3 * KT + 4)
                    if l == 0 and (p, c) == (2, 0) and x["t"] == 4:
                        act.wait_ge(ada_used, 4 * KT)
                    c0, c1 = x["cols"]
                    A(raw_of(ch, x["t"])[:, c0:c1], ps[:, x["t"], c0:c1], ACT.Copy).then_inc(acc_copied, 1)
                if p == 0:
                    full = [x for x in ch["tiles"] if x["cols"][1] == CHUNK]
                    act.wait_ge(acc_copied, ch["tiles"][-1]["acc"] + 1)
                    n = len(full)
                    buf = raw_01 if c else raw
                    ins = A(rawsq[:, 0:n, :], buf[:, 0:n, :], ACT.Square)
                    if n < len(ch["tiles"]):
                        ins = A(rawsq[:, n:, 0:256], buf[:, n:6, 0:256], ACT.Square)
                    ins.then_inc(raw_squared, 1)

            def head_sd_step(ch):
                if ch["p"] == 0:
                    k = 2 * ch["l"] + ch["c"]
                    act.wait_ge(head_ss_done, k + 1)
                    n = 36 if len(ch["tiles"]) == 6 else 24
                    A(head_sd[:, 0:n], head_ss[:, 0:n], ACT.Sqrt, bias=eps[:, :], scale=1.0 / HD) \
                        .then_inc(head_sd_done, 1)

            def turn_tiles(xs):
                for n, (y, x) in enumerate(xs):
                    tile_hi(y, x)
                    if n:
                        tile_store(xs[n - 1][1])

            def store_last(xs):
                for _, x in xs[-1:]:
                    tile_store(x)

            def project(l, p, c):
                ch = chunk_of(l, p, c)
                prev = ch["prev"]
                after = turn_schedule(chunks, ch)
                for u in range(IN_UNITS):
                    n = ch["unit"] + u
                    if l == 0 and (p, c) == (1, 1) and u == 0:
                        act.wait_ge(c_loaded, 32)
                        A(c_inner[:, :, :], c_inner[:, :, :], ACT.Silu).then_inc(c_ready, 1)
                    xs = after[u]
                    turn_tiles(xs)
                    if u == IN_UNITS - 1:
                        store_last(xs)
                        chunk_copies(ch)
                        unit_hi(n + RING)
                    else:
                        unit_hi(n + RING)
                        store_last(xs)
                    if prev and u == 0:
                        head_sd_step(prev)
                turn_tiles(after[IN_UNITS])
                store_last(after[IN_UNITS])

            def attend(l, p):
                waiting = []

                def exponentials(s):
                    it, sid, m = s["item"], s["sid"], s["m"]
                    k = it["k1"] - it["k0"]
                    act.wait_ge(bias_done, sid + 1)
                    if m == 0:
                        dst = p_sb[:, it["slots"][s["qi"]], 0:k]
                        before = it["freed_by"][s["qi"]]
                        if before:
                            act.wait_ge(turned, before["T"][-1]["tid"] + 1)
                    else:
                        dst = ptmp[:, 0:k]
                        if comb_no[sid] > 1:
                            act.wait_ge(probs_done, comb_no[sid] - 1)
                    src = ps[:, 2 * (sid % 2):2 * (sid % 2) + 2, :].rearrange("p a b -> p (a b)")[:, 0:k]
                    A(dst, src, ACT.Exp, bias=nb[:, sid % 8:sid % 8 + 1],
                      accum_out=rs[:, sid % 8:sid % 8 + 1]).then_inc(exp_done, 1)

                for kind, s in phase_of(l, p)["order"]:
                    if kind == "split":
                        while waiting:
                            exponentials(waiting.pop(0))
                        tile_hi(chunk_of(l, p, 1), s)
                    if kind == "turn":
                        tile_store(s)
                    if kind in ("split", "turn"):
                        continue
                    it = s["item"]
                    if kind == "S":
                        while waiting:
                            exponentials(waiting.pop(0))
                        waiting.append(s)
                    elif kind == "T":
                        if s["j"] == 0:
                            while waiting and waiting[0]["item"] is it:
                                exponentials(waiting.pop(0))
                        tid = s["tid"]
                        nq = it["t1"] - it["t0"]
                        act.wait_ge(turned, tid + 1)
                        if s["buf_before"] is not None:
                            act.wait_ge(pv_done, s["buf_before"] + 1)
                        A(pt_hi[s["buf"]][:, 0:nq], ps[:, 4 + tid % TURNS, 0:nq], ACT.Copy).then_inc(pt_hi_done, 1)
                        while waiting:
                            exponentials(waiting.pop(0))
                    elif s["j"] == len(it["T"]) - 1:
                        while waiting:
                            exponentials(waiting.pop(0))
                        act.wait_ge(pv_done, s["tid"] + 1)
                        nq = it["t1"] - it["t0"]
                        if p == 0:
                            r = slice(HD * (it["h"] % 2), HD * (it["h"] % 2) + HD)
                            A(o_sb[r, it["h"] // 2, it["t0"]:it["t1"]], ps[r, 7, 0:nq], ACT.Copy).then_inc(o_done, 1)
                        else:
                            A(o_sb[:, 4 + 2 * (p - 1) + it["h"], it["t0"]:it["t1"]], ps[:, 7, 0:nq], ACT.Copy) \
                                .then_inc(o_done, 1)

            act.wait_ge(small_loaded, 32)
            A(silu_cols[:, :, :].rearrange("p k s -> p (k s)"), sm[:, S_C:S_C + 2 * KT], ACT.Silu) \
                .then_inc(silu_cols_done, 1)
            act.wait_ge(lam_sum, 1)
            A(lamw[:, :], lamw[:, :], ACT.Exp).then_inc(lam_exp, 1)
            act.wait_ge(x_loaded, 16)
            for d in range(KT):
                square_x(d, 0, norms[0])
            for n in range(RAW):
                unit_hi(n)
            norm_hi(0)
            act.wait_ge(c_loaded, 16)
            A(c_bc[:, :, :], c_bc[:, :, :], ACT.Silu).then_inc(c_ready, 1)
            for l in range(DEPTH):
                groups = token_groups(l)
                T = groups[-1][1]
                for what, *args in LAYER_STEPS:
                    (project if what == "project" else attend)(l, *args)
                last_item = phase_of(l, 2)["items"][-1]
                act.wait_ge(pv_done, last_item["T"][-1]["tid"] + 1)
                if l == 0:
                    act.dma_start(x_sb[:, :, :], x_in).then_inc(x_loaded, 16)
                else:
                    act.wait_ge(x_spilled, 16)
                    act.dma_start(x_sb[:, :, 0:SEQ], x_spill).then_inc(x_loaded, 16)

                def output_hi(k):
                    for g, (t0, t1) in enumerate(groups):
                        A(oh[:, k, t0:t1], o_sb[:, k, t0:t1], ACT.Copy).then_inc(o_hi_done, 1)

                act.wait_ge(o_done, last_item["id"] + 1)
                for b in range(B_HEADS):
                    if b >= 2:
                        act.wait_ge(ss_done, 1 + (B_HEADS + 2) * l + b - 1)
                    A(osq[:, b % 2, 0:T], o_sb[:, 4 + b, 0:T], ACT.Square).then_inc(osq_done, 1)
                    if b >= 1:
                        output_hi(b - 1)
                output_hi(B_HEADS - 1)
                stats_sd(("sub", l), B_HEADS * n_tiles(groups), B_HEADS * 32, l)
                for k in range(4, KT):
                    act.wait_ge(o_normed, sub_sq[l] + k - 3)
                    output_hi(k)
                if l == 0:
                    act.wait_ge(c_loaded, 48)
                    A(c_bc[:, :, :], c_bc[:, :, :], ACT.Silu).then_inc(c_ready, 1)
                for d in range(KT):
                    act.wait_ge(bank_read, evac_index(wo_unit(l) + d) + 1)
                    unit_hi(wo_unit(l) + d + RING)
                    square_x(d, 2 * l + 1, groups)
                norm_hi(2 * l + 1)
                for part, n in enumerate(PARTS):
                    pair0 = l * FF_TILES + sum(PARTS[:part])

                    A(act_scrap[:, :], sm[:, 0:1], ACT.Silu)

                    def pairs(i, part=part, pair0=pair0, groups=groups, T=T, l=l):
                        for half in range(2):
                            for gv, buf in enumerate((conv_g, conv_v)):
                                c = up_unit(l, part) + 2 * half + gv
                                wcol = S_CONV + (l * 2 * FF_TILES + gv * FF_TILES + sum(PARTS[:part]) + half) * 4
                                wait_unit(act, c, i)
                                act.wait_ge(a_lo_done, 2 * i + (pair0 + half + 1))
                                for g, (t0, t1) in enumerate(groups):
                                    ins = A(buf[:, t0:t1], ps[:, 2 * (c % 4) + g, 0:t1 - t0], ACT.Identity,
                                            bias=sm[:, bass.ds(8 * i + (wcol + 3), 1)],
                                            scale=sm[:, bass.ds(8 * i + (wcol + 1), 1)])
                                ins.then_inc(conv_started, 1)
                                unit_hi(c + RING, i)
                            act.wait_ge(bank_read, 4 * i + (evac_index(up_unit(l, part) + 2 * half) + 1))
                            A(conv_g[:, 0:T], conv_g[:, 0:T], ACT.Silu).then_inc(silu_done, 1)
                            act.wait_ge(prod_done, 2 * i + (pair0 + half + 1))
                            A(a_hi[:, 2 * i + half, 0:T], conv_g[:, 0:T], ACT.Copy).then_inc(a_hi_done, 1)

                    step.loop(n // 2, 0, pairs)
                    last_part = part == len(PARTS) - 1
                    for d in range(KT):
                        c = down_unit(l, part) + d
                        if c + RING < N_UNITS:
                            unit_hi(c + RING)
                        if last_part:
                            act.wait_ge(bank_read, evac_index(c) + 1)
                            square_x(d, 2 * l + 2, norms[2 * l + 2])
                if l == 0:
                    act.wait_ge(bank_read, evac_index(down_unit(0, len(PARTS) - 1) + KT - 1) + 1)
                    act.dma_start(x_spill, x_sb[:, :, 0:SEQ]).then_inc(x_spilled, 16)
                norm_hi(2 * l + 2)
                if l == 0:
                    act.wait_ge(x_spilled, 16)
            for k in range(KT):
                act.wait_ge(y_done, k + 1)
                act.dma_start(out[:, k, :], y_sb[:, k, :]).then_inc(stored, 16)
            act.wait_ge(stored, 16 * KT)

        @block.vector
        def _(dve):
            V = nc.vector
            step = Steps(dve, dve_step)

            def ada_tile(c, streams, i, dst):
                buf, silu_c, junk = ada_place(c, i)
                if isinstance(i, int) and MID_ADA <= c < MID_END:
                    dve.wait_ge(first_ada_loaded[(c - MID_ADA) // ADA_GROUP], 32)
                    w = ada_first[:, c - MID_ADA, :]
                else:
                    loads = c - FIRST_ADA if c < MID_ADA else c - FIRST_ADA - (MID_END - MID_ADA)
                    dve.wait_ge(ada_loaded[c % 2], 32 * i + 16 * (loads // 2 + 1))
                    w = buf[:, :]
                if not isinstance(i, int) or c > 0:
                    dve.wait_ge(ada_used, 4 * i + c)
                for s in range(streams):
                    ins = V.tensor_tensor_reduce(junk[:, :], w, silu_c[:, s, :], 1.0, 0.0, ALU.mult, ALU.add,
                                                 dst(s))
                    if s == streams - 1:
                        ins.then_inc(ada_used, 1)
                    else:
                        step(ins)

            def ada_straight(a, b, streams=2):
                for c in range(a, b):
                    ada_tile(c, streams, 0, lambda s: mod[:, s, c:c + 1])

            def add_bias(a, b, streams=2):
                dve.wait_ge(ada_used, b)
                for s in range(streams):
                    step(V.tensor_tensor(mod[:, s, a:b], mod[:, s, a:b], sm[:, S_BADA + a:S_BADA + b], ALU.add))

            def first_modulation():
                dve.wait_ge(first_mod_done, FIRST_ADA // FIRST_GROUP)
                for s in range(2):
                    src = ps[:, 4, 0:2 * FIRST_ADA].rearrange("p (c s) -> p c s", s=2)[:, :, s]
                    step(V.tensor_tensor(mod[:, s, 0:FIRST_ADA], src, sm[:, S_BADA:S_BADA + FIRST_ADA], ALU.add))
                V.memset(zero[:, :], 0.0).then_inc(ada_used, FIRST_ADA)
                norm_gains(gs1, KT, S_GATTN)

            def norm_gains(gs, scale_at, gain, streams=2):
                for s in range(streams):
                    step(V.scalar_tensor_tensor(gs[:, s, :], mod[:, s, scale_at:scale_at + KT], 1.0,
                                                sm[:, gain:gain + KT], ALU.add, ALU.mult))

            cos = sm[:, S_COS:S_COS + 4 * HD].rearrange("p (t d) -> p t d", t=4)
            sin = sm[:, S_SIN:S_SIN + 4 * HD].rearrange("p (t d) -> p t d", t=4)

            def rope_tables(l):
                for n, col in enumerate((S_GQ, S_GK)):
                    g = sm[:, col + l * HD:col + (l + 1) * HD]
                    step(V.tensor_tensor(tabs[:, 2 * n, :, :], cos, g.unsqueeze(1).broadcast_to([P, 4, HD]), ALU.mult))
                    gv = g.rearrange("p (a b d) -> p a b d", a=2, b=2)
                    for t in range(4):
                        sv = sm[:, S_SIN + t * HD:S_SIN + (t + 1) * HD].rearrange("p (a b d) -> p a b d", a=2, b=2)
                        ov = tabs[:, 2 * n + 1, t, :].rearrange("p (a b d) -> p a b d", a=2, b=2)
                        for b in range(2):
                            step(V.tensor_tensor(ov[:, :, b, :], sv[:, :, b, :], gv[:, :, 1 - b, :], ALU.mult))

            def stats_scales(s, cols, banks_of):
                no = stat_index(s) + 1
                dve.wait_ge(sd_done, no)
                step(V.reciprocal(n_r[:, 0:cols], n_sd[:, 0:cols]))

            def diag(s, k):
                g = stat_base(s) + k
                dg = dgo if s[0] == "sub" else dgn
                if k >= 4:
                    dve.wait_ge(spread_done, g - 3)
                V.tensor_scalar(dg[:, k % 4, :], ident, n_r[:, k:k + 1], None, ALU.mult).then_inc(diag_done, 1)

            def add_squares(d, j, groups, i=0):
                T = groups[-1][1]
                dve.wait_ge(sq_done, 4 * i + (KT * j + d + 1))
                if not (isinstance(i, int) and d == 0):
                    dve.wait_ge(sqsum_done, KT * j + d)
                    V.tensor_tensor(sqsum[:, 0:T], sqsum[:, 0:T], sqt[:, d % 2, 0:T], ALU.add).then_inc(sqsum_done, 1)
                else:
                    V.tensor_copy(sqsum[:, 0:T], sqt[:, d % 2, 0:T]).then_inc(sqsum_done, 1)

            def norm(j):
                groups = norms[j]
                s = ("norm", j)
                nt = n_tiles(groups)
                _, hs = norm_counts(j)
                l = j // 2
                gs = gs1 if j % 2 == 0 else gs2
                sh = 0 if j % 2 == 0 else 3 * KT
                final = j == len(norms) - 1
                stats_scales(s, nt, None)
                for t in range(nt):
                    diag(s, t)
                if j == 0:
                    first_modulation()

                def lo(k, g):
                    t0, t1 = groups[g]
                    dve.wait_ge(h_hi_done, hs + k * len(groups) + g + 1)
                    V.scalar_tensor_tensor(h_lo[:, k, t0:t1], ht[:, k % 2, t0:t1], mod[:, g, l * N_ADA + sh + k:l * N_ADA + sh + k + 1],
                                           h_hi[:, k, t0:t1].bitcast(f32), ALU.add, ALU.subtract).then_inc(h_lo_done, 1)

                dve.wait_ge(spread_done, stat_base(s) + nt)
                for k in range(KT):
                    for g, (t0, t1) in enumerate(groups):
                        scale = sm[:, S_GFIN + k:S_GFIN + k + 1] if final else gs[:, g, k:k + 1]
                        if final:
                            dst, done = y_sb[:, k, t0:t1], y_done
                        else:
                            dst, done = ht[:, k % 2, t0:t1], ht_done
                            if k >= 2:
                                dve.wait_ge(h_lo_done, hs + (k - 2) * len(groups) + g + 1)
                        V.scalar_tensor_tensor(dst, x_sb[:, k, t0:t1], scale, ps[:, 6 + g, 0:t1 - t0],
                                               ALU.mult, ALU.mult).then_inc(done, 1)
                    if k >= 1 and not final:
                        for g in range(len(groups)):
                            lo(k - 1, g)
                if not final:
                    for g in range(len(groups)):
                        lo(KT - 1, g)

            def head_norms(ch):
                k = 2 * ch["l"] + ch["c"]
                dve.wait_ge(raw_squared, k + 1)
                nt = len(ch["tiles"])
                rows = [(0, nt, 0, 6)] if ch["tiles"][-1]["cols"][1] == CHUNK else [(0, 4, 0, 6), (4, 6, 0, 4)]
                sq = rawsq[:, :, :].rearrange("p t (s d) -> p t s d", d=HD)
                ssv = head_ss[:, :].rearrange("p (t s) -> p t s", s=6)
                if len(rows) > 1:
                    step(V.memset(head_ss[:, :], 1.0))
                for n, (a, b, s0, s1) in enumerate(rows):
                    ins = V.tensor_reduce(ssv[:, a:b, s0:s1], sq[:, a:b, s0:s1, :], AX.X, ALU.add)
                    if n == len(rows) - 1:
                        ins.then_inc(head_ss_done, 1)
                dve.wait_ge(head_sd_done, k + 1)
                n = 36 if nt == 6 else 24
                step(V.reciprocal(head_r[:, 0:n], head_sd[:, 0:n]))

            def rope_tile(ch, x):
                t, i = x["t"], x["tile"] % 2
                _, rope1, rope2, roped = turn_buffers(ch)
                if x["tile"] >= 1:
                    dve.wait_ge(rope_done, x["tile"])
                if x["tile"] >= 2:
                    dve.wait_ge(split_lo_done, x["prev2_his"])
                p = ch["p"]
                last = len(x["maps"]) - 1
                for n, (s0, m, kind, _) in enumerate(x["maps"]):
                    src = raw_of(ch, t)[:, s0 * HD:(s0 + m) * HD].rearrange("p (m d) -> p m d", m=m)
                    if p == 0:
                        r = head_r[:, 6 * t + s0:6 * t + s0 + m].unsqueeze(2).broadcast_to([P, m, HD])
                        step(V.tensor_tensor(src, src, r, ALU.mult))
                    dst = roped[:, i, s0:s0 + m, :]
                    if t >= SEQ // P:
                        if p == 0:
                            col = (S_GQ if kind == "q" else S_GK) + ch["l"] * HD
                            ins = V.tensor_tensor(dst, src, sm[:, col:col + HD].unsqueeze(1).broadcast_to([P, m, HD]),
                                                  ALU.mult)
                        else:
                            ins = V.tensor_copy(dst, src)
                    else:
                        if p == 0:
                            w = 0 if kind == "q" else 2
                            ct, st = tabs[:, w, t, :], tabs[:, w + 1, t, :]
                        else:
                            ct, st = cos[:, t, :], sin[:, t, :]
                        r1 = rope1[:, s0:s0 + m, :]
                        step.mark(V.tensor_tensor(r1, src, ct.unsqueeze(1).broadcast_to([P, m, HD]), ALU.mult))
                        sv = src.rearrange("p m (a b d) -> p m a b d", a=2, b=2)
                        tv = st.rearrange("p (a b d) -> p a b d", a=2, b=2)
                        ov = rope2[:, s0:s0 + m, :].rearrange("p m (a b d) -> p m a b d", a=2, b=2)
                        for b in range(2):
                            step.mark(V.tensor_tensor(ov[:, :, :, b, :], sv[:, :, :, 1 - b, :],
                                                      tv[:, :, b, :].unsqueeze(1).broadcast_to([P, m, 2, 16]),
                                                      ALU.mult))
                        step.wait()
                        ins = V.tensor_tensor(dst, r1, rope2[:, s0:s0 + m, :], ALU.add)
                    if n == last:
                        ins.then_inc(rope_done, 1)
                    else:
                        step.mark(ins)

            def tile_lo(ch, x):
                i = x["tile"] % 2
                split, _, _, roped = turn_buffers(ch)
                b = 0
                for n, (s0, m, kind, _) in enumerate(x["maps"]):
                    dve.wait_ge(split_hi_done, x["his"] - len(x["maps"]) + n + 1)
                    u = roped[:, i, s0:s0 + m, :]
                    if kind == "q":
                        ins = V.scalar_tensor_tensor(split[:, i, b:b + m, 1, :], u, SCALE, split[:, i, b:b + m, 0, :],
                                                     ALU.mult, ALU.subtract)
                        b += m
                    else:
                        ins = V.tensor_tensor(split[:, i, b + 1:b + 2 * m:2, :, :],
                                              u.unsqueeze(2).broadcast_to([P, m, 2, HD]),
                                              split[:, i, b:b + 2 * m:2, :, :], ALU.subtract)
                        b += 2 * m
                    ins.then_inc(split_lo_done, 1)

            def values_lo(ch, x):
                s0, n = x["v"]
                t = x["t"]
                dve.wait_ge(v_hi_done, x["vn"] + 1)
                if n == 2:
                    src = raw_of(ch, t)[:, s0 * HD:(s0 + 2) * HD].rearrange("p (k d) -> p k d", k=2)
                    hv = v_hi[:, t, :].bitcast(f32).rearrange("p (k a d) -> p k a d", k=2, a=2)
                    lv = v_lo[:, t, :].rearrange("p (k a d) -> p k a d", k=2, a=2)
                    for a in range(2):
                        ins = V.tensor_tensor(lv[:, :, a, :], src, hv[:, :, a, :], ALU.subtract)
                else:
                    ins = V.tensor_tensor(v_lo[:, t, :], raw_of(ch, t)[:, s0 * HD:(s0 + n) * HD],
                                          v_hi[:, t, :].bitcast(f32), ALU.subtract)
                ins.then_inc(v_lo_done, 1)

            tiles = [x for ch in chunks for x in ch["tiles"] if "tile" in x]
            for n, x in enumerate(tiles):
                if n >= 2:
                    x["prev2_his"] = tiles[n - 2]["his"]

            def turn_chunk(ch):
                p = ch["p"]
                if p == 0:
                    head_norms(ch)
                before = None
                for x in ch["tiles"]:
                    if "tile" in x:
                        if p > 0:
                            dve.wait_ge(acc_copied, x["acc"] + 1)
                        rope_tile(ch, x)
                    if before:
                        tile_lo(ch, before)
                    before = x if "tile" in x else None
                    if x["v"]:
                        values_lo(ch, x)
                if before:
                    tile_lo(ch, before)

            def project(l, p, c):
                ch = chunk_of(l, p, c)
                if ch["after"] is not None:
                    dve.wait_ge(pv_done, phase_of(l, ch["after"])["items"][-1]["T"][-1]["tid"] + 1)
                if l == 0 and (p, c) == (2, 0):
                    ada_straight(3 * KT + 4, 4 * KT)
                if ch["prev"]:
                    turn_chunk(ch["prev"])
                elif l == 0:
                    dve.wait_ge(c_ready, 1)
                    ada_straight(2 * KT, 3 * KT)
                    add_bias(2 * KT, 3 * KT)
                if l == 0 and (p, c) == (1, 1):
                    dve.wait_ge(c_ready, 2)
                    ada_straight(3 * KT, 3 * KT + 4)

            def attend(l, p):
                def finish(s):
                    it, sid = s["item"], s["sid"]
                    k = it["k1"] - it["k0"]
                    c = slice(sid % 8, sid % 8 + 1)
                    dve.wait_ge(exp_done, sid + 1)
                    if sid - 8 in divided:
                        dve.wait_ge(scaled_done, divided[sid - 8])
                    ins = V.reciprocal(ri[:, c], rs[:, c])
                    ins.then_inc(recip_done, 1)
                    if s["m"] == 1:
                        dve.wait_ge(recip_done, sid + 1)
                        first = slice((sid - 1) % 8, (sid - 1) % 8 + 1)
                        step(V.tensor_scalar(rl[:, c], ri[:, c], nlam[:, l:l + 1], rs[:, first], ALU.mult, ALU.mult))
                        buf = p_sb[:, it["slots"][s["qi"]], 0:k]
                        V.scalar_tensor_tensor(buf, ptmp[:, 0:k], rl[:, c], buf, ALU.mult, ALU.add) \
                            .then_inc(probs_done, 1)

                def pt_rest(s):
                    tid = s["tid"]
                    nq = s["item"]["t1"] - s["item"]["t0"]
                    dve.wait_ge(pt_hi_done, tid + 1)
                    V.tensor_tensor(pt_lo[s["buf"]][:, 0:nq], ps[:, 4 + tid % TURNS, 0:nq],
                                    pt_hi[s["buf"]][:, 0:nq].bitcast(f32), ALU.subtract).then_inc(pt_lo_done, 1)

                sums, rests = [], []
                ch = chunk_of(l, p, 1)
                for kind, s in phase_of(l, p)["order"]:
                    if kind == "split":
                        dve.wait_ge(acc_copied, s["acc"] + 1)
                        if "tile" in s:
                            rope_tile(ch, s)
                    if kind == "turn":
                        if "tile" in s:
                            tile_lo(ch, s)
                        if s["v"]:
                            values_lo(ch, s)
                    if kind in ("split", "turn"):
                        continue
                    it = s["item"]
                    if kind == "S":
                        sid = s["sid"]
                        k = it["k1"] - it["k0"]
                        dve.wait_ge(scores_done, sid + 1)
                        src = ps[:, 2 * (sid % 2):2 * (sid % 2) + 2, :].rearrange("p a b -> p (a b)")[:, 0:k]
                        V.tensor_reduce(nb[:, sid % 8:sid % 8 + 1], src, AX.X, ALU.max, negate=True) \
                            .then_inc(bias_done, 1)
                        while rests:
                            pt_rest(rests.pop(0))
                        while sums:
                            finish(sums.pop(0)[0])
                        sums.append([s, 0])
                    elif kind == "T":
                        while sums and (sums[0][0]["item"] is it or sums[0][1]):
                            finish(sums.pop(0)[0])
                        for r in sums:
                            r[1] += 1
                        while rests:
                            pt_rest(rests.pop(0))
                        rests.append(s)
                    elif rests and rests[0] is s:
                        pt_rest(rests.pop(0))
                assert not sums and not rests

            step.mark(V.memset(eps[:, :], EPS))
            V.memset(zero[:, :], 0.0).then_inc(a_lo_done, 1)
            dve.wait_ge(small_loaded, 32)
            for l in range(DEPTH):
                for n in range(2):
                    step(V.tensor_tensor_reduce(ht[:, 0, 0:HD],
                                                lamv[:, l, 2 * n, :], lamv[:, l, 2 * n + 1, :], 1.0, 0.0,
                                                ALU.mult, ALU.add, lamw[:, 2 * l + n:2 * l + n + 1]))
            V.tensor_scalar(gsub[:, 0:1], sm[:, S_GSUB:S_GSUB + 1], 1.0 - LAM_INIT[0], None, ALU.mult) \
                .then_inc(lam_sum, 1)
            step(V.tensor_scalar(gsub[:, 1:2], sm[:, S_GSUB + 1:S_GSUB + 2], 1.0 - LAM_INIT[1], None, ALU.mult))
            rope_tables(0)
            dve.wait_ge(lam_exp, 1)
            for l in range(DEPTH):
                step(V.tensor_tensor(nlam[:, l:l + 1], lamw[:, 2 * l + 1:2 * l + 2], lamw[:, 2 * l:2 * l + 1],
                                     ALU.subtract))
                step(V.tensor_scalar(nlam[:, l:l + 1], nlam[:, l:l + 1], -LAM_INIT[l], None, ALU.add))
            for d in range(KT):
                add_squares(d, 0, norms[0])
            norm(0)
            for l in range(DEPTH):
                groups = token_groups(l)
                T = groups[-1][1]
                nt = n_tiles(groups)
                for what, *args in LAYER_STEPS:
                    (project if what == "project" else attend)(l, *args)
                s = ("sub", l)

                def o_lo(k):
                    for g, (t0, t1) in enumerate(groups):
                        dve.wait_ge(o_hi_done, sub_oh[l] + k * len(groups) + g + 1)
                        V.tensor_tensor(ol[:, k, t0:t1], o_sb[:, k, t0:t1], oh[:, k, t0:t1].bitcast(f32),
                                        ALU.subtract).then_inc(o_lo_done, 1)

                for k in range(4):
                    o_lo(k)
                stats_scales(s, B_HEADS * nt, None)
                for b in range(B_HEADS):
                    for t in range(nt):
                        diag(s, b * nt + t)
                    dve.wait_ge(spread_done, stat_base(s) + (b + 1) * nt)
                    for g, (t0, t1) in enumerate(groups):
                        ins = V.scalar_tensor_tensor(o_sb[:, 4 + b, t0:t1], o_sb[:, 4 + b, t0:t1], gsub[:, l:l + 1],
                                                     ps[:, 6 + g, 0:t1 - t0], ALU.mult, ALU.mult)
                    ins.then_inc(o_normed, 1)
                    if b >= 1:
                        o_lo(4 + b - 1)
                o_lo(KT - 1)

                def update(c, gate, x_col):
                    wait_unit(dve, c)
                    for g, (t0, t1) in enumerate(groups):
                        xs = x_sb[:, x_col, t0:t1]
                        ins = V.scalar_tensor_tensor(xs, ps[:, 2 * (c % 4) + g, 0:t1 - t0],
                                                     mod[:, g, l * N_ADA + gate + x_col:l * N_ADA + gate + x_col + 1],
                                                     xs, ALU.mult, ALU.add)
                    ins.then_inc(bank_read, 1)

                dve.wait_ge(x_loaded, 16 * (l + 2))
                for d in range(KT):
                    update(wo_unit(l) + d, 2 * KT, d)
                    add_squares(d, 2 * l + 1, groups)
                    if l == 0:
                        if d == 0:
                            dve.wait_ge(c_ready, 3)
                        ada_straight(MID_ADA + d, MID_ADA + d + 1)
                if l == 0:
                    add_bias(3 * KT, 5 * KT)
                    norm_gains(gs2, 4 * KT, S_GFFN)
                norm(2 * l + 1)
                for part, n in enumerate(PARTS):
                    pair0 = l * FF_TILES + sum(PARTS[:part])
                    ada0 = 5 * KT + 2 * sum(PARTS[:part]) + (KT if part else 0)

                    def pairs(i, part=part, pair0=pair0, l=l, groups=groups, T=T, ada0=ada0):
                        for half in range(2):
                            for gv, buf in enumerate((conv_g, conv_v)):
                                c = up_unit(l, part) + 2 * half + gv
                                wcol = S_CONV + (l * 2 * FF_TILES + gv * FF_TILES + sum(PARTS[:part]) + half) * 4
                                dve.wait_ge(conv_started, 4 * i + (2 * (pair0 + half) + gv + 1))
                                for tap in range(2):
                                    w = wcol + 2 * tap
                                    for g, (t0, t1) in enumerate(groups):
                                        dst = buf[:, t0 + 1:t1] if tap == 0 else buf[:, t0:t1 - 1]
                                        n_ = t1 - t0
                                        src = ps[:, 2 * (c % 4) + g, 0:n_ - 1] if tap == 0 else \
                                            ps[:, 2 * (c % 4) + g, 1:n_]
                                        ins = V.scalar_tensor_tensor(dst, src, sm[:, bass.ds(8 * i + w, 1)], dst,
                                                                     ALU.mult, ALU.add)
                                        if tap == 0 or g < len(groups) - 1:
                                            step.mark(ins)
                                    if tap == 0:
                                        step.wait()
                                ins.then_inc(bank_read, 1)
                            dve.wait_ge(silu_done, 2 * i + (pair0 + half + 1))
                            dve.wait_ge(bank_read, 4 * i + (evac_index(c) + 1))
                            V.tensor_tensor(conv_g[:, 0:T], conv_g[:, 0:T], conv_v[:, 0:T], ALU.mult) \
                                .then_inc(prod_done, 1)
                            dve.wait_ge(a_hi_done, 2 * i + (pair0 + half + 1))
                            V.tensor_tensor(a_lo[:, 2 * i + half, 0:T], conv_g[:, 0:T],
                                            a_hi[:, 2 * i + half, 0:T].bitcast(f32), ALU.subtract).then_inc(a_lo_done, 1)
                            if l == 0:
                                for j in range(2):
                                    a = ada0 + 2 * half + j
                                    ada_tile(a, 2 if part == 0 else 1, i,
                                             lambda s: ada_sum[:, s, 2 * half + j:2 * half + j + 1])
                        if l == 0:
                            dve.wait_ge(ada_used, 4 * i + (ada0 + 4))
                            for s in range(2 if part == 0 else 1):
                                step(V.tensor_copy(mod[:, s, bass.ds(4 * i + ada0, 4)], ada_sum[:, s, :]))

                    per = 2 * 2 * (len(groups) + len(groups) - 1)
                    if l == 0:
                        per += 6 if part == 0 else 1
                    step.loop(n // 2, per, pairs)
                    if l == 0 and part == 0:
                        add_bias(5 * KT, N_ADA)
                    for d in range(KT):
                        c = down_unit(l, part) + d
                        update(c, 5 * KT, d)
                        if l == 0 and part == 0:
                            ada_straight(ada0 + 2 * n + d, ada0 + 2 * n + d + 1)
                        if part == len(PARTS) - 1:
                            add_squares(d, 2 * l + 2, norms[2 * l + 2])
                            if l == 0 and d % 2 == 1:
                                ada_straight(ada0 + 2 * n + d // 2, ada0 + 2 * n + d // 2 + 1, streams=1)
                if l == 0:
                    add_bias(N_ADA, N_ADA + 2 * KT)
                    add_bias(N_ADA + 2 * KT, 2 * N_ADA, streams=1)
                    norm_gains(gs1, N_ADA + KT, S_GATTN + KT)
                    norm_gains(gs2, N_ADA + 4 * KT, S_GFFN + KT, streams=1)
                    rope_tables(1)
                norm(2 * l + 2)


_OUT_SHAPE = (P, KT, SEQ)


def kernel(x, c, ctx, c_ctx, w_ada, b_ada, g_attn, w_in, g_qa, g_ka, lam_q1, lam_k1, lam_q2, lam_k2,
           g_sub, w_o, g_ffn, w_up, conv_w, conv_b, w_down, g_final):
    import numpy as np
    import concourse.bacc as bacc
    from concourse import mybir as mb
    from concourse.bass_utils import run_bass_kernel_spmd

    f = np.float32

    def feature_cols(v):
        v = np.asarray(v)
        return np.moveaxis(v.reshape(v.shape[:-1] + (-1, P)), -1, 0)

    def tiles(w):
        k, n = w.shape
        return w.reshape(k // P, P, n // P, P).transpose(2, 1, 0, 3).reshape(n // P, P, k)

    tok = np.concatenate([np.asarray(x)[0], np.asarray(ctx)[0]], axis=0)
    x_arr = np.ascontiguousarray(tok.T.reshape(KT, P, TOK).transpose(1, 0, 2))
    cc = np.concatenate([np.asarray(c)[0], np.asarray(c_ctx)])
    pos = np.arange(SEQ)
    quarter = HD // 4
    inv = (f(10000.0) ** (-np.arange(quarter, dtype=f) / f(quarter))).astype(f)
    ang_r = (pos // GRID_W).astype(f)[:, None] * inv[None]
    ang_c = (pos % GRID_W).astype(f)[:, None] * inv[None]
    cos = np.concatenate([np.cos(ang_r)] * 2 + [np.cos(ang_c)] * 2, -1).astype(f)
    sin = np.concatenate([-np.sin(ang_r), np.sin(ang_r), -np.sin(ang_c), np.sin(ang_c)], -1).astype(f)

    sm = np.zeros((P, S_END), f)
    sm[:, S_IDENT:S_IDENT + P] = np.eye(P, dtype=f)
    sm[:, S_ONES:S_ONES + P] = 1
    sm[:, S_COS:S_COS + 4 * HD] = cos.reshape(4, P, HD).transpose(1, 0, 2).reshape(P, -1)
    sm[:, S_SIN:S_SIN + 4 * HD] = sin.reshape(4, P, HD).transpose(1, 0, 2).reshape(P, -1)
    sm[:, S_BADA:S_GATTN] = feature_cols(b_ada).reshape(P, -1)
    sm[:, S_GATTN:S_GFFN] = feature_cols(g_attn).reshape(P, -1)
    sm[:, S_GFFN:S_GFIN] = feature_cols(g_ffn).reshape(P, -1)
    sm[:, S_GFIN:S_CONV] = feature_cols(g_final).reshape(P, -1)
    conv = np.concatenate([np.asarray(conv_w), np.asarray(conv_b)[:, None]], axis=1)
    sm[:, S_CONV:S_GSUB] = feature_cols(conv).transpose(0, 1, 3, 2).reshape(P, -1)
    sm[:, S_GSUB:S_GQ] = np.asarray(g_sub).T
    sm[:, S_GQ:S_GK] = np.asarray(g_qa).reshape(1, -1)
    sm[:, S_GK:S_C] = np.asarray(g_ka).reshape(1, -1)
    sm[:, S_C:S_END] = cc.reshape(2, KT, P).transpose(2, 1, 0).reshape(P, -1)
    lam = np.stack([np.asarray(v) for v in (lam_q1, lam_k1, lam_q2, lam_k2)], axis=1).reshape(1, -1)
    lam = np.ascontiguousarray(np.broadcast_to(lam, (P, LAM_COLS)))
    ada = np.ascontiguousarray(np.asarray(w_ada).transpose(0, 2, 1).reshape(DEPTH * N_ADA, P, D))

    n_first = FIRST_ADA // FIRST_GROUP
    first = np.asarray(w_ada)[0][:, :FIRST_ADA * P].reshape(KT, P, n_first, FIRST_GROUP * P)
    first = np.ascontiguousarray(first.transpose(2, 1, 0, 3).reshape(n_first, P, -1))

    w_in, w_o, w_up, w_down = (np.asarray(w) for w in (w_in, w_o, w_up, w_down))
    stream = np.zeros((N_UNITS, P, UNIT), f)
    aq, ak, av, bq, bk, bv = 0, 512, 640, 768, 1280, 1792
    for l in range(DEPTH):
        for p in range(3):
            if p == 0:
                cols = [[(ak, 128), (av, 128), (aq, 128)], [(aq + 128, 384)]]
            else:
                o = 256 * (p - 1)
                cols = [[(bk + o, 256), (bq + o, 128)], [(bq + o + 128, 128), (bv + o, 256)]]
            for c_ in range(2):
                w = np.concatenate([w_in[l][:, a:a + n] for a, n in cols[c_]], axis=1)
                u = in_unit(l, p, c_)
                stream[u:u + IN_UNITS, :, :UNIT_K * CHUNK] = \
                    w.reshape(IN_UNITS, UNIT_K, P, CHUNK).transpose(0, 2, 1, 3).reshape(IN_UNITS, P, -1)
        stream[wo_unit(l):wo_unit(l) + KT] = tiles(w_o[l])
        up = tiles(w_up[l])
        for part, n in enumerate(PARTS):
            k0 = sum(PARTS[:part])
            u = up_unit(l, part)
            stream[u:u + 2 * n:2] = up[k0:k0 + n]
            stream[u + 1:u + 2 * n:2] = up[FF_TILES + k0:FF_TILES + k0 + n]
            d = down_unit(l, part)
            stream[d:d + KT, :, :n * P] = tiles(w_down[l][k0 * P:(k0 + n) * P])

    nc = bacc.Bacc("TRN2", target_bir_lowering=False, num_devices=1)
    arrays = dict(x_d=x_arr, cc_d=cc, small_d=sm, lam_d=lam, first_d=first, ada_d=ada, w_d=stream)
    aps = [nc.dram_tensor(n, a.shape, mb.dt.from_np(a.dtype), kind="ExternalInput").ap() for n, a in arrays.items()]
    out = nc.dram_tensor("out_d", _OUT_SHAPE, mb.dt.float32, kind="ExternalOutput").ap()
    spill = nc.dram_tensor("x_spill_d", _OUT_SHAPE, mb.dt.float32, kind="Internal").ap()
    backbone(nc, *aps, out, spill)
    r = run_bass_kernel_spmd(nc, [arrays], core_ids=[0])
    y = r.results[0]["out_d"]
    return y.transpose(1, 0, 2).reshape(D, SEQ).T.reshape(1, SEQ, D)
```
